# Optimizing a Trainium2 kernel written in Bass

```python
import math
import jax, jax.numpy as jnp
from jax import lax
import numpy as np

D_MODEL = 1024
BATCH = 1
SEQ = 512
DEPTH = 2

CHUNK = 64
PLE_DIM = 256
CONV_K = 4
SSM_HEADS = 16
SSM_HEAD_DIM = 64
SSM_INNER = SSM_HEADS * SSM_HEAD_DIM
SSM_GROUPS = 2
SSM_STATE = 128
XBC_DIM = SSM_INNER + 2 * SSM_GROUPS * SSM_STATE
ATT_Q_HEADS = 16
ATT_KV_HEADS = 2
ATT_HEAD_DIM = 64
ATT_WINDOW = 128
WINDOW_CHUNKS = ATT_WINDOW // CHUNK
ATT_Q_DIM = ATT_Q_HEADS * ATT_HEAD_DIM
ATT_KV_DIM = ATT_KV_HEADS * ATT_HEAD_DIM
EVEN_IN = SSM_INNER + XBC_DIM + SSM_HEADS + ATT_Q_DIM + 2 * ATT_KV_DIM
EVEN_MIX = SSM_INNER + ATT_Q_DIM
MLSTM_HEADS = 16
MLSTM_HEAD_DIM = 128
MLSTM_INNER = MLSTM_HEADS * MLSTM_HEAD_DIM
ODD_IN = 4 * MLSTM_INNER + 2 * MLSTM_HEADS
PEER_HEADS = 8
PEER_TOPK = 16
N_KEYS = 128
N_EXPERTS = N_KEYS * N_KEYS
PEER_QDIM = 256
PEER_TOKEN_BLOCK = 128

N_EVEN = (DEPTH + 1) // 2
N_ODD = DEPTH // 2
F32 = jnp.float32

kernel_name = 'hybrid_ssd_swa_mlstm_peer_trunk'

def rmsnorm(x, g, eps=1e-6):
    xf = x.astype(F32)
    y = xf * lax.rsqrt(jnp.mean(xf * xf, axis=-1, keepdims=True) + eps)
    return (y * g.astype(F32)).astype(x.dtype)

def causal_dwconv(x, w, b):
    y = lax.conv_general_dilated(x, w[:, None, :].astype(x.dtype), (1,), [(w.shape[0] - 1, 0)],
                                 dimension_numbers=('NWC', 'WIO', 'NWC'), feature_group_count=x.shape[-1])
    return y + b.astype(x.dtype)

def ssd(xdt, a_dt, bm, cm):
    b, s, g, r, p = xdt.shape
    n = bm.shape[-1]
    nc = s // CHUNK
    xc = xdt.reshape(b, nc, CHUNK, g, r, p)
    ac = a_dt.reshape(b, nc, CHUNK, g, r)
    bc = bm.reshape(b, nc, CHUNK, g, n)
    cc = cm.reshape(b, nc, CHUNK, g, n)
    acs = jnp.cumsum(ac, axis=2)
    causal = jnp.tril(jnp.ones((CHUNK, CHUNK), bool))[:, :, None, None]
    seg = acs[:, :, :, None] - acs[:, :, None, :]
    lmat = jnp.exp(jnp.where(causal, seg, -jnp.inf))
    cb = jnp.einsum('bclgn,bcsgn->bclsg', cc, bc)
    y_diag = jnp.einsum('bclsgr,bcsgrp->bclgrp', cb[..., None] * lmat, xc)
    decay_states = jnp.exp(acs[:, :, -1:] - acs)
    chunk_states = jnp.einsum('bclgn,bclgr,bclgrp->bcgrpn', bc, decay_states, xc)
    chunk_decay = jnp.exp(acs[:, :, -1])

    def step(h, inp):
        st, dec = inp
        return dec[..., None, None] * h + st, h

    h0 = jnp.zeros((b, g, r, p, n), chunk_states.dtype)
    _, h_in = lax.scan(step, h0, (jnp.moveaxis(chunk_states, 1, 0), jnp.moveaxis(chunk_decay, 1, 0)))
    h_in = jnp.moveaxis(h_in, 0, 1)
    y_off = jnp.einsum('bclgn,bcgrpn,bclgr->bclgrp', cc, h_in, jnp.exp(acs))
    return (y_diag + y_off).reshape(b, s, g, r, p)

def mamba2_group(z, xbc, dt_raw, conv_w, conv_b, dt_bias, a_log, d_skip, out_norm):
    b, s, _ = z.shape
    r = SSM_HEADS // SSM_GROUPS
    xbc = jax.nn.silu(causal_dwconv(xbc, conv_w, conv_b))
    xs, bm, cm = jnp.split(xbc, [SSM_INNER, SSM_INNER + SSM_GROUPS * SSM_STATE], axis=-1)
    xs = xs.reshape(b, s, SSM_GROUPS, r, SSM_HEAD_DIM)
    bm = bm.reshape(b, s, SSM_GROUPS, SSM_STATE)
    cm = cm.reshape(b, s, SSM_GROUPS, SSM_STATE)
    dt = jax.nn.softplus(dt_raw.astype(F32) + dt_bias.astype(F32)).reshape(b, s, SSM_GROUPS, r)
    a = -jnp.exp(a_log.astype(F32)).reshape(SSM_GROUPS, r)
    y = ssd(xs * dt[..., None].astype(xs.dtype), dt * a, bm, cm)
    y = y + d_skip.reshape(SSM_GROUPS, r)[..., None].astype(xs.dtype) * xs
    y = y.reshape(b, s, SSM_INNER).astype(z.dtype)
    return rmsnorm(y * jax.nn.silu(z), out_norm)

def swa_group(q, k, v, sinks):
    b, s, _ = q.shape
    nc = s // CHUNK
    g, r, hd, w = ATT_KV_HEADS, ATT_Q_HEADS // ATT_KV_HEADS, ATT_HEAD_DIM, WINDOW_CHUNKS
    qc = q.reshape(b, nc, CHUNK, g, r, hd)
    kc = k.reshape(b, nc, CHUNK, g, hd)
    vc = v.reshape(b, nc, CHUNK, g, hd)

    def band(t):
        tp = jnp.pad(t, ((0, 0), (w - 1, 0), (0, 0), (0, 0), (0, 0)))
        return jnp.concatenate([tp[:, j:j + nc] for j in range(w)], axis=2)

    kb, vb = band(kc), band(vc)
    scores = jnp.einsum('bclgrd,bcmgd->bcgrlm', qc, kb).astype(F32) * (hd ** -0.5)
    key_chunk = jnp.arange(nc)[:, None] - (w - 1) + jnp.arange(w * CHUNK)[None, :] // CHUNK
    valid = (key_chunk >= 0)[None, :, None, None, None, :]
    scores = jnp.where(valid, scores, -jnp.inf)
    sink = jnp.broadcast_to(sinks.astype(F32).reshape(g, r)[None, None, :, :, None, None], scores.shape[:-1] + (1,))
    probs = jax.nn.softmax(jnp.concatenate([scores, sink], axis=-1), axis=-1)[..., :-1]
    out = jnp.einsum('bcgrlm,bcmgd->bclgrd', probs.astype(vb.dtype), vb)
    return out.reshape(b, s, ATT_Q_DIM)

def even_mixer(h, w_in, conv_w, conv_b, dt_bias, a_log, d_skip, out_norm, sinks, w_out):
    proj = h @ w_in
    o1 = SSM_INNER
    o2 = o1 + XBC_DIM
    o3 = o2 + SSM_HEADS
    o4 = o3 + ATT_Q_DIM
    o5 = o4 + ATT_KV_DIM
    z, xbc, dt_raw, q, k, v = jnp.split(proj, [o1, o2, o3, o4, o5], axis=-1)
    y_ssm = mamba2_group(z, xbc, dt_raw, conv_w, conv_b, dt_bias, a_log, d_skip, out_norm)
    y_att = swa_group(q, k, v, sinks)
    return jnp.concatenate([y_ssm, y_att], axis=-1) @ w_out

def mlstm_cell(q, k, v, ig, lf):
    b, s, nh, dh = q.shape
    nc = s // CHUNK

    def to_chunks(t):
        return t.reshape(b, nc, CHUNK, nh, dh).transpose(1, 0, 3, 2, 4)

    def gate_chunks(t):
        return t.reshape(b, nc, CHUNK, nh).transpose(1, 0, 3, 2)

    causal = jnp.tril(jnp.ones((CHUNK, CHUNK), bool))

    def step(carry, xs):
        c_mat, n_vec, m = carry
        qc, kc, vc, ic, fc = xs
        bcs = jnp.cumsum(fc, axis=-1)
        dlog = jnp.where(causal, bcs[..., :, None] - bcs[..., None, :] + ic[..., None, :], -jnp.inf)
        inter = bcs + m[..., None]
        m_t = jnp.maximum(inter, dlog.max(axis=-1))
        wts = jnp.exp(dlog - m_t[..., None])
        g_in = jnp.exp(inter - m_t)
        sw = jnp.einsum('bhtd,bhsd->bhts', qc, kc) * wts
        num = jnp.einsum('bhts,bhsd->bhtd', sw, vc) + g_in[..., None] * jnp.einsum('bhed,bhtd->bhte', c_mat, qc)
        den = sw.sum(axis=-1) + g_in * jnp.einsum('bhd,bhtd->bht', n_vec, qc)
        h = num / jnp.maximum(jnp.abs(den), jnp.exp(-m_t))[..., None]
        b_last = bcs[..., -1]
        logw = b_last[..., None] - bcs + ic
        m_new = jnp.maximum(b_last + m, logw.max(axis=-1))
        wk = jnp.exp(logw - m_new[..., None])
        decay = jnp.exp(b_last + m - m_new)
        c_new = decay[..., None, None] * c_mat + jnp.einsum('bhs,bhse,bhsd->bhed', wk, vc, kc)
        n_new = decay[..., None] * n_vec + jnp.einsum('bhs,bhsd->bhd', wk, kc)
        return (c_new, n_new, m_new), h.astype(vc.dtype)

    init = (jnp.zeros((b, nh, dh, dh), F32), jnp.zeros((b, nh, dh), F32), jnp.zeros((b, nh), F32))
    _, hs = lax.scan(step, init, (to_chunks(q), to_chunks(k), to_chunks(v), gate_chunks(ig), gate_chunks(lf)))
    return hs.transpose(1, 0, 3, 2, 4).reshape(b, s, nh, dh)

def mlstm_mixer(h, w_in, conv_w, conv_b, i_bias, f_bias, head_norm, w_out):
    b, s, _ = h.shape
    proj = h @ w_in
    i1 = MLSTM_INNER
    q, k, v, o, ig, fg = jnp.split(proj, [i1, 2 * i1, 3 * i1, 4 * i1, 4 * i1 + MLSTM_HEADS], axis=-1)
    qk = jax.nn.silu(causal_dwconv(jnp.concatenate([q, k], axis=-1), conv_w, conv_b))
    q, k = jnp.split(qk, 2, axis=-1)
    hs = (b, s, MLSTM_HEADS, MLSTM_HEAD_DIM)
    ig = ig.astype(F32) + i_bias.astype(F32)
    lf = jax.nn.log_sigmoid(fg.astype(F32) + f_bias.astype(F32))
    hc = mlstm_cell(q.reshape(hs), (k * (MLSTM_HEAD_DIM ** -0.5)).reshape(hs), v.reshape(hs), ig, lf)
    hc = rmsnorm(hc, head_norm.reshape(MLSTM_HEADS, MLSTM_HEAD_DIM)).reshape(b, s, MLSTM_INNER)
    return (jax.nn.sigmoid(o) * hc) @ w_out

def peer(h, w_q, sub_k1, sub_k2, u, v):
    b, s, d = h.shape
    q = jnp.einsum('bsd,dhk->bshk', h, w_q)
    q1, q2 = jnp.split(q, 2, axis=-1)
    s1 = jnp.einsum('bshk,hnk->bshn', q1, sub_k1)
    s2 = jnp.einsum('bshk,hnk->bshn', q2, sub_k2)
    v1, i1 = lax.top_k(s1, PEER_TOPK)
    v2, i2 = lax.top_k(s2, PEER_TOPK)
    cand_s = (v1[..., :, None] + v2[..., None, :]).reshape(b, s, PEER_HEADS, PEER_TOPK * PEER_TOPK)
    cand_i = (i1[..., :, None] * N_KEYS + i2[..., None, :]).reshape(b, s, PEER_HEADS, PEER_TOPK * PEER_TOPK)
    top_s, pos = lax.top_k(cand_s, PEER_TOPK)
    idx = jnp.take_along_axis(cand_i, pos, axis=-1)
    gate = jax.nn.softmax(top_s.astype(F32), axis=-1).astype(h.dtype)
    nb = (b * s) // PEER_TOKEN_BLOCK
    sel = PEER_HEADS * PEER_TOPK
    hb = h.reshape(nb, PEER_TOKEN_BLOCK, d)
    ib = idx.reshape(nb, PEER_TOKEN_BLOCK, sel)
    gb = gate.reshape(nb, PEER_TOKEN_BLOCK, sel)

    def expert_block(args):
        hx, ix, gx = args
        act = jax.nn.gelu(jnp.einsum('tkd,td->tk', u[ix], hx), approximate=False) * gx
        return jnp.einsum('tk,tkd->td', act, v[ix])

    return lax.map(expert_block, (hb, ib, gb)).reshape(b, s, d)

def setup_inputs(seed: int = 0) -> dict:
    key = jax.random.key(seed)
    keys = iter(jax.random.split(key, 48))

    def nrm(shape, scale):
        return jax.random.normal(next(keys), shape, F32) * scale

    def gain(shape):
        return 1.0 + nrm(shape, 0.02)

    ne, no = N_EVEN, N_ODD
    dt0 = jnp.exp(jax.random.uniform(next(keys), (ne, SSM_HEADS), F32, math.log(1e-3), math.log(1e-1)))
    a0 = jax.random.uniform(next(keys), (ne, SSM_HEADS), F32, 1.0, 16.0)
    out_scale = 0.5
    return {
        'x': nrm((BATCH, SEQ, D_MODEL), 1.0),
        'p': nrm((DEPTH, BATCH, SEQ, PLE_DIM), 1.0),
        'norm_mix': gain((DEPTH, D_MODEL)),
        'norm_ffn': gain((DEPTH, D_MODEL)),
        'norm_ple': gain((DEPTH, D_MODEL)),
        'norm_final': gain((D_MODEL,)),
        'ev_w_in': nrm((ne, D_MODEL, EVEN_IN), D_MODEL ** -0.5),
        'ev_conv_w': nrm((ne, CONV_K, XBC_DIM), CONV_K ** -0.5),
        'ev_conv_b': nrm((ne, XBC_DIM), 0.02),
        'ev_dt_bias': dt0 + jnp.log(-jnp.expm1(-dt0)),
        'ev_a_log': jnp.log(a0),
        'ev_d_skip': gain((ne, SSM_HEADS)),
        'ev_out_norm': gain((ne, SSM_INNER)),
        'ev_sinks': nrm((ne, ATT_Q_HEADS), 0.5),
        'ev_w_out': nrm((ne, EVEN_MIX, D_MODEL), out_scale * EVEN_MIX ** -0.5),
        'od_w_in': nrm((no, D_MODEL, ODD_IN), D_MODEL ** -0.5),
        'od_conv_w': nrm((no, CONV_K, 2 * MLSTM_INNER), CONV_K ** -0.5),
        'od_conv_b': nrm((no, 2 * MLSTM_INNER), 0.02),
        'od_i_bias': nrm((no, MLSTM_HEADS), 0.1),
        'od_f_bias': jnp.linspace(3.0, 6.0, MLSTM_HEADS, dtype=F32)[None] + nrm((no, MLSTM_HEADS), 0.1),
        'od_head_norm': gain((no, MLSTM_INNER)),
        'od_w_out': nrm((no, MLSTM_INNER, D_MODEL), out_scale * MLSTM_INNER ** -0.5),
        'pk_w_q': nrm((DEPTH, D_MODEL, PEER_HEADS, PEER_QDIM), D_MODEL ** -0.5),
        'pk_sub_k1': nrm((DEPTH, PEER_HEADS, N_KEYS, PEER_QDIM // 2), (PEER_QDIM // 2) ** -0.5),
        'pk_sub_k2': nrm((DEPTH, PEER_HEADS, N_KEYS, PEER_QDIM // 2), (PEER_QDIM // 2) ** -0.5),
        'pk_u': nrm((DEPTH, N_EXPERTS, D_MODEL), D_MODEL ** -0.5),
        'pk_v': nrm((DEPTH, N_EXPERTS, D_MODEL), 0.5 * PEER_HEADS ** -0.5),
        'ple_w': nrm((DEPTH, PLE_DIM, D_MODEL), 0.5 * PLE_DIM ** -0.5),
        'ple_gate': nrm((DEPTH, D_MODEL, D_MODEL), D_MODEL ** -0.5),
    }

def reference(x, p, norm_mix, norm_ffn, norm_ple, norm_final,
              ev_w_in, ev_conv_w, ev_conv_b, ev_dt_bias, ev_a_log, ev_d_skip, ev_out_norm, ev_sinks, ev_w_out,
              od_w_in, od_conv_w, od_conv_b, od_i_bias, od_f_bias, od_head_norm, od_w_out,
              pk_w_q, pk_sub_k1, pk_sub_k2, pk_u, pk_v, ple_w, ple_gate):
    for i in range(DEPTH):
        j = i // 2
        h = rmsnorm(x, norm_mix[i])
        if i % 2 == 0:
            x = x + even_mixer(h, ev_w_in[j], ev_conv_w[j], ev_conv_b[j], ev_dt_bias[j], ev_a_log[j],
                               ev_d_skip[j], ev_out_norm[j], ev_sinks[j], ev_w_out[j])
        else:
            x = x + mlstm_mixer(h, od_w_in[j], od_conv_w[j], od_conv_b[j], od_i_bias[j], od_f_bias[j],
                                od_head_norm[j], od_w_out[j])
        x = x + peer(rmsnorm(x, norm_ffn[i]), pk_w_q[i], pk_sub_k1[i], pk_sub_k2[i], pk_u[i], pk_v[i])
        gate = jax.nn.sigmoid(rmsnorm(x, norm_ple[i]) @ ple_gate[i])
        x = x + gate * (p[i] @ ple_w[i])
    return rmsnorm(x, norm_final)


_drawn_inputs = setup_inputs


def setup_inputs(seed=0):
    import zlib

    import numpy as np

    out = dict(_drawn_inputs(seed))
    spreads = {}
    factors = {'norm_mix': 3.047,
     'norm_ffn': 3.114,
     'norm_ple': 177.598,
     'norm_final': 23.432,
     'ev_conv_b': 3.181,
     'ev_d_skip': 113.61,
     'ev_out_norm': 4.446,
     'ev_sinks': 64.0,
     'od_conv_b': 39.39,
     'od_i_bias': 64.0,
     'od_head_norm': 77.155}
    for name, (base, spread) in spreads.items():
        noise = np.random.default_rng([zlib.crc32(name.encode()), seed]).standard_normal(out[name].shape)
        drawn = base * np.exp(spread * noise) if base else spread * noise
        out[name] = __import__('jax').numpy.asarray(drawn.astype(out[name].dtype))
    for name, factor in factors.items():
        out[name] = (out[name] * factor).astype(out[name].dtype)
    return out
```

```python
from contextlib import ExitStack

import concourse.bass as bass
import numpy as np
from concourse import mybir

F32 = mybir.dt.float32
F32R = mybir.dt.float32r
U32 = mybir.dt.uint32
ALU = mybir.AluOpType
ACT = mybir.ActivationFunctionType
AX_X = mybir.AxisListType.X

P = 128
T = 512
TT = T // P
D = 1024
DK = D // P
UNIT = DK * P
EPS = 1e-6
RAW = 4
SPL = 2
INNER = 1024
XBC = 12
CONV = 4
HEADS = 16
SEL = 16
PEER_HEADS = 8
KEYS = 128
BLOCK = 8
NBLOCK = KEYS // BLOCK
TG = 32
NTG = T // TG
NEG = -1e30

COLS = {}
_at = 0
for _name, _n in (("norm_mix0", 8), ("norm_mix1", 8), ("norm_ffn0", 8), ("norm_ffn1", 8),
                  ("norm_ple0", 8), ("norm_ple1", 8), ("norm_final", 8), ("out_norm", 8),
                  ("d_skip", 8), ("conv_w", 4 * XBC), ("conv_b", XBC), ("sinks", HEADS),
                  ("od_conv_w", 4 * 32), ("od_conv_b", 32), ("head_norm", HEADS),
                  ("dt_bias", 1), ("a_log", 1), ("i_bias", 1), ("f_bias", 1)):
    COLS[_name] = _at
    _at += _n
NPAR = _at


class Signal:

    def __init__(self, nc, ctx, name):
        self.sem = ctx.enter_context(nc.semaphore(name))
        self.base = 0

    def at(self, k):
        return self.base + k


class Chain:

    def __init__(self, eng, signal):
        self.eng, self.counter, self.n, self.off = eng, signal, 0, 0

    def __call__(self, ins):
        self.n += 1
        ins.then_inc(self.counter.sem, 1)
        self.eng.wait_ge(self.counter.sem, self.off + self.counter.base + self.n)

    def enter(self, i, per):
        self.off, self.start, self.per = i * per, self.n, per

    def leave(self, count):
        assert self.n - self.start == self.per, (self.n - self.start, self.per)
        self.n += self.per * (count - 1)
        self.off = 0

    def done(self):
        self.counter.base += self.n


class Program:
    def __init__(self, nc, ctx, dram):
        self.nc, self.ctx, self.dram = nc, ctx, dram
        self.unit = RAW
        self.out = 2
        self.sems = {}
        self.names = {}
        sb = self.sb
        self.x = sb("residual", [P, DK, T])
        self.hh = sb("h_hi", [P, DK, T], F32R)
        self.hl = sb("h_lo", [P, DK, T], F32R)
        self.yh = sb("y_hi", [P, DK, T], F32R)
        self.yl = sb("y_lo", [P, DK, T], F32R)
        self.raw = sb("w_raw", [P, RAW, UNIT])
        self.wh = sb("w_hi", [P, SPL, UNIT], F32R)
        self.wl = sb("w_lo", [P, SPL, UNIT], F32R)
        self.par = sb("params", [P, NPAR])
        self.ones = sb("ones", [P, P])
        self.ident = sb("ident", [P, P])
        self.incl = sb("incl", [P, T])
        self.after = sb("after", [P, P])
        self.iota = sb("iota", [P, P])
        self.ps = ctx.enter_context(nc.psum_tensor("ps", [P, 8, 512], F32))

    def sb(self, name, shape, dt=F32, ctx=None):
        n = self.names[name] = self.names.get(name, 0) + 1
        name = name if n == 1 else f"{name}_{n}"
        return (ctx or self.ctx).enter_context(self.nc.sbuf_tensor(name, shape, dt))

    def sig(self, name):
        if name not in self.sems:
            self.sems[name] = Signal(self.nc, self.ctx, name)
        return self.sems[name]

    def col(self, name, k=0, rows=P):
        c = COLS[name] + k
        return self.par[0:rows, c:c + 1]

    def load(self, sp, u, slot, src):
        hi, lo, loaded = self.sig("w_hi_ready"), self.sig("w_lo_ready"), self.sig(f"w_loaded{slot}")
        sp.wait_ge(hi.sem, u - RAW + 1)
        sp.wait_ge(lo.sem, u - RAW + 1)
        sp.dma_start(self.raw[:, slot, :], src).then_inc(loaded.sem, 16)

    def split_hi(self, act, u, slot, loads):
        act.wait_ge(self.sig(f"w_loaded{slot}").sem, 16 * loads)
        act.wait_ge(self.sig("w_used").sem, u - SPL + 1)
        self.nc.scalar.activation(self.wh[:, slot % SPL, :], self.raw[:, slot, :],
                                  ACT.Copy).then_inc(self.sig("w_hi_ready").sem, 1)

    def split_lo(self, dve, u, slot):
        dve.wait_ge(self.sig("w_hi_ready").sem, u + 1)
        self.nc.vector.tensor_tensor(self.wl[:, slot % SPL, :], self.raw[:, slot, :],
                                     self.wh[:, slot % SPL, :].bitcast(F32),
                                     ALU.subtract).then_inc(self.sig("w_lo_ready").sem, 1)

    def product(self, pe, u, slot, out, rh, rl, first=True, last=True, tiles=range(DK), wait_tile=None):
        pe.wait_ge(self.sig("w_lo_ready").sem, u + 1)
        s = slot % SPL
        n = len(tiles)
        for j, k in enumerate(tiles):
            if wait_tile is not None:
                wait_tile(k)
            w = slice(j * P, (j + 1) * P)
            for m, (a, b) in enumerate(((self.wh, rh), (self.wh, rl), (self.wl, rh))):
                ins = self.nc.tensor.matmul(out, a[:, s, w], b[:, k, :], start=first and j == 0 and m == 0,
                                            stop=last and j == n - 1 and m == 2)
        return ins


def prefetch(p, sp, srcs):
    for j, s in enumerate(srcs):
        u = p.unit + j
        p.load(sp, u, u % RAW, s)


def start(p, nxt):
    nc = p.nc
    ld, const = p.sig("inputs_loaded"), p.sig("const_ready")
    with nc.Block() as block:
        @block.sync
        def _(sp):
            for j in range(RAW):
                sp.sem_inc(p.sig(f"w_loaded{j}").sem, 16)
            sp.dma_start(p.x[:, :, :], p.dram["x"]).then_inc(ld.sem, 16)
            sp.dma_start(p.par[:, :], p.dram["par"]).then_inc(ld.sem, 16)
            prefetch(p, sp, nxt)
            sp.wait_ge(ld.sem, 32)

        @block.scalar
        def _(act):
            act.sem_inc(p.sig("w_hi_ready").sem, RAW)
            p.split_hi(act, RAW, 0, 2)

        @block.tensor
        def _(pe):
            pe.sem_inc(p.sig("w_used").sem, RAW)

        @block.vector
        def _(dve):
            dve.sem_inc(p.sig("w_lo_ready").sem, RAW)
            dve.sem_inc(p.sig("out_taken").sem, 2)
            p.split_lo(dve, RAW, 0)

        @block.gpsimd
        def _(pool):
            nc.gpsimd.memset(p.ones[:, :], 1.0)
            nc.gpsimd.memset(p.incl[:, :], 1.0)
            nc.gpsimd.memset(p.after[:, :], 1.0)
            nc.gpsimd.iota(p.iota[:, :], pattern=[[1, P]], base=0, channel_multiplier=0,
                           allow_small_or_imprecise_dtypes=True)
            nc.gpsimd.memset(p.ident[:, :], 0.0).then_inc(const.sem, 1)
            pool.wait_ge(const.sem, 1)
            nc.gpsimd.affine_select(out=p.ident[:, :], in_=p.ident[:, :], compare_op=ALU.not_equal,
                                    fill=1.0, base=0, pattern=[[-1, P]], channel_multiplier=1)
            nc.gpsimd.affine_select(out=p.incl[:, :], in_=p.incl[:, :], compare_op=ALU.is_ge,
                                    fill=0.0, base=0, pattern=[[1, T]], channel_multiplier=-1)
            nc.gpsimd.affine_select(out=p.after[:, :], in_=p.after[:, :], compare_op=ALU.is_ge,
                                    fill=0.0, base=-1, pattern=[[-1, P]], channel_multiplier=1)
    const.base += 1
    ld.base += 32


def norm(p, src, gain, out=None, dst=None, nxt=()):
    nc = p.nc
    sq, ssum, root, scaled, hi_done = (p.sig(n) for n in ("squared", "sumsq", "root", "scaled", "norm_hi"))
    chain = p.sig("dve_chain")
    with ExitStack() as ctx:
        s2 = p.sb("squares", [P, 2, T], ctx=ctx)
        rstd = p.sb("rstd", [P, T], ctx=ctx)
        hf = p.sb("normed", [P, 2, T], ctx=ctx)
        block = ctx.enter_context(nc.Block())

        @block.sync
        def _(sp):
            prefetch(p, sp, nxt)

        @block.scalar
        def _(act):
            for k in range(DK):
                if k >= 2:
                    act.wait_ge(ssum.sem, ssum.at(k - 1))
                nc.scalar.activation(s2[:, k % 2, :], src[:, k, :], ACT.Square).then_inc(sq.sem, 1)
            act.wait_ge(ssum.sem, ssum.at(DK))
            nc.scalar.activation(rstd[:, :], p.ps[:, 7, :], ACT.Copy, scale=1.0 / (DK * P),
                                 bias=EPS).then_inc(root.sem, 1)
            act.wait_ge(root.sem, root.at(1))
            nc.scalar.activation(rstd[:, :], rstd[:, :], ACT.Sqrt).then_inc(root.sem, 1)
            if out is not None:
                for k in range(DK):
                    act.wait_ge(scaled.sem, scaled.at(k + 1))
                    nc.scalar.activation(out[0][:, k, :], hf[:, k % 2, :], ACT.Copy).then_inc(hi_done.sem, 1)

        @block.tensor
        def _(pe):
            for k in range(DK):
                pe.wait_ge(sq.sem, sq.at(k + 1))
                nc.tensor.matmul(p.ps[:, 7, :], p.ones[:, :], s2[:, k % 2, :], start=(k == 0),
                                 stop=(k == DK - 1)).then_inc(ssum.sem, 1)

        @block.vector
        def _(dve):
            link = Chain(dve, chain)
            dve.wait_ge(root.sem, root.at(2))
            link(nc.vector.reciprocal(rstd[:, :], rstd[:, :]))
            for k in range(DK + 1):
                if k < DK:
                    o = hf[:, k % 2, :] if out is not None else dst[:, k, :]
                    if out is not None and k >= 2:
                        dve.wait_ge(hi_done.sem, hi_done.at(k - 1))
                    nc.vector.scalar_tensor_tensor(out=o, in0=src[:, k, :], scalar=p.col(gain, k),
                                                   in1=rstd[:, :], op0=ALU.mult,
                                                   op1=ALU.mult).then_inc(scaled.sem, 1)
                if k and out is not None:
                    dve.wait_ge(hi_done.sem, hi_done.at(k))
                    link(nc.vector.tensor_tensor(out[1][:, k - 1, :], hf[:, (k - 1) % 2, :],
                                                 out[0][:, k - 1, :].bitcast(F32), ALU.subtract))
            link.done()
    sq.base += DK
    ssum.base += DK
    root.base += 2
    scaled.base += DK
    if out is not None:
        hi_done.base += DK


def steps_of(p, jobs):
    u, o = p.unit, p.out
    for job in jobs:
        n, per = job[1], job[2]
        each = min(n, RAW)
        assert n % each == 0 and each % per == 0 and (each // per) % 2 == 0 and o % 2 == 0
        yield u, o, n // each, each, job
        u += n
        o += n // per


def looped(eng, p, jobs, body, skip=0):
    for u, o, count, each, job in steps_of(p, jobs):
        lo, skip = skip, 0
        if count - lo <= 0:
            continue
        if count - lo == 1:
            body(u + each * lo, o + each // job[2] * lo, lo, each, job, u)
        else:
            with eng.Fori(lo, count) as i:
                body(i * each + u, i * (each // job[2]) + o, i, each, job, u)


def linear(p, jobs, nxt):
    nc = p.nc
    used, taken = p.sig("w_used"), p.sig("out_taken")
    total = sum(j[1] for j in jobs)
    with nc.Block() as block:
        @block.sync
        def _(sp):
            def body(u, o, i, each, job, at):
                for j in range(each):
                    p.load(sp, u + j, (at + j) % RAW, job[0][i * each + j, :, :])
            assert min(jobs[0][1], RAW) == RAW
            looped(sp, p, jobs, body, skip=1)
            p.unit += total
            prefetch(p, sp, nxt)
            p.unit -= total

        @block.scalar
        def _(act):
            def body(u, o, i, each, job, at):
                for j in range(1, each + 1):
                    loads = (at + j) // RAW + 1
                    if each == RAW:
                        loads = i + loads
                    p.split_hi(act, u + j, (at + j) % RAW, loads)
            looped(act, p, jobs, body)

        @block.vector
        def _(dve):
            def body(u, o, i, each, job, at):
                per = job[2]
                for j in range(each):
                    p.split_lo(dve, u + j + 1, (at + j + 1) % RAW)
                    if j % per == per - 1:
                        q = j // per
                        dve.wait_ge(used.sem, u + j + 1)
                        job[4](i * (each // per) + q, p.ps[:, q % 2, :]).then_inc(taken.sem, 1)
            looped(dve, p, jobs, body)

        @block.tensor
        def _(pe):
            def body(u, o, i, each, job, at):
                per = job[2]
                for j in range(each):
                    q = j // per
                    if j % per == 0:
                        pe.wait_ge(taken.sem, o + q - 1)
                    rh, rl = job[3][j % per]
                    p.product(pe, u + j, (at + j) % RAW, p.ps[:, q % 2, :], rh, rl,
                              first=j % per == 0, last=j % per == per - 1).then_inc(used.sem, 1)
            looped(pe, p, jobs, body)
    p.unit += total
    p.out += sum(j[1] // j[2] for j in jobs)


def even_in(p, b, nxt):
    nc = p.nc
    with nc.Block() as block:
        @block.gpsimd
        def _(pool):
            nc.gpsimd.memset(b["xbc"][:, :, 0:CONV - 1], 0.0)
            nc.gpsimd.memset(b["kd"][:, :, :], 0.0)
            nc.gpsimd.memset(b["vt"][:, :], 0.0)
    h = [(p.hh, p.hl)]
    w = p.dram["ev_in"]
    v = nc.vector

    def tail(i, psum):
        if i < 2:
            return v.tensor_copy(b["kd"][:, i, 64:64 + T], psum)
        if i == 2:
            return v.tensor_copy(b["vt"][:, 64:64 + T], psum)
        return v.tensor_copy(b["dtraw"][:, :], psum[0:HEADS, :])

    linear(p, [(w, 8, 1, h, lambda i, ps: v.tensor_copy(b["z"][:, i, :], ps)),
               (w[8:20], XBC, 1, h, lambda i, ps: v.tensor_copy(b["xbc"][:, i, CONV - 1:], ps)),
               (w[20:28], 8, 1, h, lambda i, ps: v.tensor_copy(b["q"][:, i, :], ps)),
               (w[28:32], 4, 1, h, tail)], nxt)


def conv_steps(nc, link, src, dst, taps, bias):
    v = nc.vector
    link(v.tensor_scalar(dst[0], src[:, 0:T], taps[0], bias, ALU.mult, ALU.add))
    for k in range(1, CONV):
        ins = v.scalar_tensor_tensor(out=dst[k % 2], in0=src[:, k:k + T], scalar=taps[k],
                                     in1=dst[(k - 1) % 2], op0=ALU.mult, op1=ALU.add)
        if k < CONV - 1:
            link(ins)
    return ins


def log1p_rows(v, link, rows, small, src, bias, xb, ab, e1, ln, rc):
    dve = link.eng
    link(v.tensor_scalar(xb[:, :], src, bias, None, ALU.add))
    v.scalar_tensor_tensor(out=ab[:, :], in0=xb[:, :], scalar=-1.0, in1=xb[:, :], op0=ALU.mult,
                           op1=ALU.max).then_inc(rows.sem, 1)
    dve.wait_ge(small.sem, small.at(1))
    v.tensor_scalar(ab[:, :], e1[:, :], 1.0, None, ALU.add).then_inc(rows.sem, 1)
    dve.wait_ge(rows.sem, rows.at(2))
    link(v.reciprocal(rc[:, :], ab[:, :]))
    dve.wait_ge(small.sem, small.at(2))
    link(v.tensor_scalar(ab[:, :], ab[:, :], -1.0, None, ALU.add))
    link(v.tensor_tensor(ab[:, :], e1[:, :], ab[:, :], ALU.subtract))
    link(v.tensor_tensor(ab[:, :], ab[:, :], rc[:, :], ALU.mult))
    link(v.tensor_tensor(ln[:, :], ln[:, :], ab[:, :], ALU.add))


def log1p_act(act, nc, rows, small, e1, ab, ln):
    act.wait_ge(rows.sem, rows.at(1))
    nc.scalar.activation(e1[:, :], ab[:, :], ACT.Exp, scale=-1.0).then_inc(small.sem, 1)
    act.wait_ge(rows.sem, rows.at(2))
    nc.scalar.activation(ln[:, :], ab[:, :], ACT.Ln).then_inc(small.sem, 1)


def even_conv(p, b):
    nc = p.nc
    conv, silu, small, rows = (p.sig(n) for n in ("conv_done", "silu_done", "act_small", "rows_ready"))
    dchain = p.sig("dve_chain")
    H = HEADS
    with ExitStack() as ctx:
        tmp = p.sb("conv_sums", [P, 2, T], ctx=ctx)
        xb = p.sb("dt_biased", [H, T], ctx=ctx)
        ab = p.sb("dt_abs", [H, T], ctx=ctx)
        e1 = p.sb("dt_exp", [H, T], ctx=ctx)
        ln = p.sb("dt_log", [H, T], ctx=ctx)
        rc = p.sb("dt_recip", [H, T], ctx=ctx)
        na = p.sb("a_neg", [H, 1], ctx=ctx)
        block = ctx.enter_context(nc.Block())

        @block.vector
        def _(dve):
            v = nc.vector
            link = Chain(dve, dchain)
            log1p_rows(v, link, rows, small, b["dtraw"][:, :], p.col("dt_bias", 0, H), xb, ab, e1, ln, rc)
            link(v.tensor_scalar(xb[:, :], xb[:, :], 0.0, None, ALU.max))
            link(v.tensor_tensor(b["dt"][:, :], xb[:, :], ln[:, :], ALU.add))
            dve.wait_ge(small.sem, small.at(3))
            link(v.tensor_scalar(na[:, :], na[:, :], -1.0, None, ALU.mult))
            link(v.tensor_scalar(b["adt"][:, :], b["dt"][:, :], na[:, 0:1], None, ALU.mult))
            with dve.Fori(0, XBC) as c:
                link.enter(c, CONV - 1)
                dve.wait_ge(silu.sem, c + silu.base + 1)
                conv_steps(nc, link, b["xbc"][:, c, :], (tmp[:, 0, :], tmp[:, 1, :]),
                           [p.par[:, bass.ds(c * CONV + COLS["conv_w"] + k, 1)] for k in range(CONV)],
                           p.par[:, bass.ds(c + COLS["conv_b"], 1)]).then_inc(conv.sem, 1)
                link.leave(XBC)
            link.done()

        @block.scalar
        def _(act):
            log1p_act(act, nc, rows, small, e1, ab, ln)
            nc.scalar.activation(na[:, :], p.col("a_log", 0, H), ACT.Exp).then_inc(small.sem, 1)
            act.sem_inc(silu.sem, 1)
            with act.Fori(0, XBC) as c:
                act.wait_ge(conv.sem, c + conv.base + 1)
                nc.scalar.activation(b["xbc"][:, c, CONV - 1:], tmp[:, 1, :], ACT.Silu).then_inc(silu.sem, 1)
    conv.base += XBC
    silu.base += XBC + 1
    small.base += 3
    rows.base += 2


def even_attention(p, b):
    nc = p.nc
    names = ("att_q", "att_scores", "att_masked", "att_shifted", "att_exp", "att_sink", "att_probs",
             "att_turned", "att_copied", "att_out", "att_hi", "att_lo", "att_v", "att_masks", "att_v_taken")
    sq, sc, sm, sh, se, sk, sp_, st, sy, so, shi, slo, sv, sma, svt = (p.sig(n) for n in names)
    dchain = p.sig("dve_chain")
    SC = 64 ** -0.5
    G = 8
    with ExitStack() as ctx:
        qb = p.sb("q_tile", [P, 8, P], ctx=ctx)
        vb = p.sb("v_tiles", [P, 2, P], ctx=ctx)
        kb = p.sb("k_window", [P, 2, 192], ctx=ctx)
        vp = b["vt"][:, :].rearrange("p (m t) -> p m t", t=P)
        mask = p.sb("att_mask", [P, 2, 192], ctx=ctx)
        S = p.sb("scores", [P, G, 192], ctx=ctx)
        mx = p.sb("att_max", [P, G], ctx=ctx)
        es = p.sb("att_sink_exp", [P, G], ctx=ctx)
        sm_ = p.sb("att_sum", [P, G], ctx=ctx)
        pt = p.sb("probs_turned", [P, 2, G * P], ctx=ctx)
        block = ctx.enter_context(nc.Block())
        per = 2

        @block.gpsimd
        def _(pool):
            g = nc.gpsimd
            g.memset(mask[:, :, :], 0.0).then_inc(sma.sem, 1)
            pool.wait_ge(sma.sem, sma.at(1))
            g.memset(mask[64:P, :, 0:64], NEG)
            g.memset(mask[0:64, :, 128:192], NEG).then_inc(sma.sem, 1)
            pool.wait_ge(sma.sem, sma.at(2))
            g.memset(mask[:, 0, 0:64], NEG).then_inc(sma.sem, 1)

        @block.tensor
        def _(pe):
            for m in range(5):
                ins = nc.tensor.transpose(p.ps[:, m // 4, (m % 4) * P:(m % 4 + 1) * P],
                                          b["vt"][:, m * P:(m + 1) * P], p.ident[:, :])
            ins.then_inc(sv.sem, 1)
            pe.wait_ge(svt.sem, svt.at(1))
            with pe.Fori(0, TT) as j:
                pe.wait_ge(sq.sem, j + sq.base + 1)
                for g in range(per):
                    r = j * per + g
                    pe.wait_ge(sm.sem, r + sm.base + 1)
                    for h in range(G):
                        hd = g * G + 2 * (h % 4) + h // 4
                        rows = slice(64 * (hd % 2), 64 * (hd % 2) + 64)
                        ins = nc.tensor.matmul(p.ps[:, h // 2, (h % 2) * 256:(h % 2) * 256 + 192],
                                               qb[rows, hd // 2, :],
                                               kb[rows, g, :], start=True, stop=True)
                    ins.then_inc(sc.sem, 1)
                    pe.wait_ge(sp_.sem, r + sp_.base + 1)
                    for h in range(G):
                        nc.tensor.transpose(p.ps[:, 4 + h // 4, (h % 4) * P:(h % 4 + 1) * P],
                                            S[:, h, 0:P], p.ident[:, :])
                        ins = nc.tensor.transpose(p.ps[0:64, 6 + h // 4, (h % 4) * P:(h % 4 + 1) * P],
                                                  S[:, h, P:192], p.ident[:, :])
                    ins.then_inc(st.sem, 1)
                    pe.wait_ge(sy.sem, r + sy.base + 1)
                    for h in range(G):
                        c = slice(64 * g, 64 * g + 64)
                        o = p.ps[64 * (h // 4):64 * (h // 4) + 64, 4, (h % 4) * P:(h % 4 + 1) * P]
                        nc.tensor.matmul(o, vb[:, 0, c], pt[:, 0, h * P:(h + 1) * P], start=True, stop=False)
                        ins = nc.tensor.matmul(o, vb[0:64, 1, c], pt[0:64, 1, h * P:(h + 1) * P], start=False, stop=True)
                    ins.then_inc(so.sem, 1)
                    pe.wait_ge(slo.sem, r + slo.base + 1)

        @block.scalar
        def _(act):
            a = nc.scalar
            with act.Fori(0, TT) as j:
                for g in range(per):
                    r = j * per + g
                    act.wait_ge(sh.sem, r + sh.base + 1)
                    a.activation(es[:, :], es[:, :], ACT.Exp).then_inc(sk.sem, 1)
                    a.activation(S[:, :, :], S[:, :, :], ACT.Exp).then_inc(se.sem, 1)
                    act.wait_ge(st.sem, r + st.base + 1)
                    a.activation(pt[:, 0, :], p.ps[:, 4:6, :].rearrange("p b m -> p (b m)"), ACT.Copy)
                    a.activation(pt[0:64, 1, :], p.ps[0:64, 6:8, :].rearrange("p b m -> p (b m)"),
                                 ACT.Copy).then_inc(sy.sem, 1)
                    act.wait_ge(so.sem, r + so.base + 1)
                    a.activation(p.yh[:, g * 4:g * 4 + 4, bass.ds(j * P, P)],
                                 p.ps[:, 4, :].rearrange("p (h t) -> p h t", h=4), ACT.Copy).then_inc(shi.sem, 1)

        @block.vector
        def _(dve):
            v = nc.vector
            link = Chain(dve, dchain)
            dve.wait_ge(sma.sem, sma.at(3))
            dve.wait_ge(sv.sem, sv.at(1))
            v.tensor_copy(vp[:, 0:4, :], p.ps[:, 0, :].rearrange("p (m t) -> p m t", m=4))
            link(v.tensor_copy(vp[:, 4, :], p.ps[:, 1, 0:P]))
            dve.sem_inc(svt.sem, 1)
            dve.sem_inc(sm.sem, 1)
            with dve.Fori(0, TT) as j:
                link.enter(j, 2 + 7 * per)
                link(v.tensor_copy(qb[:, :, :], b["q"][:, :, bass.ds(j * P, P)]))
                v.tensor_copy(kb[:, :, :], b["kd"][:, :, bass.ds(j * P, 192)])
                v.tensor_copy(vb[:, :, :], vp[:, bass.ds(j, 2), :]).then_inc(sq.sem, 1)
                for g in range(per):
                    r = j * per + g
                    sink = p.par[:, COLS["sinks"] + g * G:COLS["sinks"] + (g + 1) * G]
                    dve.wait_ge(sc.sem, r + sc.base + 1)
                    raw = p.ps[:, 0:4, :].rearrange("p b (h m) -> p (b h) m", h=2)[:, :, 0:192]
                    m = mask[:, 0, :].unsqueeze(1).to_broadcast([P, G, 192])
                    ins = v.scalar_tensor_tensor(out=S[:, :, :], in0=raw, scalar=SC, in1=m, op0=ALU.mult, op1=ALU.add)
                    link(ins)
                    dve.sem_inc(sm.sem, 1)
                    link(v.tensor_reduce(mx[:, :], S[:, :, :], AX_X, ALU.max))
                    link(v.tensor_tensor(mx[:, :], mx[:, :], sink, ALU.max))
                    link(v.tensor_tensor(es[:, :], sink, mx[:, :], ALU.subtract))
                    v.tensor_tensor(S[:, :, :], S[:, :, :], mx[:, :].unsqueeze(2).to_broadcast([P, G, 192]),
                                    ALU.subtract).then_inc(sh.sem, 1)
                    dve.wait_ge(se.sem, r + se.base + 1)
                    dve.wait_ge(sk.sem, r + sk.base + 1)
                    link(v.tensor_reduce(sm_[:, :], S[:, :, :], AX_X, ALU.add))
                    link(v.tensor_tensor(sm_[:, :], sm_[:, :], es[:, :], ALU.add))
                    link(v.reciprocal(sm_[:, :], sm_[:, :]))
                    v.tensor_tensor(S[:, :, :], S[:, :, :], sm_[:, :].unsqueeze(2).to_broadcast([P, G, 192]),
                                    ALU.mult).then_inc(sp_.sem, 1)
                    dve.wait_ge(shi.sem, r + shi.base + 1)
                    y = slice(g * 4, g * 4 + 4)
                    v.tensor_tensor(p.yl[:, y, bass.ds(j * P, P)],
                                    p.ps[:, 4, :].rearrange("p (h t) -> p h t", h=4),
                                    p.yh[:, y, bass.ds(j * P, P)].bitcast(F32), ALU.subtract).then_inc(slo.sem, 1)
                link(v.tensor_copy(mask[:, 0, :], mask[:, 1, :]))
                link.leave(TT)
            link.done()
    n = TT * per
    sq.base += TT
    for s in (sc, sh, se, sk, sp_, st, sy, so, shi, slo):
        s.base += n
    sm.base += n + 1
    sv.base += 1
    sma.base += 3
    svt.base += 1


def even_ssd(p, b):
    nc = p.nc
    names = ("ssd_turned", "ssd_cols", "ssd_cb", "ssd_cb_done", "ssd_x", "ssd_xt", "ssd_xdt", "ssd_factors",
             "ssd_arg", "ssd_exp", "ssd_m", "ssd_z", "ssd_out", "ssd_m_used", "ssd_decays")
    (tn, co, cb, cbd, sx, sxt, sxd, fa, ar, ex, sm, sz, ou, mf, dc) = (p.sig(n) for n in names)
    dchain = p.sig("dve_chain")
    H = HEADS
    with ExitStack() as ctx:
        cbm = b["q"]
        cols = p.sb("dt_cols", [P, 2, TT, H + 2], ctx=ctx)
        ac = p.sb("decay_cols", [P, TT, 2], ctx=ctx)
        xs = p.sb("x_pair", [P, T], ctx=ctx)
        xd = p.sb("x_dt", [P, TT, P], ctx=ctx)
        fa1 = p.sb("decays_after", [P, 2, TT, P], ctx=ctx)
        fb1 = p.sb("decays_all", [P, 2, TT, P], ctx=ctx)
        E = p.sb("decay_exp", [P, 2, T], ctx=ctx)
        M = p.sb("ssd_weights", [P, 2, T], ctx=ctx)
        zs = p.sb("z_silu", [P, T], ctx=ctx)
        yt = xs
        block = ctx.enter_context(nc.Block())

        def width(i):
            return T - i * P

        @block.tensor
        def _(pe):
            t = nc.tensor
            for k in range(2):
                for j in range(TT):
                    ins = t.transpose(p.ps[:, 6, (k * TT + j) * H:(k * TT + j + 1) * H],
                                      b[("adt", "dt")[k]][:, j * P:(j + 1) * P], p.ident[0:H, 0:H])
            ins.then_inc(tn.sem, 1)
            for g in range(2):
                if g:
                    pe.wait_ge(cbd.sem, cbd.at(4))
                for i in range(TT):
                    ins = t.matmul(p.ps[:, i, 0:width(i)], b["xbc"][:, 8 + g, 3 + i * P:3 + (i + 1) * P],
                                   b["xbc"][:, 10 + g, 3 + i * P:], start=True, stop=True)
                ins.then_inc(cb.sem, 1)
            pe.wait_ge(cbd.sem, cbd.at(8))
            pe.sem_inc(mf.sem, 2)
            pe.sem_inc(ar.sem, 8)
            for g in range(2):
                with pe.Fori(0, 4) as cc:
                    c = cc + 4 * g
                    pe.wait_ge(sx.sem, c + sx.base + 1)
                    for j in range(TT):
                        ins = t.transpose(p.ps[:, 4, j * P:(j + 1) * P], xs[:, j * P:(j + 1) * P], p.ident[:, :])
                    ins.then_inc(sxt.sem, 1)

                    def weigh(n):
                        h, i = divmod(n, TT)
                        pe.wait_ge(sm.sem, c * 8 + sm.base + n + 3)
                        if n == 0:
                            pe.wait_ge(sxd.sem, c + sxd.base + 1)
                        o = p.ps[64 * h:64 * h + 64, 5, i * P:T]
                        return t.matmul(o, xd[:, i, 64 * h:64 * h + 64], M[:, n % 2, 0:width(i)],
                                        start=i == 0, stop=i == TT - 1, skip_group_check=True)

                    for n in range(8):
                        h, i = divmod(n, TT)
                        if i == 0:
                            pe.wait_ge(fa.sem, c * 2 + fa.base + h + 1)
                        pe.wait_ge(ex.sem, c * 8 + ex.base + n + 1)
                        bank = p.ps[:, n % 2, :]
                        for j in range(i, TT):
                            f = fa1 if j == i else fb1
                            ins = t.matmul(bank[:, (j - i) * P:width(i)], f[:, h, j, :], p.incl[:, 0:width(j)],
                                           start=j == i, stop=j == TT - 1, skip_group_check=True)
                        ins.then_inc(ar.sem, 1)
                        if n:
                            weigh(n - 1).then_inc(mf.sem, 1)
                    ins = weigh(7)
                    ins.then_inc(mf.sem, 1)

        @block.scalar
        def _(act):
            a = nc.scalar
            act.sem_inc(ex.sem, 2)
            with act.Fori(0, 8) as c:
                act.wait_ge(ou.sem, c + ou.base + 1)
                a.activation(zs[:, :], b["z"][:, c, :], ACT.Silu).then_inc(sz.sem, 1)
                for n in range(8):
                    i = n % TT
                    act.wait_ge(ar.sem, c * 8 + ar.base + 8 + n + 1)
                    act.wait_ge(sm.sem, c * 8 + sm.base + n + 1)
                    a.activation(E[:, n % 2, 0:width(i)], p.ps[:, n % 2, 0:width(i)], ACT.Exp).then_inc(ex.sem, 1)

        @block.gpsimd
        def _(pool):
            g_ = nc.gpsimd
            with pool.Fori(0, 8) as c:
                pool.wait_ge(dc.sem, c + dc.base + 1)
                for h in range(2):
                    pool.wait_ge(ar.sem, c * 8 + ar.base + 4 * h + 4)
                    s = ac[:, :, h:h + 1].to_broadcast([P, TT, P])
                    g_.tensor_tensor(fa1[:, h, :, :], p.after[:, :].unsqueeze(1).to_broadcast([P, TT, P]),
                                     s, ALU.mult)
                    g_.tensor_copy(fb1[:, h, :, :], s).then_inc(fa.sem, 1)

        @block.vector
        def _(dve):
            v = nc.vector
            link = Chain(dve, dchain)
            dve.wait_ge(tn.sem, tn.at(1))
            v.memset(cols[:, :, :, H:], 0.0)
            v.tensor_copy(cols[:, :, :, 0:H],
                          p.ps[:, 6, 0:2 * TT * H].rearrange("p (k j h) -> p k j h", k=2, j=TT)
                          ).then_inc(co.sem, 1)
            for g in range(2):
                dve.wait_ge(cb.sem, cb.at(g + 1))
                for i in range(TT):
                    v.tensor_tensor(cbm[:, g * TT + i, 0:width(i)], p.ps[:, i, 0:width(i)],
                                    p.incl[:, 0:width(i)], ALU.mult).then_inc(cbd.sem, 1)
            dve.wait_ge(cbd.sem, cbd.at(8))
            dve.wait_ge(co.sem, co.at(1))
            v.tensor_copy(ac[:, :, :], cols[:, 0, :, 0:2]).then_inc(dc.sem, 1)
            dve.sem_inc(ou.sem, 1)
            dve.sem_inc(sm.sem, 2)
            for g in range(2):
                with dve.Fori(0, 4) as cc:
                    c = cc + 4 * g
                    link.enter(cc, 2)
                    v.tensor_copy(xs[:, :], b["xbc"][:, c, 3:]).then_inc(sx.sem, 1)
                    dve.wait_ge(sxt.sem, c + sxt.base + 1)
                    for h in range(2):
                        ins = v.tensor_tensor(
                            xd[:, :, 64 * h:64 * h + 64],
                            p.ps[:, 4, :].rearrange("p (j q) -> p j q", j=TT)[:, :, 64 * h:64 * h + 64],
                            cols[:, 1, :, bass.ds(c * 2 + h, 1)].to_broadcast([P, TT, 64]), ALU.mult)
                    ins.then_inc(sxd.sem, 1)
                    for n in range(8):
                        i = n % TT
                        dve.wait_ge(ex.sem, c * 8 + ex.base + n + 3)
                        dve.wait_ge(mf.sem, c * 8 + mf.base + n + 1)
                        v.tensor_tensor(M[:, n % 2, 0:width(i)], E[:, n % 2, 0:width(i)],
                                        cbm[:, g * TT + i, 0:width(i)], ALU.mult).then_inc(sm.sem, 1)
                        if n == 4:
                            v.tensor_copy(ac[:, :, :], cols[:, 0, :, bass.ds(c * 2 + 2, 2)]).then_inc(dc.sem, 1)
                    dve.wait_ge(mf.sem, c * 8 + mf.base + 8 + 2)
                    link(v.scalar_tensor_tensor(out=yt[:, :], in0=xs[:, :],
                                                scalar=p.par[:, bass.ds(c + COLS["d_skip"], 1)],
                                                in1=p.ps[:, 5, :], op0=ALU.mult, op1=ALU.add))
                    dve.wait_ge(sz.sem, c + sz.base + 1)
                    link(v.tensor_tensor(b["z"][:, c, :], yt[:, :], zs[:, :], ALU.mult))
                    dve.sem_inc(ou.sem, 1)
                    link.leave(4)
            link.done()
    for s, n in ((tn, 1), (co, 1), (cb, 2), (cbd, 8), (sx, 8), (sxt, 8), (sxd, 8), (fa, 16), (ar, 72),
                 (ex, 66), (sm, 66), (mf, 66), (sz, 8), (ou, 9), (dc, 9)):
        s.base += n


def peer_topk(p, b, u_src, sub):
    nc = p.nc
    names = ("q_taken", "scores_ready", "scores_taken", "topk_free")
    qt, sr, stk, tf = (p.sig(n) for n in names)
    used, dchain = p.sig("w_used"), p.sig("dve_chain")
    with ExitStack() as ctx:
        subk = p.sb("sub_keys", [P, 16, KEYS], ctx=ctx)
        qf = p.sb("peer_q", [P, 2, T], ctx=ctx)
        s1 = p.sb("peer_scores", [P, 2, TT * KEYS], ctx=ctx)
        s2 = p.sb("peer_scores_left", [P, TT * KEYS], ctx=ctx)
        V = p.sb("side_top", [P, TT, 2, SEL], ctx=ctx)
        I = p.sb("side_index", [P, TT, 2, SEL], U32, ctx=ctx)
        cs = p.sb("pair_sums", [P, TT, SEL * SEL], ctx=ctx)
        held = p.sb("wait_holder", [P, 4], ctx=ctx)
        tv = p.sb("pair_top", [P, TT, SEL], ctx=ctx)
        ti = p.sb("pair_pos", [P, TT, SEL], U32, ctx=ctx)
        cl = p.sb("pair_sums_left", [P, TT, SEL * SEL], ctx=ctx)
        u0 = p.unit
        N = 2 * PEER_HEADS
        block = ctx.enter_context(nc.Block())
        sl = p.sig("sub_loaded")

        @block.sync
        def _(sp):
            sp.dma_start(subk[:, :, :], sub).then_inc(sl.sem, 16)
            with sp.Fori(1, N // 4) as i:
                for j in range(4):
                    p.load(sp, i * 4 + u0 + j, (u0 + j) % RAW, u_src[i * 4 + j, :, :])
            p.unit += N
            prefetch(p, sp, b["next"])
            p.unit -= N
            sp.wait_ge(sl.sem, sl.at(16))

        @block.tensor
        def _(pe):
            pe.wait_ge(sl.sem, sl.at(16))
            pe.sem_inc(sr.sem, 2)
            with pe.Fori(0, N // 4) as i:
                for j in range(4):
                    u = i * 4 + u0 + j
                    p.product(pe, u, (u0 + j) % RAW, p.ps[:, j % 2, :], p.hh, p.hl).then_inc(used.sem, 1)
                    pe.wait_ge(qt.sem, i * 4 + qt.base + j + 1)
                    pe.wait_ge(stk.sem, i * 4 + stk.base + j + 1)
                    for t in range(TT):
                        ins = nc.tensor.matmul(p.ps[:, 2 + j % 2, t * KEYS:(t + 1) * KEYS],
                                               qf[:, j % 2, t * P:(t + 1) * P],
                                               subk[:, i * 4 + j, :], start=True, stop=True)
                    ins.then_inc(sr.sem, 1)

        @block.scalar
        def _(act):
            act.sem_inc(stk.sem, 2)
            with act.Fori(0, N // 4) as i:
                for j in range(4):
                    act.wait_ge(used.sem, i * 4 + u0 + j + 1)
                    act.wait_ge(sr.sem, i * 4 + sr.base + j + 1)
                    nc.scalar.activation(qf[:, j % 2, :], p.ps[:, j % 2, :], ACT.Copy).then_inc(qt.sem, 1)
                    p.split_hi(act, i * 4 + u0 + j + 1, (u0 + j + 1) % RAW, i + (u0 + j + 1) // RAW + 1)
                    act.wait_ge(sr.sem, i * 4 + sr.base + j + 3)
                    act.wait_ge(tf.sem, i * 4 + tf.base + j + 1)
                    nc.scalar.activation(s1[:, j % 2, :], p.ps[:, 2 + j % 2, :], ACT.Copy).then_inc(stk.sem, 1)

        @block.vector
        def _(dve):
            v = nc.vector
            link = Chain(dve, dchain)
            dve.sem_inc(tf.sem, 2)

            def top16(values, left, vals, index):
                v.memset(held[:, 0:1], 0.0)
                for t in range(TT):
                    ins = v.max(out=vals[t][:, 0:8], in_=values[t])
                link(ins)
                v.memset(held[:, 1:2], 0.0)
                for t in range(TT):
                    v.max_index(out=index[t][:, 0:8], in_max=vals[t][:, 0:8], in_values=values[t])
                    ins = v.match_replace(out=left[t], in_to_replace=vals[t][:, 0:8], in_values=values[t],
                                          imm_value=-3.0e38)
                link(ins)
                v.memset(held[:, 2:3], 0.0)
                for t in range(TT):
                    ins = v.max(out=vals[t][:, 8:16], in_=left[t])
                link(ins)
                v.memset(held[:, 3:4], 0.0)
                for t in range(TT):
                    ins = v.max_index(out=index[t][:, 8:16], in_max=vals[t][:, 8:16], in_values=left[t])
                return ins

            with dve.Fori(0, N // 4) as i:
                link.enter(i, 24)
                for j in range(4):
                    side = j % 2
                    p.split_lo(dve, i * 4 + u0 + j + 1, (u0 + j + 1) % RAW)
                    dve.wait_ge(stk.sem, i * 4 + stk.base + j + 3)
                    sv = [s1[:, j % 2, t * KEYS:(t + 1) * KEYS] for t in range(TT)]
                    lv = [s2[:, t * KEYS:(t + 1) * KEYS] for t in range(TT)]
                    top16(sv, lv, [V[:, t, side, :] for t in range(TT)],
                          [I[:, t, side, :] for t in range(TT)]).then_inc(tf.sem, 1)
                    dve.wait_ge(tf.sem, i * 4 + tf.base + j + 3)
                    if side == 0:
                        continue
                    h = i * 2 + j // 2
                    ix = b["side_index"][:, :, :, bass.ds(h * SEL, SEL)]
                    v.tensor_copy(ix, I[:, :, :, :])
                    for t in range(TT):
                        ins = v.tensor_tensor(cs[:, t, :].rearrange("p (a c) -> p a c", a=SEL),
                                              V[:, t, 0, :].unsqueeze(2).to_broadcast([P, SEL, SEL]),
                                              V[:, t, 1, :].unsqueeze(1).to_broadcast([P, SEL, SEL]), ALU.add)
                    link(ins)
                    link(top16([cs[:, t, :] for t in range(TT)], [cl[:, t, :] for t in range(TT)],
                               [tv[:, t, :] for t in range(TT)], [ti[:, t, :] for t in range(TT)]))
                    v.tensor_copy(b["top"][:, :, bass.ds(h * SEL, SEL)], tv[:, :, :])
                    link(v.tensor_copy(b["pos"][:, :, bass.ds(h * SEL, SEL)], ti[:, :, :]))
                link.leave(N // 4)
            link.done()
    qt.base += N
    sr.base += N + 2
    stk.base += N + 2
    tf.base += N + 2
    sl.base += 16
    p.unit += N


def peer_decode(p, b):
    nc = p.nc
    names = ("gate_shifted", "gate_exp", "dec_ready", "dec_turned", "dec_done")
    gs, ge, dr, dt, dd = (p.sig(n) for n in names)
    S = PEER_HEADS * SEL
    NS = TT * S
    with ExitStack() as ctx:
        pi = p.sb("pos_half", [P, 2, NS], U32, ctx=ctx)
        pf = p.sb("pos_float", [P, 2, NS], ctx=ctx)
        eq = p.sb("pos_equal", [P, S * SEL], ctx=ctx)
        key = p.sb("keys_found", [P, 3, NS], ctx=ctx)
        gsum = p.sb("gate_sum", [P, TT * PEER_HEADS], ctx=ctx)
        gx = p.sb("gate_terms", [P, NS], ctx=ctx)
        block = ctx.enter_context(nc.Block())

        @block.scalar
        def _(act):
            act.wait_ge(gs.sem, gs.at(1))
            nc.scalar.activation(gx[:, :], gx[:, :], ACT.Exp).then_inc(ge.sem, 1)

        @block.tensor
        def _(pe):
            pe.wait_ge(dr.sem, dr.at(1))
            for k in range(3):
                for t in range(TT):
                    ins = nc.tensor.transpose(p.ps[:, 2 + k, t * P:(t + 1) * P],
                                              key[:, k, t * P:(t + 1) * P], p.ident[:, :])
            ins.then_inc(dt.sem, 1)

        @block.vector
        def _(dve):
            v = nc.vector
            link = Chain(dve, p.sig("dve_chain"))
            top = b["top"][:, :, :].rearrange("p t (h s) -> p (t h) s", s=SEL)
            g3 = gx[:, :].rearrange("p (g s) -> p g s", s=SEL)
            v.tensor_tensor(g3, top, top[:, :, 0:1].to_broadcast([P, TT * PEER_HEADS, SEL]),
                            ALU.subtract).then_inc(gs.sem, 1)
            pos = b["pos"][:, :, :].rearrange("p t s -> p (t s)")
            v.tensor_scalar(pi[:, 0, :], pos, 4, None, ALU.logical_shift_right)
            link(v.tensor_scalar(pi[:, 1, :], pos, 15, None, ALU.bitwise_and))
            link(v.tensor_copy(pf[:, :, :], pi[:, :, :]))
            for t in range(TT):
                for k in range(2):
                    e3 = eq[:, :].rearrange("p (s n) -> p s n", n=SEL)
                    want = pf[:, k, t * S:(t + 1) * S].unsqueeze(2).to_broadcast([P, S, SEL])
                    have = p.iota[:, 0:SEL].unsqueeze(1).to_broadcast([P, S, SEL])
                    link(v.tensor_tensor(e3, want, have, ALU.is_equal))
                    e4 = eq[:, :].rearrange("p (h s n) -> p h s n", h=PEER_HEADS, n=SEL)
                    tab = b["side_index"][:, t, k, :].rearrange("p (h n) -> p h n", n=SEL)
                    link(v.tensor_tensor(e4, e4, tab.unsqueeze(2).to_broadcast([P, PEER_HEADS, SEL, SEL]),
                                         ALU.mult))
                    link(v.tensor_reduce(key[:, k, t * S:(t + 1) * S], e3, AX_X, ALU.add))
            dve.wait_ge(ge.sem, ge.at(1))
            link(v.tensor_reduce(gsum[:, :], g3, AX_X, ALU.add))
            link(v.reciprocal(gsum[:, :], gsum[:, :]))
            v.tensor_tensor(key[:, 2, :].rearrange("p (g s) -> p g s", s=SEL), g3,
                            gsum[:, :].unsqueeze(2).to_broadcast([P, TT * PEER_HEADS, SEL]),
                            ALU.mult).then_inc(dr.sem, 1)
            dve.wait_ge(dt.sem, dt.at(1))
            link(v.tensor_copy(b["sel"][:, :, :], p.ps[:, 2:5, :]))
            link.done()
    for s in (gs, ge, dr, dt):
        s.base += 1


def peer_gates(p, b, gates):
    nc = p.nc
    names = ("hot_first", "hot_second", "gate_summed", "gate_copied", "gate_stored", "gate_keys")
    h1, h2, gm, gc, gd, gk = (p.sig(n) for n in names)
    R = 8
    H0 = 1
    with ExitStack() as ctx:
        o1 = p.sb("first_hot", [P, R, KEYS], ctx=ctx)
        o2 = p.sb("second_hot", [P, R, KEYS], ctx=ctx)
        held = p.sb("wait_holder", [P, TG // 4], ctx=ctx)
        kb = p.sb("second_keys", [P, 2, TG // 2], ctx=ctx)
        gb = p.sb("gate_group", [P, KEYS, TG], ctx=ctx)
        sel = b["sel"]
        block = ctx.enter_context(nc.Block())

        @block.vector
        def _(dve):
            TH = TG // 2
            flat = sel[:, :, :].rearrange("p k t -> p (k t)")
            nc.vector.tensor_copy(kb[:, 0, :], sel[:, 1, 0:TH]).then_inc(gk.sem, 1)
            with dve.Fori(0, NTG) as g:
                for t in range(TG):
                    if t == 0:
                        dve.wait_ge(h2.sem, g * TG + h2.base + H0)
                        nc.vector.tensor_copy(kb[:, 1, :], sel[:, 1, bass.ds(g * TG + TH, TH)]
                                              ).then_inc(gk.sem, 1)
                    if t == TH + R:
                        dve.wait_ge(h2.sem, g * TG + h2.base + TH + H0)
                        nc.vector.tensor_copy(kb[:, 0, :], flat[:, bass.ds(g * TG + T + TG, TH)]
                                              ).then_inc(gk.sem, 1)
                    dve.wait_ge(gm.sem, g * TG + gm.base + t + 1)
                    nc.vector.tensor_scalar(o1[:, t % R, :], p.iota[:, :], sel[:, 0, bass.ds(g * TG + t, 1)],
                                            sel[:, 2, bass.ds(g * TG + t, 1)], ALU.is_equal,
                                            ALU.mult).then_inc(h1.sem, 1)

        @block.gpsimd
        def _(pool):
            pool.sem_inc(h2.sem, H0)
            with pool.Fori(0, NTG) as g:
                for t in range(0, TG, 4):
                    half, at = divmod(t, TG // 2)
                    if at == 0:
                        pool.wait_ge(gk.sem, g * 2 + gk.base + half + 1)
                    pool.wait_ge(gm.sem, g * TG + gm.base + t + 4)
                    nc.gpsimd.tensor_tensor(held[:, t // 4:t // 4 + 1], p.ones[:, 0:1], p.ones[:, 0:1], ALU.mult)
                    for k in range(4):
                        ins = nc.gpsimd.tensor_scalar(o2[:, (t + k) % R, :], p.iota[:, :],
                                                      kb[:, half, at + k:at + k + 1], None, ALU.is_equal)
                    ins.then_inc(h2.sem, 4)

        @block.tensor
        def _(pe):
            pe.sem_inc(gm.sem, R)
            with pe.Fori(0, NTG) as g:
                for t in range(TG):
                    q, r = divmod(t, 4)
                    pe.wait_ge(h1.sem, g * TG + h1.base + t + 1)
                    pe.wait_ge(h2.sem, g * TG + h2.base + H0 + t + 1)
                    if r == 0:
                        pe.wait_ge(gc.sem, g * 8 + gc.base + q + 1)
                    nc.tensor.matmul(p.ps[:, 2 + q % 2, r * KEYS:(r + 1) * KEYS], o2[:, t % R, :],
                                     o1[:, t % R, :], start=True, stop=True).then_inc(gm.sem, 1)

        @block.scalar
        def _(act):
            act.sem_inc(gc.sem, 2)
            with act.Fori(0, NTG) as g:
                act.wait_ge(gd.sem, g * 16 + gd.base + 16)
                for q in range(TG // 4):
                    act.wait_ge(gm.sem, g * TG + gm.base + R + 4 * q + 4)
                    nc.scalar.activation(gb[:, :, 4 * q:4 * q + 4].rearrange("p a t -> p t a"),
                                         p.ps[:, 2 + q % 2, :].rearrange("p (t a) -> p t a", t=4),
                                         ACT.Copy).then_inc(gc.sem, 1)

        @block.sync
        def _(sp):
            sp.sem_inc(gd.sem, 16)
            with sp.Fori(0, NTG) as g:
                sp.wait_ge(gc.sem, g * 8 + gc.base + 10)
                sp.dma_start(gates[g, :, :], gb[:, :, :].rearrange("p a t -> p (a t)")).then_inc(gd.sem, 16)
            sp.wait_ge(gd.sem, gd.at(16 * (NTG + 1)))
    h1.base += T
    h2.base += T + H0
    gk.base += 2 * NTG + 1
    gm.base += T + R
    gc.base += T // 4 + 2
    gd.base += 16 * (NTG + 1)


def peer_experts(p, b, us, vs, gates, nxt):
    nc = p.nc
    names = ("gelu_ready", "act_ready", "act_hi", "act_lo", "gates_loaded0", "gates_loaded1")
    ge, ar, ah, al, gl0, gl1 = (p.sig(n) for n in names)
    gl = (gl0, gl1)
    used, taken = p.sig("w_used"), p.sig("out_taken")
    u0, o0 = p.unit, p.out
    B = BLOCK
    N = 2 * B
    with ExitStack() as ctx:
        ga = p.sb("gelu", [P, 2, T], ctx=ctx)
        gt = p.sb("gate_block", [P, 2, NTG, B * TG], ctx=ctx)
        block = ctx.enter_context(nc.Block())

        @block.sync
        def _(sp):
            for j in range(RAW, B):
                p.load(sp, u0 + j, (u0 + j) % RAW, us[j, :, :])
            for j in range(B):
                p.load(sp, u0 + B + j, (u0 + j) % RAW, vs[j, :, :])
            with sp.Fori(1, NBLOCK) as i:
                for k, w in enumerate((us, vs)):
                    for j in range(B):
                        p.load(sp, i * N + u0 + k * B + j, (u0 + j) % RAW, w[i * B + j, :, :])
            p.unit += N * NBLOCK
            prefetch(p, sp, nxt)
            p.unit -= N * NBLOCK

        @block.gpsimd
        def _(pool):
            with pool.Fori(0, NBLOCK // 2) as i:
                for k in range(2):
                    blk = i * 2 + k
                    pool.wait_ge(ar.sem, blk * B + ar.base + B)
                    pool.dma_start(gt[:, k, :, :],
                                   gates.rearrange("g p m -> p g m")[:, :, bass.ds(blk * (B * TG), B * TG)]
                                   ).then_inc(gl[k].sem, 16)

        @block.tensor
        def _(pe):
            with pe.Fori(0, NBLOCK) as i:
                for j in range(B):
                    if j < 2:
                        pe.wait_ge(taken.sem, i * B + o0 + j - 1)
                    else:
                        pe.wait_ge(ge.sem, i * B + ge.base + j - 1)
                    p.product(pe, i * N + u0 + j, (u0 + j) % RAW, p.ps[:, j % 2, :], p.hh,
                              p.hl).then_inc(used.sem, 1)
                for j in range(B):
                    if j < 2:
                        pe.wait_ge(ge.sem, i * B + ge.base + B + j - 1)
                    else:
                        pe.wait_ge(taken.sem, i * B + o0 + j - 1)

                    def tile(k):
                        if j == 0:
                            pe.wait_ge(al.sem, i * B + al.base + k + 3)
                    p.product(pe, i * N + u0 + B + j, (u0 + j) % RAW, p.ps[:, j % 2, :], p.yh, p.yl,
                              wait_tile=tile).then_inc(used.sem, 1)

        @block.scalar
        def _(act):
            with act.Fori(0, NBLOCK) as i:
                for j in range(N):
                    p.split_hi(act, i * N + u0 + j + 1, (u0 + j + 1) % RAW,
                               i * (N // RAW) + (u0 + j + 1) // RAW + 1)
                    if 1 <= j <= B:
                        act.wait_ge(ar.sem, i * B + ar.base + 2 * B + j)
                        nc.scalar.activation(p.yh[:, j - 1, :], ga[:, (j - 1) % 2, :],
                                             ACT.Copy).then_inc(ah.sem, 1)
                    if j < B:
                        act.wait_ge(used.sem, i * N + u0 + j + 1)
                        act.wait_ge(al.sem, i * B + al.base + j + 1)
                        nc.scalar.activation(ga[:, j % 2, :], p.ps[:, j % 2, :], ACT.Gelu).then_inc(ge.sem, 1)

        @block.vector
        def _(dve):
            dve.sem_inc(al.sem, 2)
            dve.sem_inc(ar.sem, 2 * B)
            with dve.Fori(0, NBLOCK // 2) as ii:
                for k in range(2):
                    i = ii * 2 + k
                    for j in range(N):
                        p.split_lo(dve, i * N + u0 + j + 1, (u0 + j + 1) % RAW)
                        if 1 <= j <= B:
                            dve.wait_ge(ah.sem, i * B + ah.base + j)
                            nc.vector.tensor_tensor(p.yl[:, j - 1, :], ga[:, (j - 1) % 2, :],
                                                    p.yh[:, j - 1, :].bitcast(F32),
                                                    ALU.subtract).then_inc(al.sem, 1)
                        if j < B:
                            if j == 0:
                                dve.wait_ge(gl[k].sem, ii * 16 + gl[k].base + 16)
                            dve.wait_ge(ge.sem, i * B + ge.base + j + 1)
                            g = gt[:, k, :, j * TG:(j + 1) * TG]
                            a3 = ga[:, j % 2, :].rearrange("p (g t) -> p g t", g=NTG)
                            nc.vector.tensor_tensor(a3, a3, g, ALU.mult).then_inc(ar.sem, 1)
                        else:
                            dve.wait_ge(used.sem, i * N + u0 + j + 1)
                            n = j - B
                            nc.vector.tensor_tensor(p.x[:, n, :], p.ps[:, n % 2, :], p.x[:, n, :],
                                                    ALU.add).then_inc(taken.sem, 1)
    ge.base += KEYS
    ar.base += KEYS + 2 * B
    ah.base += KEYS
    al.base += KEYS + 2
    gl0.base += 16 * NBLOCK // 2
    gl1.base += 16 * NBLOCK // 2
    p.unit += N * NBLOCK
    p.out += KEYS


def ple_embed(p, pw, w, emb, nxt):
    nc = p.nc
    ld, hi, lo, used = p.sig("emb_loaded"), p.sig("emb_hi"), p.sig("emb_lo"), p.sig("w_used")
    pt = p.sig("emb_taken")
    u0 = p.unit
    with ExitStack() as ctx:
        e = p.sb("embedding", [P, 2, T], ctx=ctx)
        block = ctx.enter_context(nc.Block())

        @block.sync
        def _(sp):
            sp.dma_start(e[:, :, :], emb).then_inc(ld.sem, 16)
            p.unit += 4
            prefetch(p, sp, nxt[:2])
            p.unit -= 4
            sp.wait_ge(ld.sem, ld.at(16))

        @block.scalar
        def _(act):
            act.wait_ge(ld.sem, ld.at(16))
            nc.scalar.activation(p.yh[:, 0:2, :], e[:, :, :], ACT.Copy).then_inc(hi.sem, 1)
            for j in range(1, 3):
                p.split_hi(act, u0 + j, (u0 + j) % RAW, (u0 + j) // RAW + 1)

        @block.vector
        def _(dve):
            v = nc.vector
            dve.wait_ge(hi.sem, hi.at(1))
            v.tensor_tensor(p.yl[:, 0:2, :], e[:, :, :], p.yh[:, 0:2, :].bitcast(F32),
                            ALU.subtract).then_inc(lo.sem, 1)
            for j in range(2):
                p.split_lo(dve, u0 + j + 1, (u0 + j + 1) % RAW)
                dve.wait_ge(used.sem, u0 + j + 1)
                v.tensor_copy(pw[:, 4 * j:4 * j + 4, :], p.ps[:, 4 * j:4 * j + 4, :]).then_inc(pt.sem, 1)

        @block.tensor
        def _(pe):
            pe.wait_ge(lo.sem, lo.at(1))
            for j in range(2):
                u = u0 + j
                pe.wait_ge(p.sig("w_lo_ready").sem, u + 1)
                for q in range(4):
                    for k in range(2):
                        w_ = slice((q * 2 + k) * P, (q * 2 + k + 1) * P)
                        for m, (a, y) in enumerate(((p.wh, p.yh), (p.wh, p.yl), (p.wl, p.yh))):
                            ins = nc.tensor.matmul(p.ps[:, 4 * j + q, :], a[:, u % SPL, w_], y[:, k, :],
                                                   start=k == 0 and m == 0, stop=k == 1 and m == 2)
                ins.then_inc(used.sem, 1)
    ld.base += 16
    hi.base += 1
    lo.base += 1
    pt.base += 2
    p.unit += 2


def ple_add(p, sg, pw):
    nc = p.nc
    sd, md = p.sig("sigmoid_done"), p.sig("ple_mul")
    with nc.Block() as block:
        @block.scalar
        def _(act):
            for k in range(DK):
                nc.scalar.activation(sg[:, k, :], sg[:, k, :], ACT.Sigmoid).then_inc(sd.sem, 1)

        @block.vector
        def _(dve):
            v = nc.vector
            for k in range(DK + 1):
                if k < DK:
                    dve.wait_ge(sd.sem, sd.at(k + 1))
                    v.tensor_tensor(pw[:, k, :], sg[:, k, :], pw[:, k, :], ALU.mult).then_inc(md.sem, 1)
                if k:
                    dve.wait_ge(md.sem, md.at(k))
                    v.tensor_tensor(p.x[:, k - 1, :], p.x[:, k - 1, :], pw[:, k - 1, :], ALU.add)
    sd.base += DK
    md.base += DK


def odd_gates(p, b, nxt):
    nc = p.nc
    small, rows, used = p.sig("act_small"), p.sig("rows_ready"), p.sig("w_used")
    tn = p.sig("gates_turned")
    H = HEADS
    u = p.unit
    with ExitStack() as ctx:
        names = ("xb", "ab", "e1", "ln", "rc", "F", "ig", "G", "one", "em")
        r = {n: p.sb(f"gate_{n}", [H, T], ctx=ctx) for n in names}
        block = ctx.enter_context(nc.Block())

        @block.sync
        def _(sp):
            p.unit += 4
            prefetch(p, sp, nxt[3:4])
            p.unit -= 4

        @block.scalar
        def _(act):
            p.split_hi(act, u + 1, (u + 1) % RAW, (u + 1) // RAW + 1)
            log1p_act(act, nc, rows, small, r["e1"], r["ab"], r["ln"])
            act.wait_ge(rows.sem, rows.at(3))
            nc.scalar.activation(r["em"][:, :], r["em"][:, :], ACT.Exp, scale=-1.0).then_inc(small.sem, 1)

        @block.tensor
        def _(pe):
            p.product(pe, u, u % RAW, p.ps[:, 7, :], p.hh, p.hl).then_inc(used.sem, 1)
            pe.wait_ge(small.sem, small.at(3))
            for k, n in enumerate(("ig", "em")):
                for j in range(TT):
                    ins = nc.tensor.transpose(p.ps[:, 6, (k * TT + j) * H:(k * TT + j + 1) * H],
                                              r[n][:, j * P:(j + 1) * P], p.ident[0:H, 0:H])
            ins.then_inc(tn.sem, 1)

        @block.vector
        def _(dve):
            v = nc.vector
            link = Chain(dve, p.sig("dve_chain"))
            v.memset(r["one"][:, :], 1.0)
            p.split_lo(dve, u + 1, (u + 1) % RAW)
            dve.wait_ge(used.sem, u + 1)
            link(v.tensor_copy(r["G"][:, :], p.ps[32:32 + H, 7, :]))
            log1p_rows(v, link, rows, small, r["G"][:, :], p.col("f_bias", 0, H), r["xb"], r["ab"],
                       r["e1"], r["ln"], r["rc"])
            link(v.tensor_scalar(r["xb"][:, :], r["xb"][:, :], 0.0, None, ALU.min))
            link(v.tensor_tensor(r["xb"][:, :], r["xb"][:, :], r["ln"][:, :], ALU.subtract))
            link(v.tensor_tensor_scan(r["F"][:, :], r["one"][:, :], r["xb"][:, :], 0.0, ALU.mult, ALU.add))
            link(v.tensor_scalar(r["ig"][:, :], p.ps[0:H, 7, :], p.col("i_bias", 0, H), None, ALU.add))
            link(v.tensor_tensor(r["ig"][:, :], r["ig"][:, :], r["F"][:, :], ALU.subtract))
            link(v.tensor_tensor_scan(r["G"][:, :], r["one"][:, :], r["ig"][:, :], 0.0, ALU.mult, ALU.max))
            link(v.tensor_scalar(b["negG"][:, :], r["G"][:, :], -1.0, None, ALU.mult))
            v.tensor_tensor(r["em"][:, :], r["F"][:, :], r["G"][:, :], ALU.add).then_inc(rows.sem, 1)
            dve.wait_ge(tn.sem, tn.at(1))
            link(v.tensor_copy(b["cols"][:, :, :, :].rearrange("p k j h -> p (k j h)"),
                               p.ps[:, 6, 0:2 * TT * H]))
            link(v.memset(b["hn"][:, :, :], 0.0))
            link(v.memset(b["os"][:, :], 0.0))
            link(v.memset(b["qk"][:, :, 0:CONV - 1], 0.0))
            link(v.memset(b["vs"][:, :, :], 1.0))
            link.done()
    small.base += 3
    rows.base += 3
    tn.base += 1
    p.unit += 1


def odd_heads(p, b, half, w, nxt):
    nc = p.nc
    names = ("od_conv", "od_silu", "od_y", "od_yhi", "od_sel", "od_bc", "od_s", "od_arg", "od_exp", "od_sw",
             "od_vt", "od_vs", "od_num", "od_sig", "od_ssq", "od_ms", "od_root", "od_hn", "od_turn")
    (cv, si, yy, yh, se, bc, sc, ag, ex, sw, vt, vs, nu, sg, sq, ms, ro, hn, tu) = (p.sig(n) for n in names)
    used, taken = p.sig("w_used"), p.sig("out_taken")
    u0, o0 = p.unit, p.out
    NH = HEADS // 2
    SC = P ** -0.5
    W = b["w"]
    blocks = [(4, 0), (5, 0), (6, 0), (6, 256)]

    def width(i):
        return T - i * P

    def turn(pe, n):
        pe.wait_ge(hn.sem, n)
        for j in range(TT):
            ins = nc.tensor.transpose(p.ps[:, 7, j * P:(j + 1) * P], b["hn"][:, j, :], p.ident[:, :])
        ins.then_inc(tu.sem, 1)

    def gate(dve, n, h):
        dve.wait_ge(tu.sem, n + tu.base + 1)
        dve.wait_ge(sg.sem, n + sg.base + 1)
        return nc.vector.scalar_tensor_tensor(out=b["yf"][:, :], in0=p.ps[:, 7, :],
                                              scalar=p.par[:, bass.ds(h + COLS["head_norm"], 1)],
                                              in1=b["os"][:, :], op0=ALU.mult, op1=ALU.mult)

    def split(dve, n, slot):
        dve.wait_ge(yh.sem, n + yh.base + 1)
        return nc.vector.tensor_tensor(p.yl[:, slot, :], b["yf"][:, :], p.yh[:, slot, :].bitcast(F32),
                                       ALU.subtract)

    with nc.Block() as block:
        @block.sync
        def _(sp):
            with sp.Fori(1, NH) as i:
                for j in range(4):
                    p.load(sp, i * 4 + u0 + j, (u0 + j) % RAW, w[i * 4 + j, :, :])
            p.unit += 4 * NH
            prefetch(p, sp, nxt)
            p.unit -= 4 * NH

        @block.tensor
        def _(pe):
            t = nc.tensor

            def lin(i, j):
                if j == 1:
                    pe.wait_ge(sg.sem, i + sg.base + 1)
                else:
                    pe.wait_ge(taken.sem, i * 3 + o0 + (0, None, 1, 2)[j])
                p.product(pe, i * 4 + u0 + j, (u0 + j) % RAW, p.ps[:, j % 2, :], p.hh, p.hl
                          ).then_inc(used.sem, 1)
            with pe.Fori(0, NH) as i:
                lin(i, 0)
                turn(pe, i + hn.base + 1)
                lin(i, 1)
                lin(i, 2)
                pe.wait_ge(se.sem, i + se.base + 1)
                t.matmul(p.ps[:, 2, :], p.ones[0:HEADS, :], b["rsel"][:, :], start=True, stop=True
                         ).then_inc(bc.sem, 1)
                pe.wait_ge(si.sem, i * 2 + si.base + 2)
                for s in range(TT):
                    bank, c = blocks[s]
                    ins = t.matmul(p.ps[:, bank, c:c + width(s)], b["kT"][:, s * P:(s + 1) * P],
                                   b["qT"][:, s * P:], start=True, stop=True, skip_group_check=True)
                ins.then_inc(sc.sem, 1)
                lin(i, 3)
                pe.wait_ge(taken.sem, i * 3 + o0 + 3)
                for j in range(TT):
                    ins = t.transpose(p.ps[:, 3, j * P:(j + 1) * P], b["vT"][:, j * P:(j + 1) * P], p.ident[:, :])
                ins.then_inc(vt.sem, 1)
                pe.wait_ge(vs.sem, i + vs.base + 1)
                pe.wait_ge(sw.sem, i + sw.base + 1)
                for j in range(TT):
                    for s in range(j + 1):
                        ins = t.matmul(p.ps[:, 2 + j // 2, (j % 2) * 130:(j % 2) * 130 + 130],
                                       W[:, s, j * P:(j + 1) * P], b["vs"][:, s, :], start=s == 0, stop=s == j)
                ins.then_inc(nu.sem, 1)
            turn(pe, NH + hn.base + 1)

        @block.scalar
        def _(act):
            a = nc.scalar
            if half == 0:
                act.sem_inc(sg.sem, 1)
            with act.Fori(0, NH) as i:
                for j in range(4):
                    p.split_hi(act, i * 4 + u0 + j + 1, (u0 + j + 1) % RAW, i + (u0 + j + 1) // RAW + 1)
                    if j == 0:
                        act.wait_ge(yy.sem, i + yy.base + 1)
                        a.activation(p.yh[:, i, :], b["yf"][:, :], ACT.Copy).then_inc(yh.sem, 1)
                    if j < 2:
                        act.wait_ge(cv.sem, i * 2 + cv.base + j + 1)
                        a.activation(b["kT" if j == 0 else "qT"][:, :], b["tmp"][:, 1, :], ACT.Silu
                                     ).then_inc(si.sem, 1)
                for s in range(TT):
                    act.wait_ge(ag.sem, i * 4 + ag.base + s + 1)
                    a.activation(W[:, s, s * P:], W[:, s, s * P:], ACT.Exp).then_inc(ex.sem, 1)
                act.wait_ge(used.sem, i * 4 + u0 + 4)
                a.activation(b["os"][:, :], p.ps[:, 1, :], ACT.Sigmoid).then_inc(sg.sem, 1)
                act.wait_ge(nu.sem, i + nu.base + 1)
                for j in range(TT):
                    ins = a.activation(b["sqj"][:, :], p.ps[:, 2 + j // 2, (j % 2) * 130:(j % 2) * 130 + P],
                                       ACT.Square, accum_out=b["small"][:, 0, j:j + 1])
                    ins.then_inc(sq.sem, 1)
                    act.wait_ge(sq.sem, i * 4 + sq.base + j + 1)
                act.wait_ge(ms.sem, i + ms.base + 1)
                a.activation(b["small"][:, 3, :], b["small"][:, 3, :], ACT.Sqrt).then_inc(ro.sem, 1)
            act.wait_ge(yy.sem, NH + yy.base + 1)
            a.activation(p.yh[:, 0, :], b["yf"][:, :], ACT.Copy).then_inc(yh.sem, 1)

        @block.vector
        def _(dve):
            v = nc.vector
            link = Chain(dve, p.sig("dve_chain"))
            sm = b["small"]
            dve.sem_inc(hn.sem, 1)

            def lo(i, j):
                p.split_lo(dve, i * 4 + u0 + j + 1, (u0 + j + 1) % RAW)

            def conv(i, j):
                dve.wait_ge(used.sem, i * 4 + u0 + j + 1)
                v.tensor_copy(b["qk"][:, j, CONV - 1:], p.ps[:, j % 2, :]).then_inc(taken.sem, 1)
                dve.wait_ge(taken.sem, i * 3 + o0 + j + 1)
                if j:
                    dve.wait_ge(si.sem, i * 2 + si.base + j)
                tile = i + (HEADS if j == 0 else 0) + half * NH
                conv_steps(nc, link, b["qk"][:, j, :], (b["tmp"][:, 0, :], b["tmp"][:, 1, :]),
                           [p.par[:, bass.ds(tile * CONV + COLS["od_conv_w"] + k, 1)] for k in range(CONV)],
                           p.par[:, bass.ds(tile + COLS["od_conv_b"], 1)]).then_inc(cv.sem, 1)

            with dve.Fori(0, NH) as i:
                link.enter(i, 2 * 3 + 13)
                h = i + half * NH
                lo(i, 0)
                gate(dve, i, h - 1).then_inc(yy.sem, 1)
                conv(i, 0)
                lo(i, 1)
                link(split(dve, i, i))
                conv(i, 1)
                lo(i, 2)
                dve.wait_ge(used.sem, i * 4 + u0 + 3)
                v.tensor_copy(b["vT"][:, :], p.ps[:, 0, :]).then_inc(taken.sem, 1)
                v.tensor_scalar(b["rsel"][:, :], b["negG"][:, :], p.ident[0:HEADS, bass.ds(h, 1)], None,
                                ALU.mult).then_inc(se.sem, 1)
                lo(i, 3)
                dve.wait_ge(bc.sem, i + bc.base + 1)
                for s in range(TT):
                    v.tensor_scalar(W[:, s, s * P:], p.ps[:, 2, s * P:], b["cols"][:, 0, s, bass.ds(h, 1)], 0.0,
                                    ALU.add, ALU.min).then_inc(ag.sem, 1)
                dve.wait_ge(sc.sem, i + sc.base + 1)
                for s in range(TT):
                    dve.wait_ge(ex.sem, i * 4 + ex.base + s + 1)
                    bank, c = blocks[s]
                    ins = v.scalar_tensor_tensor(out=W[:, s, s * P:], in0=p.ps[:, bank, c:c + width(s)],
                                                 scalar=SC, in1=W[:, s, s * P:], op0=ALU.mult, op1=ALU.mult)
                    link(ins)
                for s in range(TT):
                    ins = v.tensor_tensor(W[:, s, s * P:(s + 1) * P], W[:, s, s * P:(s + 1) * P],
                                          p.incl[:, 0:P], ALU.mult)
                ins.then_inc(sw.sem, 1)
                dve.wait_ge(vt.sem, i + vt.base + 1)
                v.tensor_copy(b["vs"][:, :, 0:P], p.ps[:, 3, :].rearrange("p (j e) -> p j e", j=TT)
                              ).then_inc(vs.sem, 1)
                dve.wait_ge(sq.sem, i * 4 + sq.base + 4)
                den = p.ps[:, 2:4, 0:260].rearrange("p b (j e) -> p b j e", e=130)[:, :, :, P]
                s4 = [sm[:, k, :] for k in range(5)]
                link(v.tensor_copy(s4[1].rearrange("p (b j) -> p b j", b=2), den))
                link(v.scalar_tensor_tensor(out=s4[2], in0=s4[1], scalar=-1.0, in1=s4[1], op0=ALU.mult,
                                            op1=ALU.max))
                link(v.tensor_tensor(s4[2], s4[2], b["cols"][:, 1, :, bass.ds(h, 1)].rearrange("p j o -> p (j o)"),
                                     ALU.max))
                link(v.reciprocal(s4[1], s4[2]))
                link(v.scalar_tensor_tensor(out=s4[2], in0=s4[0], scalar=1.0 / P, in1=s4[1], op0=ALU.mult,
                                            op1=ALU.mult))
                link(v.tensor_tensor(s4[2], s4[2], s4[1], ALU.mult))
                v.tensor_scalar(s4[3], s4[2], EPS, None, ALU.add).then_inc(ms.sem, 1)
                dve.wait_ge(ro.sem, i + ro.base + 1)
                link(v.reciprocal(s4[4], s4[3]))
                link(v.tensor_tensor(s4[4], s4[4], s4[1], ALU.mult))
                num = p.ps[:, 2:4, 0:260].rearrange("p b (j e) -> p b j e", e=130)[:, :, :, 0:P]
                v.tensor_tensor(b["hn"][:, :, :].rearrange("p (b j) e -> p b j e", b=2), num,
                                s4[4].rearrange("p (b j) -> p b j", b=2).unsqueeze(3).to_broadcast([P, 2, 2, P]),
                                ALU.mult).then_inc(hn.sem, 1)
                link.leave(NH)
            gate(dve, NH, half * NH + NH - 1).then_inc(yy.sem, 1)
            link(split(dve, NH, 0))
            link.done()
    for s, n in ((cv, 2), (si, 2), (se, 1), (bc, 1), (sc, 1), (ag, 4), (ex, 4), (sw, 1), (vt, 1),
                 (vs, 1), (nu, 1), (sg, 1), (sq, 4), (ms, 1), (ro, 1)):
        s.base += n * NH
    for s in (yy, yh, hn, tu):
        s.base += NH + 1
    p.unit += 4 * NH
    p.out += 3 * NH


def store(p, src):
    nc = p.nc
    done = p.sig("stored")
    with nc.Block() as block:
        @block.sync
        def _(sp):
            sp.dma_start(p.dram["out"], src[:, :, :]).then_inc(done.sem, 16)
            sp.wait_ge(done.sem, done.at(16))
    done.base += 16


def add_to(p):
    return lambda i, ps: p.nc.vector.tensor_tensor(p.x[:, i, :], ps, p.x[:, i, :], ALU.add)


def firsts(src, n=RAW):
    return [src[j, :, :] for j in range(n)]


def ffn(p, layer, nxt):
    d = p.dram
    wq, us, vs, gate, pw_ = (d[f"{n}{layer}"] for n in ("wq", "u", "v", "gate", "plew"))
    norm(p, p.x, f"norm_ffn{layer}", out=(p.hh, p.hl))
    with ExitStack() as outer:
        b = {"sel": p.sb("selected", [P, 3, T], ctx=outer)}
        with ExitStack() as ctx:
            b["side_index"] = p.sb("key_index", [P, TT, 2, P], ctx=ctx)
            b["top"] = p.sb("top_sums", [P, TT, P], ctx=ctx)
            b["pos"] = p.sb("top_pos", [P, TT, P], U32, ctx=ctx)
            b["next"] = firsts(us)
            peer_topk(p, b, wq, d[f"sub{layer}"])
            peer_decode(p, b)
        peer_gates(p, b, d["gates"])
    peer_experts(p, b, us, vs, d["gates"], [pw_[0, :, :], pw_[1, :, :], gate[0, :, :], gate[1, :, :]])
    norm(p, p.x, f"norm_ple{layer}", out=(p.hh, p.hl))
    with ExitStack() as ctx:
        pw = p.sb("embedded", [P, DK, T], ctx=ctx)
        sg = p.sb("ple_gate", [P, DK, T], ctx=ctx)
        ple_embed(p, pw, pw_, d["emb"][layer], [gate[2, :, :], gate[3, :, :]])
        linear(p, [(gate, DK, 1, [(p.hh, p.hl)],
                    lambda i, ps: p.nc.vector.tensor_copy(sg[:, i, :], ps))], nxt)
        ple_add(p, sg, pw)


def trunk(nc, dram):
    with ExitStack() as ctx:
        p = Program(nc, ctx, dram)
        start(p, firsts(dram["ev_in"]))
        norm(p, p.x, "norm_mix0", out=(p.hh, p.hl))
        with ExitStack() as c:
            b = {"z": p.sb("z", [P, DK, T], ctx=c), "xbc": p.sb("xbc", [P, XBC, CONV - 1 + T], ctx=c),
                 "q": p.sb("q", [P, 8, T], ctx=c)}
            with ExitStack() as c2:
                b["dtraw"] = p.sb("dt_raw", [HEADS, T], ctx=c2)
                with ExitStack() as c3:
                    b["kd"] = p.sb("k_twice", [P, 2, 640], ctx=c3)
                    b["vt"] = p.sb("v_rows", [P, 640], ctx=c3)
                    even_in(p, b, firsts(dram["ev_out"]))
                    even_attention(p, b)
                b["dt"] = p.sb("dt", [HEADS, T], ctx=c2)
                b["adt"] = p.sb("a_dt", [HEADS, T], ctx=c2)
                even_conv(p, b)
                even_ssd(p, b)
            norm(p, b["z"], "out_norm", out=(p.hh, p.hl))
        linear(p, [(dram["ev_out"], 16, 2, [(p.hh, p.hl), (p.yh, p.yl)], add_to(p))], firsts(dram["wq0"]))
        ffn(p, 0, firsts(dram["od_in"]))
        norm(p, p.x, "norm_mix1", out=(p.hh, p.hl))
        with ExitStack() as c:
            b = {"negG": p.sb("neg_g", [HEADS, T], ctx=c), "cols": p.sb("gate_cols", [P, 2, TT, HEADS], ctx=c),
                 "hn": p.sb("head_out", [P, TT, P], ctx=c), "os": p.sb("o_sigmoid", [P, T], ctx=c),
                 "qk": p.sb("qk_rows", [P, 2, CONV - 1 + T], ctx=c), "vs": p.sb("v_turned_od", [P, TT, 130], ctx=c)}
            odd_gates(p, b, firsts(dram["od_in"], 5)[1:])
            for n, shape in (("w", [P, TT, T]), ("kT", [P, T]), ("qT", [P, T]), ("vT", [P, T]),
                             ("tmp", [P, 2, T]), ("yf", [P, T]), ("rsel", [HEADS, T]), ("sqj", [P, P]),
                             ("small", [P, 5, TT])):
                b[n] = p.sb(f"od_{n}", shape, ctx=c)
            y = [(p.yh, p.yl)]
            w = dram["od_in"]
            odd_heads(p, b, 0, w[1:33], firsts(dram["od_out"]))
            linear(p, [(dram["od_out"], 8, 1, y, add_to(p))], firsts(w[33:65]))
            odd_heads(p, b, 1, w[33:65], firsts(dram["od_out"][8:16]))
            linear(p, [(dram["od_out"][8:16], 8, 1, y, add_to(p))], firsts(dram["wq1"]))
        ffn(p, 1, firsts(dram["ev_in"], 1))
        norm(p, p.x, "norm_final", dst=p.x)
        store(p, p.x)


def _units(w, tiles=DK):
    K, N = w.shape
    return np.ascontiguousarray(w.reshape(K // (tiles * P), tiles, P, N // P, P).transpose(3, 0, 2, 1, 4)
                                ).reshape(-1, P, tiles * P)


def _cols(v):
    return v.reshape(-1, P).T


def _rows16(v):
    out = np.zeros((P, 1), v.dtype)
    out[:HEADS, 0] = v
    return out


def _lay_out(i):
    w = i["ev_w_in"][0]
    at = np.cumsum([0, INNER, XBC * P, HEADS, 1024, P, P])
    z, xbc, dt, q, k, v = (w[:, a:c] for a, c in zip(at[:-1], at[1:]))
    dt = np.pad(dt, ((0, 0), (0, P - HEADS)))
    kk = [k[:, :64], k[:, :64], k[:, 64:], k[:, 64:]]
    m = {"ev_in": _units(np.concatenate([z, xbc, q, *kk, v, dt], 1)), "ev_out": _units(i["ev_w_out"][0])}
    w = i["od_w_in"][0]
    I = HEADS * P
    q, k, v, o = (w[:, a * I:(a + 1) * I].reshape(D, HEADS, P) for a in range(4))
    g = np.zeros((D, P), w.dtype)
    g[:, 0:HEADS] = w[:, 4 * I:4 * I + HEADS]
    g[:, 32:32 + HEADS] = w[:, 4 * I + HEADS:]
    m["od_in"] = _units(np.concatenate([g, np.stack([k, q, v, o], 2).reshape(D, 4 * I)], 1))
    w = i["od_w_out"][0]
    m["od_out"] = np.concatenate([_units(np.roll(x.reshape(8, P, D), 1, 0).reshape(1024, D))
                                  for x in (w[:1024], w[1024:])], 0)
    for n in range(2):
        m[f"wq{n}"] = _units(i["pk_w_q"][n].reshape(D, -1))
        s = np.stack([i["pk_sub_k1"][n], i["pk_sub_k2"][n]], 1)
        m[f"sub{n}"] = s.reshape(16, KEYS, P).transpose(2, 0, 1)
        m[f"u{n}"] = _units(i["pk_u"][n].T)
        m[f"v{n}"] = i["pk_v"][n].reshape(NBLOCK, BLOCK, KEYS, DK, P).transpose(0, 3, 2, 1, 4).reshape(-1, P, UNIT)
        m[f"gate{n}"] = _units(i["ple_gate"][n])
        m[f"plew{n}"] = i["ple_w"][n].reshape(2, P, 2, 4, P).transpose(2, 1, 3, 0, 4).reshape(2, P, UNIT)
        m[f"emb{n}"] = i["p"][n, 0].T.reshape(2, P, T).transpose(1, 0, 2)
    m["x"] = i["x"][0].T.reshape(DK, P, T).transpose(1, 0, 2)
    taps = lambda w: w.reshape(CONV, -1, P).transpose(2, 1, 0).reshape(P, -1)
    m["par"] = np.concatenate(
        [_cols(i[n][l]) for n in ("norm_mix", "norm_ffn", "norm_ple") for l in range(2)]
        + [_cols(i["norm_final"]), _cols(i["ev_out_norm"][0]), _cols(np.repeat(i["ev_d_skip"][0], 64)),
           taps(i["ev_conv_w"][0]), _cols(i["ev_conv_b"][0]), 
           np.repeat(i["ev_sinks"].reshape(2, 4, 2).transpose(0, 2, 1).reshape(1, -1), P, 0),
           taps(i["od_conv_w"][0]), _cols(i["od_conv_b"][0]), _cols(i["od_head_norm"][0]),
           _rows16(i["ev_dt_bias"][0]), _rows16(i["ev_a_log"][0]), _rows16(i["od_i_bias"][0]),
           _rows16(i["od_f_bias"][0])], 1)
    return {k: np.ascontiguousarray(a) for k, a in m.items()}


def build(nc, shapes):
    dram = {n: nc.dram_tensor(f"in_{n}", s, F32, kind="ExternalInput").ap() for n, s in shapes.items()}
    dram["emb"] = [dram["emb0"], dram["emb1"]]
    dram["out"] = nc.dram_tensor("out_0", [P, DK, T], F32, kind="ExternalOutput").ap()
    dram["gates"] = nc.dram_tensor("gates", [NTG, P, KEYS * TG], F32, kind="Internal").ap()
    trunk(nc, dram)


def kernel(**inputs):
    import concourse.bacc as bacc
    from concourse.bass_utils import run_bass_kernel_spmd

    arrays = _lay_out({k: np.asarray(v) for k, v in inputs.items()})
    nc = bacc.Bacc("TRN2", target_bir_lowering=False, num_devices=1)
    build(nc, {n: list(a.shape) for n, a in arrays.items()})
    r = run_bass_kernel_spmd(nc, [{f"in_{n}": a for n, a in arrays.items()}], core_ids=[0])
    return r.results[0]["out_0"].transpose(2, 1, 0).reshape(1, T, D)
```

```python
from contextlib import ExitStack

import concourse.bass as bass
import numpy as np
from concourse import mybir

F32 = mybir.dt.float32
F32R = mybir.dt.float32r
U32 = mybir.dt.uint32
ALU = mybir.AluOpType
ACT = mybir.ActivationFunctionType
AX_X = mybir.AxisListType.X

P = 128
T = 512
TT = T // P
D = 1024
DK = D // P
UNIT = DK * P
EPS = 1e-6
RAW = 4
SPL = 2
INNER = 1024
XBC = 12
CONV = 4
HEADS = 16
SEL = 16
PEER_HEADS = 8
KEYS = 128
BLOCK = 8
NBLOCK = KEYS // BLOCK
TG = 32
NTG = T // TG
NEG = -1e30

COLS = {}
_at = 0
for _name, _n in (("norm_mix0", 8), ("norm_mix1", 8), ("norm_ffn0", 8), ("norm_ffn1", 8),
                  ("norm_ple0", 8), ("norm_ple1", 8), ("norm_final", 8), ("out_norm", 8),
                  ("d_skip", 8), ("conv_w", 4 * XBC), ("conv_b", XBC), ("sinks", HEADS),
                  ("od_conv_w", 4 * 32), ("od_conv_b", 32), ("head_norm", HEADS),
                  ("dt_bias", 1), ("a_log", 1), ("i_bias", 1), ("f_bias", 1)):
    COLS[_name] = _at
    _at += _n
NPAR = _at


class Signal:

    def __init__(self, nc, ctx, name):
        self.sem = ctx.enter_context(nc.semaphore(name))
        self.base = 0

    def at(self, k):
        return self.base + k


class Chain:

    def __init__(self, eng, signal):
        self.eng, self.counter, self.n, self.off = eng, signal, 0, 0

    def __call__(self, ins):
        self.n += 1
        ins.then_inc(self.counter.sem, 1)
        self.eng.wait_ge(self.counter.sem, self.off + self.counter.base + self.n)

    def enter(self, i, per):
        self.off, self.start, self.per = i * per, self.n, per

    def leave(self, count):
        assert self.n - self.start == self.per, (self.n - self.start, self.per)
        self.n += self.per * (count - 1)
        self.off = 0

    def done(self):
        self.counter.base += self.n


class Program:
    def __init__(self, nc, ctx, dram):
        self.nc, self.ctx, self.dram = nc, ctx, dram
        self.unit = RAW
        self.out = 2
        self.sems = {}
        self.names = {}
        sb = self.sb
        self.x = sb("residual", [P, DK, T])
        self.hh = sb("h_hi", [P, DK, T], F32R)
        self.hl = sb("h_lo", [P, DK, T], F32R)
        self.yh = sb("y_hi", [P, DK, T], F32R)
        self.yl = sb("y_lo", [P, DK, T], F32R)
        self.raw = sb("w_raw", [P, RAW, UNIT])
        self.wh = sb("w_hi", [P, SPL, UNIT], F32R)
        self.wl = sb("w_lo", [P, SPL, UNIT], F32R)
        self.par = sb("params", [P, NPAR])
        self.ones = sb("ones", [P, P])
        self.ident = sb("ident", [P, P])
        self.incl = sb("incl", [P, T])
        self.after = sb("after", [P, P])
        self.iota = sb("iota", [P, P])
        self.ps = ctx.enter_context(nc.psum_tensor("ps", [P, 8, 512], F32))

    def sb(self, name, shape, dt=F32, ctx=None):
        n = self.names[name] = self.names.get(name, 0) + 1
        name = name if n == 1 else f"{name}_{n}"
        return (ctx or self.ctx).enter_context(self.nc.sbuf_tensor(name, shape, dt))

    def sig(self, name):
        if name not in self.sems:
            self.sems[name] = Signal(self.nc, self.ctx, name)
        return self.sems[name]

    def col(self, name, k=0, rows=P):
        c = COLS[name] + k
        return self.par[0:rows, c:c + 1]

    def load(self, sp, u, slot, src):
        hi, lo, loaded = self.sig("w_hi_ready"), self.sig("w_lo_ready"), self.sig(f"w_loaded{slot}")
        sp.wait_ge(hi.sem, u - RAW + 1)
        sp.wait_ge(lo.sem, u - RAW + 1)
        sp.dma_start(self.raw[:, slot, :], src).then_inc(loaded.sem, 16)

    def split_hi(self, act, u, slot, loads):
        act.wait_ge(self.sig(f"w_loaded{slot}").sem, 16 * loads)
        act.wait_ge(self.sig("w_used").sem, u - SPL + 1)
        self.nc.scalar.activation(self.wh[:, slot % SPL, :], self.raw[:, slot, :],
                                  ACT.Copy).then_inc(self.sig("w_hi_ready").sem, 1)

    def split_lo(self, dve, u, slot):
        dve.wait_ge(self.sig("w_hi_ready").sem, u + 1)
        self.nc.vector.tensor_tensor(self.wl[:, slot % SPL, :], self.raw[:, slot, :],
                                     self.wh[:, slot % SPL, :].bitcast(F32),
                                     ALU.subtract).then_inc(self.sig("w_lo_ready").sem, 1)

    def product(self, pe, u, slot, out, rh, rl, first=True, last=True, tiles=range(DK), wait_tile=None):
        pe.wait_ge(self.sig("w_lo_ready").sem, u + 1)
        s = slot % SPL
        n = len(tiles)
        for j, k in enumerate(tiles):
            if wait_tile is not None:
                wait_tile(k)
            w = slice(j * P, (j + 1) * P)
            for m, (a, b) in enumerate(((self.wh, rh), (self.wh, rl), (self.wl, rh))):
                ins = self.nc.tensor.matmul(out, a[:, s, w], b[:, k, :], start=first and j == 0 and m == 0,
                                            stop=last and j == n - 1 and m == 2)
        return ins


def prefetch(p, sp, srcs):
    for j, s in enumerate(srcs):
        u = p.unit + j
        p.load(sp, u, u % RAW, s)


def start(p, nxt):
    nc = p.nc
    ld, const = p.sig("inputs_loaded"), p.sig("const_ready")
    with nc.Block() as block:
        @block.sync
        def _(sp):
            for j in range(RAW):
                sp.sem_inc(p.sig(f"w_loaded{j}").sem, 16)
            sp.dma_start(p.x[:, :, :], p.dram["x"]).then_inc(ld.sem, 16)
            sp.dma_start(p.par[:, :], p.dram["par"]).then_inc(ld.sem, 16)
            prefetch(p, sp, nxt)
            sp.wait_ge(ld.sem, 32)

        @block.scalar
        def _(act):
            act.sem_inc(p.sig("w_hi_ready").sem, RAW)
            p.split_hi(act, RAW, 0, 2)

        @block.tensor
        def _(pe):
            pe.sem_inc(p.sig("w_used").sem, RAW)

        @block.vector
        def _(dve):
            dve.sem_inc(p.sig("w_lo_ready").sem, RAW)
            dve.sem_inc(p.sig("out_taken").sem, 2)
            p.split_lo(dve, RAW, 0)

        @block.gpsimd
        def _(pool):
            nc.gpsimd.memset(p.ones[:, :], 1.0)
            nc.gpsimd.memset(p.incl[:, :], 1.0)
            nc.gpsimd.memset(p.after[:, :], 1.0)
            nc.gpsimd.iota(p.iota[:, :], pattern=[[1, P]], base=0, channel_multiplier=0,
                           allow_small_or_imprecise_dtypes=True)
            nc.gpsimd.memset(p.ident[:, :], 0.0).then_inc(const.sem, 1)
            pool.wait_ge(const.sem, 1)
            nc.gpsimd.affine_select(out=p.ident[:, :], in_=p.ident[:, :], compare_op=ALU.not_equal,
                                    fill=1.0, base=0, pattern=[[-1, P]], channel_multiplier=1)
            nc.gpsimd.affine_select(out=p.incl[:, :], in_=p.incl[:, :], compare_op=ALU.is_ge,
                                    fill=0.0, base=0, pattern=[[1, T]], channel_multiplier=-1)
            nc.gpsimd.affine_select(out=p.after[:, :], in_=p.after[:, :], compare_op=ALU.is_ge,
                                    fill=0.0, base=-1, pattern=[[-1, P]], channel_multiplier=1)
    const.base += 1
    ld.base += 32


def norm(p, src, gain, out=None, dst=None, nxt=()):
    nc = p.nc
    sq, ssum, root, scaled, hi_done = (p.sig(n) for n in ("squared", "sumsq", "root", "scaled", "norm_hi"))
    chain = p.sig("dve_chain")
    with ExitStack() as ctx:
        s2 = p.sb("squares", [P, 2, T], ctx=ctx)
        rstd = p.sb("rstd", [P, T], ctx=ctx)
        hf = p.sb("normed", [P, 2, T], ctx=ctx)
        block = ctx.enter_context(nc.Block())

        @block.sync
        def _(sp):
            prefetch(p, sp, nxt)

        @block.scalar
        def _(act):
            for k in range(DK):
                if k >= 2:
                    act.wait_ge(ssum.sem, ssum.at(k - 1))
                nc.scalar.activation(s2[:, k % 2, :], src[:, k, :], ACT.Square).then_inc(sq.sem, 1)
            act.wait_ge(ssum.sem, ssum.at(DK))
            nc.scalar.activation(rstd[:, :], p.ps[:, 7, :], ACT.Copy, scale=1.0 / (DK * P),
                                 bias=EPS).then_inc(root.sem, 1)
            act.wait_ge(root.sem, root.at(1))
            nc.scalar.activation(rstd[:, :], rstd[:, :], ACT.Sqrt).then_inc(root.sem, 1)
            if out is not None:
                for k in range(DK):
                    act.wait_ge(scaled.sem, scaled.at(k + 1))
                    nc.scalar.activation(out[0][:, k, :], hf[:, k % 2, :], ACT.Copy).then_inc(hi_done.sem, 1)

        @block.tensor
        def _(pe):
            for k in range(DK):
                pe.wait_ge(sq.sem, sq.at(k + 1))
                nc.tensor.matmul(p.ps[:, 7, :], p.ones[:, :], s2[:, k % 2, :], start=(k == 0),
                                 stop=(k == DK - 1)).then_inc(ssum.sem, 1)

        @block.vector
        def _(dve):
            link = Chain(dve, chain)
            dve.wait_ge(root.sem, root.at(2))
            link(nc.vector.reciprocal(rstd[:, :], rstd[:, :]))
            for k in range(DK + 1):
                if k < DK:
                    o = hf[:, k % 2, :] if out is not None else dst[:, k, :]
                    if out is not None and k >= 2:
                        dve.wait_ge(hi_done.sem, hi_done.at(k - 1))
                    nc.vector.scalar_tensor_tensor(out=o, in0=src[:, k, :], scalar=p.col(gain, k),
                                                   in1=rstd[:, :], op0=ALU.mult,
                                                   op1=ALU.mult).then_inc(scaled.sem, 1)
                if k and out is not None:
                    dve.wait_ge(hi_done.sem, hi_done.at(k))
                    link(nc.vector.tensor_tensor(out[1][:, k - 1, :], hf[:, (k - 1) % 2, :],
                                                 out[0][:, k - 1, :].bitcast(F32), ALU.subtract))
            link.done()
    sq.base += DK
    ssum.base += DK
    root.base += 2
    scaled.base += DK
    if out is not None:
        hi_done.base += DK


def steps_of(p, jobs):
    u, o = p.unit, p.out
    for job in jobs:
        n, per = job[1], job[2]
        each = min(n, RAW)
        assert n % each == 0 and each % per == 0 and (each // per) % 2 == 0 and o % 2 == 0
        yield u, o, n // each, each, job
        u += n
        o += n // per


def looped(eng, p, jobs, body, skip=0):
    for u, o, count, each, job in steps_of(p, jobs):
        lo, skip = skip, 0
        if count - lo <= 0:
            continue
        if count - lo == 1:
            body(u + each * lo, o + each // job[2] * lo, lo, each, job, u)
        else:
            with eng.Fori(lo, count) as i:
                body(i * each + u, i * (each // job[2]) + o, i, each, job, u)


def linear(p, jobs, nxt):
    nc = p.nc
    used, taken = p.sig("w_used"), p.sig("out_taken")
    total = sum(j[1] for j in jobs)
    with nc.Block() as block:
        @block.sync
        def _(sp):
            def body(u, o, i, each, job, at):
                for j in range(each):
                    p.load(sp, u + j, (at + j) % RAW, job[0][i * each + j, :, :])
            assert min(jobs[0][1], RAW) == RAW
            looped(sp, p, jobs, body, skip=1)
            p.unit += total
            prefetch(p, sp, nxt)
            p.unit -= total

        @block.scalar
        def _(act):
            def body(u, o, i, each, job, at):
                for j in range(1, each + 1):
                    loads = (at + j) // RAW + 1
                    if each == RAW:
                        loads = i + loads
                    p.split_hi(act, u + j, (at + j) % RAW, loads)
            looped(act, p, jobs, body)

        @block.vector
        def _(dve):
            def body(u, o, i, each, job, at):
                per = job[2]
                for j in range(each):
                    p.split_lo(dve, u + j + 1, (at + j + 1) % RAW)
                    if j % per == per - 1:
                        q = j // per
                        dve.wait_ge(used.sem, u + j + 1)
                        job[4](i * (each // per) + q, p.ps[:, q % 2, :]).then_inc(taken.sem, 1)
            looped(dve, p, jobs, body)

        @block.tensor
        def _(pe):
            def body(u, o, i, each, job, at):
                per = job[2]
                for j in range(each):
                    q = j // per
                    if j % per == 0:
                        pe.wait_ge(taken.sem, o + q - 1)
                    rh, rl = job[3][j % per]
                    p.product(pe, u + j, (at + j) % RAW, p.ps[:, q % 2, :], rh, rl,
                              first=j % per == 0, last=j % per == per - 1).then_inc(used.sem, 1)
            looped(pe, p, jobs, body)
    p.unit += total
    p.out += sum(j[1] // j[2] for j in jobs)


def even_in(p, b, nxt):
    nc = p.nc
    with nc.Block() as block:
        @block.gpsimd
        def _(pool):
            nc.gpsimd.memset(b["xbc"][:, :, 0:CONV - 1], 0.0)
            nc.gpsimd.memset(b["kd"][:, :, :], 0.0)
            nc.gpsimd.memset(b["vt"][:, :], 0.0)
    h = [(p.hh, p.hl)]
    w = p.dram["ev_in"]
    v = nc.vector

    def tail(i, psum):
        if i < 2:
            return v.tensor_copy(b["kd"][:, i, 64:64 + T], psum)
        if i == 2:
            return v.tensor_copy(b["vt"][:, 64:64 + T], psum)
        return v.tensor_copy(b["dtraw"][:, :], psum[0:HEADS, :])

    linear(p, [(w, 8, 1, h, lambda i, ps: v.tensor_copy(b["z"][:, i, :], ps)),
               (w[8:20], XBC, 1, h, lambda i, ps: v.tensor_copy(b["xbc"][:, i, CONV - 1:], ps)),
               (w[20:28], 8, 1, h, lambda i, ps: v.tensor_copy(b["q"][:, i, :], ps)),
               (w[28:32], 4, 1, h, tail)], nxt)


def conv_steps(nc, link, src, dst, taps, bias):
    v = nc.vector
    link(v.tensor_scalar(dst[0], src[:, 0:T], taps[0], bias, ALU.mult, ALU.add))
    for k in range(1, CONV):
        ins = v.scalar_tensor_tensor(out=dst[k % 2], in0=src[:, k:k + T], scalar=taps[k],
                                     in1=dst[(k - 1) % 2], op0=ALU.mult, op1=ALU.add)
        if k < CONV - 1:
            link(ins)
    return ins


def log1p_rows(v, link, rows, small, src, bias, xb, ab, e1, ln, rc):
    dve = link.eng
    link(v.tensor_scalar(xb[:, :], src, bias, None, ALU.add))
    v.scalar_tensor_tensor(out=ab[:, :], in0=xb[:, :], scalar=-1.0, in1=xb[:, :], op0=ALU.mult,
                           op1=ALU.max).then_inc(rows.sem, 1)
    dve.wait_ge(small.sem, small.at(1))
    v.tensor_scalar(ab[:, :], e1[:, :], 1.0, None, ALU.add).then_inc(rows.sem, 1)
    dve.wait_ge(rows.sem, rows.at(2))
    link(v.reciprocal(rc[:, :], ab[:, :]))
    dve.wait_ge(small.sem, small.at(2))
    link(v.tensor_scalar(ab[:, :], ab[:, :], -1.0, None, ALU.add))
    link(v.tensor_tensor(ab[:, :], e1[:, :], ab[:, :], ALU.subtract))
    link(v.tensor_tensor(ab[:, :], ab[:, :], rc[:, :], ALU.mult))
    link(v.tensor_tensor(ln[:, :], ln[:, :], ab[:, :], ALU.add))


def log1p_act(act, nc, rows, small, e1, ab, ln):
    act.wait_ge(rows.sem, rows.at(1))
    nc.scalar.activation(e1[:, :], ab[:, :], ACT.Exp, scale=-1.0).then_inc(small.sem, 1)
    act.wait_ge(rows.sem, rows.at(2))
    nc.scalar.activation(ln[:, :], ab[:, :], ACT.Ln).then_inc(small.sem, 1)


def even_conv(p, b):
    nc = p.nc
    conv, silu, small, rows = (p.sig(n) for n in ("conv_done", "silu_done", "act_small", "rows_ready"))
    dchain = p.sig("dve_chain")
    H = HEADS
    with ExitStack() as ctx:
        tmp = p.sb("conv_sums", [P, 2, T], ctx=ctx)
        xb = p.sb("dt_biased", [H, T], ctx=ctx)
        ab = p.sb("dt_abs", [H, T], ctx=ctx)
        e1 = p.sb("dt_exp", [H, T], ctx=ctx)
        ln = p.sb("dt_log", [H, T], ctx=ctx)
        rc = p.sb("dt_recip", [H, T], ctx=ctx)
        na = p.sb("a_neg", [H, 1], ctx=ctx)
        block = ctx.enter_context(nc.Block())

        @block.vector
        def _(dve):
            v = nc.vector
            link = Chain(dve, dchain)
            log1p_rows(v, link, rows, small, b["dtraw"][:, :], p.col("dt_bias", 0, H), xb, ab, e1, ln, rc)
            link(v.tensor_scalar(xb[:, :], xb[:, :], 0.0, None, ALU.max))
            link(v.tensor_tensor(b["dt"][:, :], xb[:, :], ln[:, :], ALU.add))
            dve.wait_ge(small.sem, small.at(3))
            link(v.tensor_scalar(na[:, :], na[:, :], -1.0, None, ALU.mult))
            link(v.tensor_scalar(b["adt"][:, :], b["dt"][:, :], na[:, 0:1], None, ALU.mult))
            with dve.Fori(0, XBC) as c:
                link.enter(c, CONV - 1)
                dve.wait_ge(silu.sem, c + silu.base + 1)
                conv_steps(nc, link, b["xbc"][:, c, :], (tmp[:, 0, :], tmp[:, 1, :]),
                           [p.par[:, bass.ds(c * CONV + COLS["conv_w"] + k, 1)] for k in range(CONV)],
                           p.par[:, bass.ds(c + COLS["conv_b"], 1)]).then_inc(conv.sem, 1)
                link.leave(XBC)
            link.done()

        @block.scalar
        def _(act):
            log1p_act(act, nc, rows, small, e1, ab, ln)
            nc.scalar.activation(na[:, :], p.col("a_log", 0, H), ACT.Exp).then_inc(small.sem, 1)
            act.sem_inc(silu.sem, 1)
            with act.Fori(0, XBC) as c:
                act.wait_ge(conv.sem, c + conv.base + 1)
                nc.scalar.activation(b["xbc"][:, c, CONV - 1:], tmp[:, 1, :], ACT.Silu).then_inc(silu.sem, 1)
    conv.base += XBC
    silu.base += XBC + 1
    small.base += 3
    rows.base += 2


def even_attention(p, b):
    nc = p.nc
    names = ("att_q", "att_scores", "att_masked", "att_shifted", "att_exp", "att_sink", "att_probs",
             "att_turned", "att_copied", "att_out", "att_hi", "att_lo", "att_v", "att_masks", "att_v_taken")
    sq, sc, sm, sh, se, sk, sp_, st, sy, so, shi, slo, sv, sma, svt = (p.sig(n) for n in names)
    dchain = p.sig("dve_chain")
    SC = 64 ** -0.5
    G = 8
    with ExitStack() as ctx:
        qb = p.sb("q_tile", [P, 8, P], ctx=ctx)
        vb = p.sb("v_tiles", [P, 2, P], ctx=ctx)
        kb = p.sb("k_window", [P, 2, 192], ctx=ctx)
        vp = b["vt"][:, :].rearrange("p (m t) -> p m t", t=P)
        mask = p.sb("att_mask", [P, 2, 192], ctx=ctx)
        S = p.sb("scores", [P, G, 192], ctx=ctx)
        mx = p.sb("att_max", [P, G], ctx=ctx)
        es = p.sb("att_sink_exp", [P, G], ctx=ctx)
        sm_ = p.sb("att_sum", [P, G], ctx=ctx)
        pt = p.sb("probs_turned", [P, 2, G * P], ctx=ctx)
        block = ctx.enter_context(nc.Block())
        per = 2

        @block.gpsimd
        def _(pool):
            g = nc.gpsimd
            g.memset(mask[:, :, :], 0.0).then_inc(sma.sem, 1)
            pool.wait_ge(sma.sem, sma.at(1))
            g.memset(mask[64:P, :, 0:64], NEG)
            g.memset(mask[0:64, :, 128:192], NEG).then_inc(sma.sem, 1)
            pool.wait_ge(sma.sem, sma.at(2))
            g.memset(mask[:, 0, 0:64], NEG).then_inc(sma.sem, 1)

        @block.tensor
        def _(pe):
            for m in range(5):
                ins = nc.tensor.transpose(p.ps[:, m // 4, (m % 4) * P:(m % 4 + 1) * P],
                                          b["vt"][:, m * P:(m + 1) * P], p.ident[:, :])
            ins.then_inc(sv.sem, 1)
            pe.wait_ge(svt.sem, svt.at(1))
            with pe.Fori(0, TT) as j:
                pe.wait_ge(sq.sem, j + sq.base + 1)
                for g in range(per):
                    r = j * per + g
                    pe.wait_ge(sm.sem, r + sm.base + 1)
                    for h in range(G):
                        hd = g * G + 2 * (h % 4) + h // 4
                        rows = slice(64 * (hd % 2), 64 * (hd % 2) + 64)
                        ins = nc.tensor.matmul(p.ps[:, h // 2, (h % 2) * 256:(h % 2) * 256 + 192],
                                               qb[rows, hd // 2, :],
                                               kb[rows, g, :], start=True, stop=True)
                    ins.then_inc(sc.sem, 1)
                    pe.wait_ge(sp_.sem, r + sp_.base + 1)
                    for h in range(G):
                        nc.tensor.transpose(p.ps[:, 4 + h // 4, (h % 4) * P:(h % 4 + 1) * P],
                                            S[:, h, 0:P], p.ident[:, :])
                        ins = nc.tensor.transpose(p.ps[0:64, 6 + h // 4, (h % 4) * P:(h % 4 + 1) * P],
                                                  S[:, h, P:192], p.ident[:, :])
                    ins.then_inc(st.sem, 1)
                    pe.wait_ge(sy.sem, r + sy.base + 1)
                    for h in range(G):
                        c = slice(64 * g, 64 * g + 64)
                        o = p.ps[64 * (h // 4):64 * (h // 4) + 64, 4, (h % 4) * P:(h % 4 + 1) * P]
                        nc.tensor.matmul(o, vb[:, 0, c], pt[:, 0, h * P:(h + 1) * P], start=True, stop=False)
                        ins = nc.tensor.matmul(o, vb[0:64, 1, c], pt[0:64, 1, h * P:(h + 1) * P], start=False, stop=True)
                    ins.then_inc(so.sem, 1)
                    pe.wait_ge(slo.sem, r + slo.base + 1)

        @block.scalar
        def _(act):
            a = nc.scalar
            with act.Fori(0, TT) as j:
                for g in range(per):
                    r = j * per + g
                    act.wait_ge(sh.sem, r + sh.base + 1)
                    a.activation(es[:, :], es[:, :], ACT.Exp).then_inc(sk.sem, 1)
                    a.activation(S[:, :, :], S[:, :, :], ACT.Exp).then_inc(se.sem, 1)
                    act.wait_ge(st.sem, r + st.base + 1)
                    a.activation(pt[:, 0, :], p.ps[:, 4:6, :].rearrange("p b m -> p (b m)"), ACT.Copy)
                    a.activation(pt[0:64, 1, :], p.ps[0:64, 6:8, :].rearrange("p b m -> p (b m)"),
                                 ACT.Copy).then_inc(sy.sem, 1)
                    act.wait_ge(so.sem, r + so.base + 1)
                    a.activation(p.yh[:, g * 4:g * 4 + 4, bass.ds(j * P, P)],
                                 p.ps[:, 4, :].rearrange("p (h t) -> p h t", h=4), ACT.Copy).then_inc(shi.sem, 1)

        @block.vector
        def _(dve):
            v = nc.vector
            link = Chain(dve, dchain)
            dve.wait_ge(sma.sem, sma.at(3))
            dve.wait_ge(sv.sem, sv.at(1))
            v.tensor_copy(vp[:, 0:4, :], p.ps[:, 0, :].rearrange("p (m t) -> p m t", m=4))
            link(v.tensor_copy(vp[:, 4, :], p.ps[:, 1, 0:P]))
            dve.sem_inc(svt.sem, 1)
            dve.sem_inc(sm.sem, 1)
            with dve.Fori(0, TT) as j:
                link.enter(j, 2 + 7 * per)
                link(v.tensor_copy(qb[:, :, :], b["q"][:, :, bass.ds(j * P, P)]))
                v.tensor_copy(kb[:, :, :], b["kd"][:, :, bass.ds(j * P, 192)])
                v.tensor_copy(vb[:, :, :], vp[:, bass.ds(j, 2), :]).then_inc(sq.sem, 1)
                for g in range(per):
                    r = j * per + g
                    sink = p.par[:, COLS["sinks"] + g * G:COLS["sinks"] + (g + 1) * G]
                    dve.wait_ge(sc.sem, r + sc.base + 1)
                    raw = p.ps[:, 0:4, :].rearrange("p b (h m) -> p (b h) m", h=2)[:, :, 0:192]
                    m = mask[:, 0, :].unsqueeze(1).to_broadcast([P, G, 192])
                    ins = v.scalar_tensor_tensor(out=S[:, :, :], in0=raw, scalar=SC, in1=m, op0=ALU.mult, op1=ALU.add)
                    link(ins)
                    dve.sem_inc(sm.sem, 1)
                    link(v.tensor_reduce(mx[:, :], S[:, :, :], AX_X, ALU.max))
                    link(v.tensor_tensor(mx[:, :], mx[:, :], sink, ALU.max))
                    link(v.tensor_tensor(es[:, :], sink, mx[:, :], ALU.subtract))
                    v.tensor_tensor(S[:, :, :], S[:, :, :], mx[:, :].unsqueeze(2).to_broadcast([P, G, 192]),
                                    ALU.subtract).then_inc(sh.sem, 1)
                    dve.wait_ge(se.sem, r + se.base + 1)
                    dve.wait_ge(sk.sem, r + sk.base + 1)
                    link(v.tensor_reduce(sm_[:, :], S[:, :, :], AX_X, ALU.add))
                    link(v.tensor_tensor(sm_[:, :], sm_[:, :], es[:, :], ALU.add))
                    link(v.reciprocal(sm_[:, :], sm_[:, :]))
                    v.tensor_tensor(S[:, :, :], S[:, :, :], sm_[:, :].unsqueeze(2).to_broadcast([P, G, 192]),
                                    ALU.mult).then_inc(sp_.sem, 1)
                    dve.wait_ge(shi.sem, r + shi.base + 1)
                    y = slice(g * 4, g * 4 + 4)
                    v.tensor_tensor(p.yl[:, y, bass.ds(j * P, P)],
                                    p.ps[:, 4, :].rearrange("p (h t) -> p h t", h=4),
                                    p.yh[:, y, bass.ds(j * P, P)].bitcast(F32), ALU.subtract).then_inc(slo.sem, 1)
                link(v.tensor_copy(mask[:, 0, :], mask[:, 1, :]))
                link.leave(TT)
            link.done()
    n = TT * per
    sq.base += TT
    for s in (sc, sh, se, sk, sp_, st, sy, so, shi, slo):
        s.base += n
    sm.base += n + 1
    sv.base += 1
    sma.base += 3
    svt.base += 1


def even_ssd(p, b):
    nc = p.nc
    names = ("ssd_turned", "ssd_cols", "ssd_cb", "ssd_cb_done", "ssd_x", "ssd_xt", "ssd_xdt", "ssd_factors",
             "ssd_arg", "ssd_exp", "ssd_m", "ssd_z", "ssd_out", "ssd_m_used", "ssd_decays")
    (tn, co, cb, cbd, sx, sxt, sxd, fa, ar, ex, sm, sz, ou, mf, dc) = (p.sig(n) for n in names)
    dchain = p.sig("dve_chain")
    H = HEADS
    with ExitStack() as ctx:
        cbm = b["q"]
        cols = p.sb("dt_cols", [P, 2, TT, H + 2], ctx=ctx)
        ac = p.sb("decay_cols", [P, TT, 2], ctx=ctx)
        xs = p.sb("x_pair", [P, T], ctx=ctx)
        xd = p.sb("x_dt", [P, TT, P], ctx=ctx)
        fa1 = p.sb("decays_after", [P, 2, TT, P], ctx=ctx)
        fb1 = p.sb("decays_all", [P, 2, TT, P], ctx=ctx)
        E = p.sb("decay_exp", [P, 2, T], ctx=ctx)
        M = p.sb("ssd_weights", [P, 2, T], ctx=ctx)
        zs = p.sb("z_silu", [P, T], ctx=ctx)
        yt = xs
        block = ctx.enter_context(nc.Block())

        def width(i):
            return T - i * P

        @block.tensor
        def _(pe):
            t = nc.tensor
            for k in range(2):
                for j in range(TT):
                    ins = t.transpose(p.ps[:, 6, (k * TT + j) * H:(k * TT + j + 1) * H],
                                      b[("adt", "dt")[k]][:, j * P:(j + 1) * P], p.ident[0:H, 0:H])
            ins.then_inc(tn.sem, 1)
            for g in range(2):
                if g:
                    pe.wait_ge(cbd.sem, cbd.at(4))
                for i in range(TT):
                    ins = t.matmul(p.ps[:, i, 0:width(i)], b["xbc"][:, 8 + g, 3 + i * P:3 + (i + 1) * P],
                                   b["xbc"][:, 10 + g, 3 + i * P:], start=True, stop=True)
                ins.then_inc(cb.sem, 1)
            pe.wait_ge(cbd.sem, cbd.at(8))
            pe.sem_inc(mf.sem, 2)
            pe.sem_inc(ar.sem, 8)
            for g in range(2):
                with pe.Fori(0, 4) as cc:
                    c = cc + 4 * g
                    pe.wait_ge(sx.sem, c + sx.base + 1)
                    for j in range(TT):
                        ins = t.transpose(p.ps[:, 4, j * P:(j + 1) * P], xs[:, j * P:(j + 1) * P], p.ident[:, :])
                    ins.then_inc(sxt.sem, 1)

                    def weigh(n):
                        h, i = divmod(n, TT)
                        pe.wait_ge(sm.sem, c * 8 + sm.base + n + 3)
                        if n == 0:
                            pe.wait_ge(sxd.sem, c + sxd.base + 1)
                        o = p.ps[64 * h:64 * h + 64, 5, i * P:T]
                        return t.matmul(o, xd[:, i, 64 * h:64 * h + 64], M[:, n % 2, 0:width(i)],
                                        start=i == 0, stop=i == TT - 1, skip_group_check=True)

                    for n in range(8):
                        h, i = divmod(n, TT)
                        if i == 0:
                            pe.wait_ge(fa.sem, c * 2 + fa.base + h + 1)
                        pe.wait_ge(ex.sem, c * 8 + ex.base + n + 1)
                        bank = p.ps[:, n % 2, :]
                        for j in range(i, TT):
                            f = fa1 if j == i else fb1
                            ins = t.matmul(bank[:, (j - i) * P:width(i)], f[:, h, j, :], p.incl[:, 0:width(j)],
                                           start=j == i, stop=j == TT - 1, skip_group_check=True)
                        ins.then_inc(ar.sem, 1)
                        if n:
                            weigh(n - 1).then_inc(mf.sem, 1)
                    ins = weigh(7)
                    ins.then_inc(mf.sem, 1)

        @block.scalar
        def _(act):
            a = nc.scalar
            act.sem_inc(ex.sem, 2)
            with act.Fori(0, 8) as c:
                act.wait_ge(ou.sem, c + ou.base + 1)
                a.activation(zs[:, :], b["z"][:, c, :], ACT.Silu).then_inc(sz.sem, 1)
                for n in range(8):
                    i = n % TT
                    act.wait_ge(ar.sem, c * 8 + ar.base + 8 + n + 1)
                    act.wait_ge(sm.sem, c * 8 + sm.base + n + 1)
                    a.activation(E[:, n % 2, 0:width(i)], p.ps[:, n % 2, 0:width(i)], ACT.Exp).then_inc(ex.sem, 1)

        @block.gpsimd
        def _(pool):
            g_ = nc.gpsimd
            with pool.Fori(0, 8) as c:
                pool.wait_ge(dc.sem, c + dc.base + 1)
                for h in range(2):
                    pool.wait_ge(ar.sem, c * 8 + ar.base + 4 * h + 4)
                    s = ac[:, :, h:h + 1].to_broadcast([P, TT, P])
                    g_.tensor_tensor(fa1[:, h, :, :], p.after[:, :].unsqueeze(1).to_broadcast([P, TT, P]),
                                     s, ALU.mult)
                    g_.tensor_copy(fb1[:, h, :, :], s).then_inc(fa.sem, 1)

        @block.vector
        def _(dve):
            v = nc.vector
            link = Chain(dve, dchain)
            dve.wait_ge(tn.sem, tn.at(1))
            v.memset(cols[:, :, :, H:], 0.0)
            v.tensor_copy(cols[:, :, :, 0:H],
                          p.ps[:, 6, 0:2 * TT * H].rearrange("p (k j h) -> p k j h", k=2, j=TT)
                          ).then_inc(co.sem, 1)
            for g in range(2):
                dve.wait_ge(cb.sem, cb.at(g + 1))
                for i in range(TT):
                    v.tensor_tensor(cbm[:, g * TT + i, 0:width(i)], p.ps[:, i, 0:width(i)],
                                    p.incl[:, 0:width(i)], ALU.mult).then_inc(cbd.sem, 1)
            dve.wait_ge(cbd.sem, cbd.at(8))
            dve.wait_ge(co.sem, co.at(1))
            v.tensor_copy(ac[:, :, :], cols[:, 0, :, 0:2]).then_inc(dc.sem, 1)
            dve.sem_inc(ou.sem, 1)
            dve.sem_inc(sm.sem, 2)
            for g in range(2):
                with dve.Fori(0, 4) as cc:
                    c = cc + 4 * g
                    link.enter(cc, 2)
                    v.tensor_copy(xs[:, :], b["xbc"][:, c, 3:]).then_inc(sx.sem, 1)
                    dve.wait_ge(sxt.sem, c + sxt.base + 1)
                    for h in range(2):
                        ins = v.tensor_tensor(
                            xd[:, :, 64 * h:64 * h + 64],
                            p.ps[:, 4, :].rearrange("p (j q) -> p j q", j=TT)[:, :, 64 * h:64 * h + 64],
                            cols[:, 1, :, bass.ds(c * 2 + h, 1)].to_broadcast([P, TT, 64]), ALU.mult)
                    ins.then_inc(sxd.sem, 1)
                    for n in range(8):
                        i = n % TT
                        dve.wait_ge(ex.sem, c * 8 + ex.base + n + 3)
                        dve.wait_ge(mf.sem, c * 8 + mf.base + n + 1)
                        v.tensor_tensor(M[:, n % 2, 0:width(i)], E[:, n % 2, 0:width(i)],
                                        cbm[:, g * TT + i, 0:width(i)], ALU.mult).then_inc(sm.sem, 1)
                        if n == 4:
                            v.tensor_copy(ac[:, :, :], cols[:, 0, :, bass.ds(c * 2 + 2, 2)]).then_inc(dc.sem, 1)
                    dve.wait_ge(mf.sem, c * 8 + mf.base + 8 + 2)
                    link(v.scalar_tensor_tensor(out=yt[:, :], in0=xs[:, :],
                                                scalar=p.par[:, bass.ds(c + COLS["d_skip"], 1)],
                                                in1=p.ps[:, 5, :], op0=ALU.mult, op1=ALU.add))
                    dve.wait_ge(sz.sem, c + sz.base + 1)
                    link(v.tensor_tensor(b["z"][:, c, :], yt[:, :], zs[:, :], ALU.mult))
                    dve.sem_inc(ou.sem, 1)
                    link.leave(4)
            link.done()
    for s, n in ((tn, 1), (co, 1), (cb, 2), (cbd, 8), (sx, 8), (sxt, 8), (sxd, 8), (fa, 16), (ar, 72),
                 (ex, 66), (sm, 66), (mf, 66), (sz, 8), (ou, 9), (dc, 9)):
        s.base += n


class Rows:

    def __init__(self, p, acts, ga):
        self.p, self.acts, self.ga = p, acts, ga
        self.ge = p.sig("gelu_ready")
        self.stored = (p.sig("gelu_stored0"), p.sig("gelu_stored1"))

    def open(self, act):
        act.sem_inc(self.ge.sem, 2)
        for s in range(2):
            act.sem_inc(self.stored[s].sem, 16)

    def multiply(self, pe, n, s, u, slot):
        p = self.p
        pe.wait_ge(self.ge.sem, n + self.ge.base + 1)
        p.product(pe, u, slot, p.ps[:, s, :], p.hh, p.hl).then_inc(p.sig("w_used").sem, 1)

    def gelu(self, act, n, m, s, u):
        p = self.p
        act.wait_ge(p.sig("w_used").sem, u + 1)
        act.wait_ge(self.stored[s].sem, m * 16 + self.stored[s].base + 16)
        p.nc.scalar.activation(self.ga[:, s, :], p.ps[:, s, :], ACT.Gelu).then_inc(self.ge.sem, 1)
        act.wait_ge(self.ge.sem, n + self.ge.base + 3)
        act.dma_start(self.row(n), self.ga[:, s, :]).then_inc(self.stored[s].sem, 16)

    def row(self, n):
        return self.acts[n, :, :]

    def close(self, act):
        for s in range(2):
            act.wait_ge(self.stored[s].sem, self.stored[s].at(16 + 16 * KEYS // 2))

    def done(self):
        self.ge.base += KEYS + 2
        for s in range(2):
            self.stored[s].base += 16 + 16 * KEYS // 2


def peer_topk(p, b, rows, wq, us, sub, nxt):
    nc = p.nc
    names = ("q_taken", "scores_ready", "scores_taken", "topk_free")
    qt, sr, stk, tf = (p.sig(n) for n in names)
    used, dchain = p.sig("w_used"), p.sig("dve_chain")
    H = PEER_HEADS
    with ExitStack() as ctx:
        subk = p.sb("sub_keys", [P, 2 * H, KEYS], ctx=ctx)
        qf = p.sb("peer_q", [P, 2, T], ctx=ctx)
        s1 = p.sb("peer_scores", [P, 2, TT * KEYS], ctx=ctx)
        s2 = p.sb("peer_scores_left", [P, TT * KEYS], ctx=ctx)
        V = p.sb("side_top", [P, TT, 2, SEL], ctx=ctx)
        I = p.sb("side_index", [P, TT, 2, SEL], U32, ctx=ctx)
        cs = p.sb("pair_sums", [P, TT, SEL * SEL], ctx=ctx)
        held = p.sb("wait_holder", [P, 8], ctx=ctx)
        tv = p.sb("pair_top", [P, TT, SEL], ctx=ctx)
        ti = p.sb("pair_pos", [P, TT, SEL], U32, ctx=ctx)
        cl = p.sb("pair_sums_left", [P, TT, SEL * SEL], ctx=ctx)
        u0 = p.unit
        N = 4 * H + 4
        block = ctx.enter_context(nc.Block())
        sl = p.sig("sub_loaded")

        @block.sync
        def _(sp):
            sp.dma_start(subk[:, :, :], sub).then_inc(sl.sem, 16)
            with sp.Fori(1, H) as h:
                for j in range(4):
                    p.load(sp, h * 4 + u0 + j, (u0 + j) % RAW, (wq, us)[j % 2][h * 2 + j // 2, :, :])
            for j in range(4):
                p.load(sp, u0 + 4 * H + j, (u0 + j) % RAW, us[2 * H + j, :, :])
            p.unit += N
            prefetch(p, sp, nxt)
            p.unit -= N
            sp.wait_ge(sl.sem, sl.at(16))

        @block.tensor
        def _(pe):
            pe.wait_ge(sl.sem, sl.at(16))
            pe.sem_inc(sr.sem, 2)
            with pe.Fori(0, H) as h:
                for s in range(2):
                    u = h * 4 + u0 + 2 * s
                    pe.wait_ge(qt.sem, h * 2 + qt.base + s + 1)
                    p.product(pe, u, (u0 + 2 * s) % RAW, p.ps[:, 4 + s, :], p.hh, p.hl).then_inc(used.sem, 1)
                    rows.multiply(pe, h * 2 + s, s, u + 1, (u0 + 2 * s + 1) % RAW)
                    pe.wait_ge(qt.sem, h * 2 + qt.base + s + 3)
                    pe.wait_ge(stk.sem, h * 2 + stk.base + s + 1)
                    for t in range(TT):
                        ins = nc.tensor.matmul(p.ps[:, 2 + s, t * KEYS:(t + 1) * KEYS],
                                               qf[:, s, t * P:(t + 1) * P],
                                               subk[:, bass.ds(h * 2 + s, 1), :].rearrange("p o k -> p (o k)"),
                                               start=True, stop=True)
                    ins.then_inc(sr.sem, 1)
            for j in range(4):
                rows.multiply(pe, 2 * H + j, j % 2, u0 + 4 * H + j, (u0 + j) % RAW)

        @block.scalar
        def _(act):
            rows.open(act)
            act.sem_inc(qt.sem, 2)
            act.sem_inc(stk.sem, 2)
            with act.Fori(0, H) as h:
                for s in range(2):
                    u, at = h * 4 + u0 + 2 * s, u0 + 2 * s
                    p.split_hi(act, u + 1, (at + 1) % RAW, h + (at + 1) // RAW + 1)
                    act.wait_ge(used.sem, u + 1)
                    act.wait_ge(sr.sem, h * 2 + sr.base + s + 1)
                    nc.scalar.activation(qf[:, s, :], p.ps[:, 4 + s, :], ACT.Copy).then_inc(qt.sem, 1)
                    p.split_hi(act, u + 2, (at + 2) % RAW, h + (at + 2) // RAW + 1)
                    rows.gelu(act, h * 2 + s, h, s, u + 1)
                    act.wait_ge(sr.sem, h * 2 + sr.base + s + 3)
                    act.wait_ge(tf.sem, h * 2 + tf.base + s + 1)
                    nc.scalar.activation(s1[:, s, :], p.ps[:, 2 + s, :], ACT.Copy).then_inc(stk.sem, 1)
            for j in range(4):
                u = u0 + 4 * H + j
                p.split_hi(act, u + 1, (u + 1) % RAW, (u + 1) // RAW + 1)
                rows.gelu(act, 2 * H + j, H + j // 2, j % 2, u)

        @block.vector
        def _(dve):
            v = nc.vector
            link = Chain(dve, dchain)
            dve.sem_inc(tf.sem, 2)

            def best8(values, vals, hold):
                v.memset(held[:, hold:hold + 1], 0.0)
                for t in range(TT):
                    ins = v.max(out=vals[t], in_=values[t])
                return ins

            def where8(values, vals, index, hold, left=None):
                v.memset(held[:, hold:hold + 1], 0.0)
                for t in range(TT):
                    ins = v.max_index(out=index[t], in_max=vals[t], in_values=values[t])
                    if left:
                        ins = v.match_replace(out=left[t], in_to_replace=vals[t], in_values=values[t],
                                              imm_value=-3.0e38)
                return ins

            def top_side(s):
                sv = [s1[:, s, t * KEYS:(t + 1) * KEYS] for t in range(TT)]
                lv = [s2[:, t * KEYS:(t + 1) * KEYS] for t in range(TT)]
                vv = [[V[:, t, s, 8 * k:8 * k + 8] for t in range(TT)] for k in range(2)]
                iv = [[I[:, t, s, 8 * k:8 * k + 8] for t in range(TT)] for k in range(2)]
                link(best8(sv, vv[0], 0))
                link(where8(sv, vv[0], iv[0], 1, lv))
                link(best8(lv, vv[1], 2))
                where8(lv, vv[1], iv[1], 3).then_inc(tf.sem, 1)

            def step(h, first=False, last=False):
                csv, clv = [cs[:, t, :] for t in range(TT)], [cl[:, t, :] for t in range(TT)]
                tvv = [[tv[:, t, 8 * k:8 * k + 8] for t in range(TT)] for k in range(2)]
                tiv = [[ti[:, t, 8 * k:8 * k + 8] for t in range(TT)] for k in range(2)]

                def lo(j):
                    p.split_lo(dve, h * 4 + u0 + j + 1, (u0 + j + 1) % RAW)
                lo(0)
                if not first:
                    dve.wait_ge(stk.sem, h * 2 + stk.base + 2)
                    top_side(1)
                lo(1)
                if not first:
                    dve.wait_ge(tf.sem, h * 2 + tf.base + 2)
                    v.tensor_copy(b["side_index"][:, :, :, bass.ds((h - 1) * SEL, SEL)], I[:, :, :, :])
                    for t in range(TT):
                        ins = v.tensor_tensor(cs[:, t, :].rearrange("p (a c) -> p a c", a=SEL),
                                              V[:, t, 0, :].unsqueeze(2).to_broadcast([P, SEL, SEL]),
                                              V[:, t, 1, :].unsqueeze(1).to_broadcast([P, SEL, SEL]), ALU.add)
                    link(ins)
                    link(best8(csv, tvv[0], 4))
                lo(2)
                if not first:
                    link(where8(csv, tvv[0], tiv[0], 5, clv))
                    link(best8(clv, tvv[1], 6))
                    link(where8(clv, tvv[1], tiv[1], 7))
                    v.tensor_copy(b["top"][:, :, bass.ds((h - 1) * SEL, SEL)], tv[:, :, :])
                    link(v.tensor_copy(b["pos"][:, :, bass.ds((h - 1) * SEL, SEL)], ti[:, :, :]))
                lo(3)
                if not last:
                    dve.wait_ge(stk.sem, h * 2 + stk.base + 3)
                    top_side(0)

            step(0, first=True)
            with dve.Fori(1, H) as h:
                link.enter(h - 1, 12)
                step(h)
                link.leave(H - 1)
            step(H, last=True)
            link.done()
    qt.base += 2 * H + 2
    sr.base += 2 * H + 2
    stk.base += 2 * H + 2
    tf.base += 2 * H + 2
    sl.base += 16
    p.unit += N


def peer_decode(p, b, rows, us, n0, nxt):
    nc = p.nc
    names = ("gate_shifted", "gate_exp", "dec_ready", "dec_turned")
    gs, ge, dr, dt = (p.sig(n) for n in names)
    S = PEER_HEADS * SEL
    NS = TT * S
    N, u0 = 12, p.unit
    with ExitStack() as ctx:
        pi = p.sb("pos_half", [P, 2, NS], U32, ctx=ctx)
        pf = p.sb("pos_float", [P, 2, NS], ctx=ctx)
        eq = p.sb("pos_equal", [P, S * SEL], ctx=ctx)
        key = p.sb("keys_found", [P, 3, NS], ctx=ctx)
        gsum = p.sb("gate_sum", [P, TT * PEER_HEADS], ctx=ctx)
        gx = p.sb("gate_terms", [P, NS], ctx=ctx)
        block = ctx.enter_context(nc.Block())

        @block.sync
        def _(sp):
            with sp.Fori(1, N // 4) as i:
                for j in range(4):
                    p.load(sp, i * 4 + u0 + j, (u0 + j) % RAW, us[i * 4 + n0 + j, :, :])
            p.unit += N
            prefetch(p, sp, nxt)
            p.unit -= N

        @block.scalar
        def _(act):
            act.wait_ge(gs.sem, gs.at(1))
            nc.scalar.activation(gx[:, :], gx[:, :], ACT.Exp).then_inc(ge.sem, 1)
            with act.Fori(0, N // 4) as i:
                for j in range(4):
                    u = u0 + j + 1
                    p.split_hi(act, i * 4 + u, u % RAW, i + u // RAW + 1)
                    rows.gelu(act, i * 4 + n0 + j, i * 2 + (n0 + j) // 2, (n0 + j) % 2, i * 4 + u0 + j)

        @block.tensor
        def _(pe):
            with pe.Fori(0, N // 4) as i:
                for j in range(4):
                    rows.multiply(pe, i * 4 + n0 + j, (n0 + j) % 2, i * 4 + u0 + j, (u0 + j) % RAW)
            pe.wait_ge(dr.sem, dr.at(1))
            for k in range(3):
                for t in range(TT):
                    ins = nc.tensor.transpose(p.ps[:, 2 + k, t * P:(t + 1) * P],
                                              key[:, k, t * P:(t + 1) * P], p.ident[:, :])
            ins.then_inc(dt.sem, 1)

        @block.vector
        def _(dve):
            v = nc.vector
            link = Chain(dve, p.sig("dve_chain"))
            los = iter(range(u0 + 1, u0 + N + 1))

            def lo():
                u = next(los, None)
                if u is not None:
                    p.split_lo(dve, u, u % RAW)

            top = b["top"][:, :, :].rearrange("p t (h s) -> p (t h) s", s=SEL)
            g3 = gx[:, :].rearrange("p (g s) -> p g s", s=SEL)
            v.tensor_tensor(g3, top, top[:, :, 0:1].to_broadcast([P, TT * PEER_HEADS, SEL]),
                            ALU.subtract).then_inc(gs.sem, 1)
            lo()
            pos = b["pos"][:, :, :].rearrange("p t s -> p (t s)")
            v.tensor_scalar(pi[:, 0, :], pos, 4, None, ALU.logical_shift_right)
            link(v.tensor_scalar(pi[:, 1, :], pos, 15, None, ALU.bitwise_and))
            link(v.tensor_copy(pf[:, :, :], pi[:, :, :]))
            dve.wait_ge(ge.sem, ge.at(1))
            link(v.tensor_reduce(gsum[:, :], g3, AX_X, ALU.add))
            link(v.reciprocal(gsum[:, :], gsum[:, :]))
            link(v.tensor_tensor(key[:, 2, :].rearrange("p (g s) -> p g s", s=SEL), g3,
                                 gsum[:, :].unsqueeze(2).to_broadcast([P, TT * PEER_HEADS, SEL]), ALU.mult))
            for t in range(TT):
                for k in range(2):
                    e3 = eq[:, :].rearrange("p (s n) -> p s n", n=SEL)
                    want = pf[:, k, t * S:(t + 1) * S].unsqueeze(2).to_broadcast([P, S, SEL])
                    have = p.iota[:, 0:SEL].unsqueeze(1).to_broadcast([P, S, SEL])
                    link(v.tensor_tensor(e3, want, have, ALU.is_equal))
                    lo()
                    e4 = eq[:, :].rearrange("p (h s n) -> p h s n", h=PEER_HEADS, n=SEL)
                    tab = b["side_index"][:, t, k, :].rearrange("p (h n) -> p h n", n=SEL)
                    link(v.tensor_tensor(e4, e4, tab.unsqueeze(2).to_broadcast([P, PEER_HEADS, SEL, SEL]),
                                         ALU.mult))
                    if k:
                        lo()
                    link(v.tensor_reduce(key[:, k, t * S:(t + 1) * S], e3, AX_X, ALU.add))
            dve.sem_inc(dr.sem, 1)
            dve.wait_ge(dt.sem, dt.at(1))
            v.memset(b["sel"][:, :, T:], 0.0)
            link(v.tensor_copy(b["sel"][:, :, 0:T], p.ps[:, 2:5, :]))
            link.done()
            assert next(los, None) is None
    for s in (gs, ge, dr, dt):
        s.base += 1
    p.unit += N


def peer_gates(p, b, rows, us, n0, gates, nxt):
    nc = p.nc
    names = ("hot_first", "hot_second", "gate_summed", "gate_copied", "gate_stored0", "gate_stored1",
             "gate_keys", "gate_zeroed")
    h1, h2, gm, gc, gd0, gd1, gk, gz = (p.sig(n) for n in names)
    gd = (gd0, gd1)
    R = 16
    H0 = 1
    TS = 2 * TG
    Q = TS // 4
    UN = 12
    NS = T // TS
    u0 = p.unit
    assert NS * UN == KEYS - n0

    def fours(k):
        return range(Q * k // UN, Q * (k + 1) // UN)

    with ExitStack() as ctx:
        o1 = p.sb("first_hot", [P, R, KEYS], ctx=ctx)
        o2 = p.sb("second_hot", [P, R, KEYS], ctx=ctx)
        held = p.sb("wait_holder", [P, Q], ctx=ctx)
        kb = p.sb("token_keys", [P, 2, 3, TG], ctx=ctx)
        gb = p.sb("gate_group", [P, 2, KEYS, TG], ctx=ctx)
        sel = b["sel"]
        block = ctx.enter_context(nc.Block())

        @block.vector
        def _(dve):
            v = nc.vector
            v.tensor_copy(kb[:, 0, :, :], sel[:, :, 0:TG]).then_inc(gk.sem, 1)
            with dve.Fori(0, NS) as g:
                for k in range(UN):
                    p.split_lo(dve, g * UN + u0 + k + 1, (u0 + k + 1) % RAW)
                    for q in fours(k):
                        if q == 4:
                            dve.wait_ge(h2.sem, g * TS + h2.base + H0)
                            v.tensor_copy(kb[:, 1, :, :], sel[:, :, bass.ds(g * TS + TG, TG)]
                                          ).then_inc(gk.sem, 1)
                        if q == 12:
                            dve.wait_ge(h2.sem, g * TS + h2.base + TG + H0)
                            v.tensor_copy(kb[:, 0, :, :], sel[:, :, bass.ds(g * TS + TS, TG)]
                                          ).then_inc(gk.sem, 1)
                        if q % 8 == 0:
                            dve.wait_ge(gk.sem, g * 2 + gk.base + q // 8 + 1)
                        dve.wait_ge(gm.sem, g * TS + gm.base + 4 * q + 4)
                        for t in range(4 * q, 4 * q + 4):
                            c = kb[:, t // TG, :, t % TG:t % TG + 1]
                            ins = v.tensor_scalar(o1[:, t % R, :], p.iota[:, :], c[:, 0, :], c[:, 2, :],
                                                  ALU.is_equal, ALU.mult)
                        ins.then_inc(h1.sem, 4)

        @block.gpsimd
        def _(pool):
            pool.sem_inc(h2.sem, H0)
            nc.gpsimd.memset(gb[:, :, :, :], 0.0).then_inc(gz.sem, 1)

            def store(half, place):
                pool.dma_start(gates[place, :, :], gb[:, half, :, :].rearrange("p a t -> p (a t)")
                               ).then_inc(gd[half].sem, 16)

            pool.wait_ge(gz.sem, gz.at(1))
            store(0, NTG + 1)
            with pool.Fori(0, NS) as g:
                for q in range(Q):
                    if q == 5:
                        pool.wait_ge(gc.sem, g * Q + gc.base + 2)
                        store(1, g * 2)
                    if q == 13:
                        pool.wait_ge(gc.sem, g * Q + gc.base + 2 + Q // 2)
                        store(0, g * 2 + 1)
                    if q % 8 == 0:
                        pool.wait_ge(gk.sem, g * 2 + gk.base + q // 8 + 1)
                    pool.wait_ge(gm.sem, g * TS + gm.base + 4 * q + 4)
                    nc.gpsimd.tensor_tensor(held[:, q:q + 1], p.ones[:, 0:1], p.ones[:, 0:1], ALU.mult)
                    for t in range(4 * q, 4 * q + 4):
                        ins = nc.gpsimd.tensor_scalar(o2[:, t % R, :], p.iota[:, :],
                                                      kb[:, t // TG, 1, t % TG:t % TG + 1], None,
                                                      ALU.is_equal)
                    ins.then_inc(h2.sem, 4)
            pool.wait_ge(gc.sem, gc.at(2 + Q * NS))
            store(1, NTG)
            for s in range(2):
                pool.wait_ge(gd[s].sem, gd[s].at(16 * (NS + 1)))

        @block.tensor
        def _(pe):
            pe.sem_inc(gm.sem, R)
            with pe.Fori(0, NS) as g:
                for k in range(UN):
                    rows.multiply(pe, g * UN + n0 + k, (n0 + k) % 2, g * UN + u0 + k, (u0 + k) % RAW)
                    for q in fours(k):
                        pe.wait_ge(h1.sem, g * TS + h1.base + 4 * q + 4)
                        pe.wait_ge(h2.sem, g * TS + h2.base + H0 + 4 * q + 4)
                        pe.wait_ge(gc.sem, g * Q + gc.base + q + 1)
                        for r in range(4):
                            ins = nc.tensor.matmul(p.ps[:, 2 + q % 2, r * KEYS:(r + 1) * KEYS],
                                                   o2[:, (4 * q + r) % R, :], o1[:, (4 * q + r) % R, :],
                                                   start=True, stop=True)
                        ins.then_inc(gm.sem, 4)

        @block.scalar
        def _(act):
            act.wait_ge(gz.sem, gz.at(1))
            act.sem_inc(gc.sem, 2)
            with act.Fori(0, NS) as g:
                for k in range(UN):
                    u = u0 + k + 1
                    p.split_hi(act, g * UN + u, u % RAW, g * (UN // RAW) + u // RAW + 1)
                    rows.gelu(act, g * UN + n0 + k, g * (UN // 2) + (n0 + k) // 2, (n0 + k) % 2, g * UN + u0 + k)
                    for q in fours(k):
                        half, at = divmod(4 * q, TG)
                        act.wait_ge(gm.sem, g * TS + gm.base + R + 4 * q + 4)
                        if at == 0:
                            act.wait_ge(gd[half].sem, g * 16 + gd[half].base + 16)
                        nc.scalar.activation(gb[:, half, :, at:at + 4].rearrange("p a t -> p t a"),
                                             p.ps[:, 2 + q % 2, :].rearrange("p (t a) -> p t a", t=4),
                                             ACT.Copy).then_inc(gc.sem, 1)
            rows.close(act)

        @block.sync
        def _(sp):
            for j in range(RAW, UN):
                p.load(sp, u0 + j, (u0 + j) % RAW, us[n0 + j, :, :])
            with sp.Fori(1, NS) as g:
                for k in range(UN):
                    p.load(sp, g * UN + u0 + k, (u0 + k) % RAW, us[g * UN + n0 + k, :, :])
            p.unit += NS * UN
            prefetch(p, sp, nxt)
            p.unit -= NS * UN
    h1.base += T
    h2.base += T + H0
    gm.base += T + R
    gc.base += T // 4 + 2
    gk.base += 2 * NS + 1
    gz.base += 1
    for s in gd:
        s.base += 16 * (NS + 1)
    rows.done()
    p.unit += NS * UN


def peer_values(p, acts, gates, vs, nxt):
    nc = p.nc
    names = ("gated", "act_hi", "act_lo", "block_loaded0", "block_loaded1")
    gt_, ah, al, bl0, bl1 = (p.sig(n) for n in names)
    bl = (bl0, bl1)
    used = p.sig("w_used")
    u0 = p.unit
    B = BLOCK
    halves = ((p.yh, p.yl), (p.hh, p.hl))
    with ExitStack() as ctx:
        at = p.sb("gelu_block", [P, 2, B, T], ctx=ctx)
        gt = p.sb("gate_block", [P, 2, NTG, B * TG], ctx=ctx)
        block = ctx.enter_context(nc.Block())

        def blocks(eng, body):
            body(0, 0, 0, 0)
            with eng.Fori(0, NBLOCK // 2 - 1) as ii:
                for k in range(2):
                    body(ii * 2 + 1 + k, (1 + k) % 2, None, ii + 1)
            body(NBLOCK - 1, 1, NBLOCK - 1, None)

        @block.sync
        def _(sp):
            for j in range(RAW, B):
                p.load(sp, u0 + j, (u0 + j) % RAW, vs[j, :, :])
            with sp.Fori(1, NBLOCK) as i:
                for j in range(B):
                    p.load(sp, i * B + u0 + j, (u0 + j) % RAW, vs[i * B + j, :, :])
            p.unit += B * NBLOCK
            prefetch(p, sp, nxt)
            p.unit -= B * NBLOCK

        @block.gpsimd
        def _(pool):
            with pool.Fori(0, NBLOCK // 2) as ii:
                for s in range(2):
                    i = ii * 2 + s
                    pool.wait_ge(al.sem, i * B + al.base + B)
                    pool.dma_start(at[:, s, :, :], acts.rearrange("n p t -> p n t")[:, bass.ds(i * B, B), :]
                                   ).then_inc(bl[s].sem, 16)
                    pool.dma_start(gt[:, s, :, :],
                                   gates[1:NTG + 1, :, :].rearrange("g p m -> p g m")[:, :, bass.ds(i * (B * TG), B * TG)]
                                   ).then_inc(bl[s].sem, 16)

        def hi(act, i, s, j):
            act.wait_ge(gt_.sem, i * B + gt_.base + j + 1)
            nc.scalar.activation(halves[s][0][:, j, :], at[:, s, j, :], ACT.Copy).then_inc(ah.sem, 1)

        def mult(dve, i, s, j, ii):
            if j == 0:
                dve.wait_ge(bl[s].sem, ii * 32 + bl[s].base + 32)
            a3 = at[:, s, j, :].rearrange("p (g t) -> p g t", g=NTG)
            nc.vector.tensor_tensor(a3, a3, gt[:, s, :, j * TG:(j + 1) * TG], ALU.mult).then_inc(gt_.sem, 1)

        def lo(dve, i, s, j):
            dve.wait_ge(ah.sem, i * B + ah.base + j + 1)
            nc.vector.tensor_tensor(halves[s][1][:, j, :], at[:, s, j, :],
                                    halves[s][0][:, j, :].bitcast(F32), ALU.subtract).then_inc(al.sem, 1)

        @block.tensor
        def _(pe):
            def body(i, s, fixed, half):
                for j in range(B):
                    def tile(k):
                        if j == 0:
                            pe.wait_ge(al.sem, i * B + al.base + 2 * B + k + 1)
                    p.product(pe, i * B + u0 + j, (u0 + j) % RAW, p.ps[:, j, :], *halves[s],
                              first=fixed == 0, last=fixed == NBLOCK - 1, wait_tile=tile
                              ).then_inc(used.sem, 1)
            blocks(pe, body)

        @block.scalar
        def _(act):
            for j in range(B):
                hi(act, 0, 0, j)

            def body(i, s, fixed, half):
                for j in range(B):
                    u = u0 + j + 1
                    p.split_hi(act, i * B + u, u % RAW, i * (B // RAW) + u // RAW + 1)
                    if fixed != NBLOCK - 1:
                        hi(act, i + 1, 1 - s, j)
            blocks(act, body)

        @block.vector
        def _(dve):
            dve.sem_inc(al.sem, 2 * B)
            for j in range(B):
                mult(dve, 0, 0, j, 0)
                if j:
                    lo(dve, 0, 0, j - 1)

            def body(i, s, fixed, half):
                for j in range(B):
                    p.split_lo(dve, i * B + u0 + j + 1, (u0 + j + 1) % RAW)
                    if j == 0:
                        lo(dve, i, s, B - 1)
                    if fixed != NBLOCK - 1:
                        mult(dve, i + 1, 1 - s, j, half)
                        if j:
                            lo(dve, i + 1, 1 - s, j - 1)
                    else:
                        dve.wait_ge(used.sem, u0 + i * B + j + 1)
                        nc.vector.tensor_tensor(p.x[:, j, :], p.ps[:, j, :], p.x[:, j, :], ALU.add)
            blocks(dve, body)
    for s in (gt_, ah):
        s.base += KEYS
    al.base += KEYS + 2 * B
    for s in bl:
        s.base += 32 * NBLOCK // 2
    p.unit += B * NBLOCK


def ple_embed(p, pw, w, emb, nxt):
    nc = p.nc
    ld, hi, lo, used = p.sig("emb_loaded"), p.sig("emb_hi"), p.sig("emb_lo"), p.sig("w_used")
    pt = p.sig("emb_taken")
    u0 = p.unit
    with ExitStack() as ctx:
        e = p.sb("embedding", [P, 2, T], ctx=ctx)
        block = ctx.enter_context(nc.Block())

        @block.sync
        def _(sp):
            sp.dma_start(e[:, :, :], emb).then_inc(ld.sem, 16)
            p.unit += 4
            prefetch(p, sp, nxt[:2])
            p.unit -= 4
            sp.wait_ge(ld.sem, ld.at(16))

        @block.scalar
        def _(act):
            act.wait_ge(ld.sem, ld.at(16))
            nc.scalar.activation(p.yh[:, 0:2, :], e[:, :, :], ACT.Copy).then_inc(hi.sem, 1)
            for j in range(1, 3):
                p.split_hi(act, u0 + j, (u0 + j) % RAW, (u0 + j) // RAW + 1)

        @block.vector
        def _(dve):
            v = nc.vector
            dve.wait_ge(hi.sem, hi.at(1))
            v.tensor_tensor(p.yl[:, 0:2, :], e[:, :, :], p.yh[:, 0:2, :].bitcast(F32),
                            ALU.subtract).then_inc(lo.sem, 1)
            for j in range(2):
                p.split_lo(dve, u0 + j + 1, (u0 + j + 1) % RAW)
                dve.wait_ge(used.sem, u0 + j + 1)
                v.tensor_copy(pw[:, 4 * j:4 * j + 4, :], p.ps[:, 4 * j:4 * j + 4, :]).then_inc(pt.sem, 1)

        @block.tensor
        def _(pe):
            pe.wait_ge(lo.sem, lo.at(1))
            for j in range(2):
                u = u0 + j
                pe.wait_ge(p.sig("w_lo_ready").sem, u + 1)
                for q in range(4):
                    for k in range(2):
                        w_ = slice((q * 2 + k) * P, (q * 2 + k + 1) * P)
                        for m, (a, y) in enumerate(((p.wh, p.yh), (p.wh, p.yl), (p.wl, p.yh))):
                            ins = nc.tensor.matmul(p.ps[:, 4 * j + q, :], a[:, u % SPL, w_], y[:, k, :],
                                                   start=k == 0 and m == 0, stop=k == 1 and m == 2)
                ins.then_inc(used.sem, 1)
    ld.base += 16
    hi.base += 1
    lo.base += 1
    pt.base += 2
    p.unit += 2


def ple_add(p, sg, pw):
    nc = p.nc
    sd, md = p.sig("sigmoid_done"), p.sig("ple_mul")
    with nc.Block() as block:
        @block.scalar
        def _(act):
            for k in range(DK):
                nc.scalar.activation(sg[:, k, :], sg[:, k, :], ACT.Sigmoid).then_inc(sd.sem, 1)

        @block.vector
        def _(dve):
            v = nc.vector
            for k in range(DK + 1):
                if k < DK:
                    dve.wait_ge(sd.sem, sd.at(k + 1))
                    v.tensor_tensor(pw[:, k, :], sg[:, k, :], pw[:, k, :], ALU.mult).then_inc(md.sem, 1)
                if k:
                    dve.wait_ge(md.sem, md.at(k))
                    v.tensor_tensor(p.x[:, k - 1, :], p.x[:, k - 1, :], pw[:, k - 1, :], ALU.add)
    sd.base += DK
    md.base += DK


def odd_gates(p, b, nxt):
    nc = p.nc
    small, rows, used = p.sig("act_small"), p.sig("rows_ready"), p.sig("w_used")
    tn = p.sig("gates_turned")
    H = HEADS
    u = p.unit
    with ExitStack() as ctx:
        names = ("xb", "ab", "e1", "ln", "rc", "F", "ig", "G", "one", "em")
        r = {n: p.sb(f"gate_{n}", [H, T], ctx=ctx) for n in names}
        block = ctx.enter_context(nc.Block())

        @block.sync
        def _(sp):
            p.unit += 4
            prefetch(p, sp, nxt[3:4])
            p.unit -= 4

        @block.scalar
        def _(act):
            p.split_hi(act, u + 1, (u + 1) % RAW, (u + 1) // RAW + 1)
            log1p_act(act, nc, rows, small, r["e1"], r["ab"], r["ln"])
            act.wait_ge(rows.sem, rows.at(3))
            nc.scalar.activation(r["em"][:, :], r["em"][:, :], ACT.Exp, scale=-1.0).then_inc(small.sem, 1)

        @block.tensor
        def _(pe):
            p.product(pe, u, u % RAW, p.ps[:, 7, :], p.hh, p.hl).then_inc(used.sem, 1)
            pe.wait_ge(small.sem, small.at(3))
            for k, n in enumerate(("ig", "em")):
                for j in range(TT):
                    ins = nc.tensor.transpose(p.ps[:, 6, (k * TT + j) * H:(k * TT + j + 1) * H],
                                              r[n][:, j * P:(j + 1) * P], p.ident[0:H, 0:H])
            ins.then_inc(tn.sem, 1)

        @block.vector
        def _(dve):
            v = nc.vector
            link = Chain(dve, p.sig("dve_chain"))
            v.memset(r["one"][:, :], 1.0)
            p.split_lo(dve, u + 1, (u + 1) % RAW)
            dve.wait_ge(used.sem, u + 1)
            link(v.tensor_copy(r["G"][:, :], p.ps[32:32 + H, 7, :]))
            log1p_rows(v, link, rows, small, r["G"][:, :], p.col("f_bias", 0, H), r["xb"], r["ab"],
                       r["e1"], r["ln"], r["rc"])
            link(v.tensor_scalar(r["xb"][:, :], r["xb"][:, :], 0.0, None, ALU.min))
            link(v.tensor_tensor(r["xb"][:, :], r["xb"][:, :], r["ln"][:, :], ALU.subtract))
            link(v.tensor_tensor_scan(r["F"][:, :], r["one"][:, :], r["xb"][:, :], 0.0, ALU.mult, ALU.add))
            link(v.tensor_scalar(r["ig"][:, :], p.ps[0:H, 7, :], p.col("i_bias", 0, H), None, ALU.add))
            link(v.tensor_tensor(r["ig"][:, :], r["ig"][:, :], r["F"][:, :], ALU.subtract))
            link(v.tensor_tensor_scan(r["G"][:, :], r["one"][:, :], r["ig"][:, :], 0.0, ALU.mult, ALU.max))
            link(v.tensor_scalar(b["negG"][:, :], r["G"][:, :], -1.0, None, ALU.mult))
            v.tensor_tensor(r["em"][:, :], r["F"][:, :], r["G"][:, :], ALU.add).then_inc(rows.sem, 1)
            dve.wait_ge(tn.sem, tn.at(1))
            link(v.tensor_copy(b["cols"][:, :, :, :].rearrange("p k j h -> p (k j h)"),
                               p.ps[:, 6, 0:2 * TT * H]))
            link(v.memset(b["hn"][:, :, :], 0.0))
            link(v.memset(b["os"][:, :], 0.0))
            link(v.memset(b["qk"][:, :, 0:CONV - 1], 0.0))
            link(v.memset(b["vs"][:, :, :], 1.0))
            link.done()
    small.base += 3
    rows.base += 3
    tn.base += 1
    p.unit += 1


def odd_heads(p, b, half, w, nxt):
    nc = p.nc
    names = ("od_conv", "od_silu", "od_y", "od_yhi", "od_sel", "od_bc", "od_s", "od_arg", "od_exp", "od_sw",
             "od_vt", "od_vs", "od_num", "od_sig", "od_ssq", "od_ms", "od_root", "od_hn", "od_turn")
    (cv, si, yy, yh, se, bc, sc, ag, ex, sw, vt, vs, nu, sg, sq, ms, ro, hn, tu) = (p.sig(n) for n in names)
    used, taken = p.sig("w_used"), p.sig("out_taken")
    u0, o0 = p.unit, p.out
    NH = HEADS // 2
    SC = P ** -0.5
    W = b["w"]
    blocks = [(4, 0), (5, 0), (6, 0), (6, 256)]

    def width(i):
        return T - i * P

    def turn(pe, n):
        pe.wait_ge(hn.sem, n)
        for j in range(TT):
            ins = nc.tensor.transpose(p.ps[:, 7, j * P:(j + 1) * P], b["hn"][:, j, :], p.ident[:, :])
        ins.then_inc(tu.sem, 1)

    def gate(dve, n, h):
        dve.wait_ge(tu.sem, n + tu.base + 1)
        dve.wait_ge(sg.sem, n + sg.base + 1)
        return nc.vector.scalar_tensor_tensor(out=b["yf"][:, :], in0=p.ps[:, 7, :],
                                              scalar=p.par[:, bass.ds(h + COLS["head_norm"], 1)],
                                              in1=b["os"][:, :], op0=ALU.mult, op1=ALU.mult)

    def split(dve, n, slot):
        dve.wait_ge(yh.sem, n + yh.base + 1)
        return nc.vector.tensor_tensor(p.yl[:, slot, :], b["yf"][:, :], p.yh[:, slot, :].bitcast(F32),
                                       ALU.subtract)

    with nc.Block() as block:
        @block.sync
        def _(sp):
            with sp.Fori(1, NH) as i:
                for j in range(4):
                    p.load(sp, i * 4 + u0 + j, (u0 + j) % RAW, w[i * 4 + j, :, :])
            p.unit += 4 * NH
            prefetch(p, sp, nxt)
            p.unit -= 4 * NH

        @block.tensor
        def _(pe):
            t = nc.tensor

            def lin(i, j):
                if j == 1:
                    pe.wait_ge(sg.sem, i + sg.base + 1)
                else:
                    pe.wait_ge(taken.sem, i * 3 + o0 + (0, None, 1, 2)[j])
                p.product(pe, i * 4 + u0 + j, (u0 + j) % RAW, p.ps[:, j % 2, :], p.hh, p.hl
                          ).then_inc(used.sem, 1)
            with pe.Fori(0, NH) as i:
                lin(i, 0)
                turn(pe, i + hn.base + 1)
                lin(i, 1)
                lin(i, 2)
                pe.wait_ge(se.sem, i + se.base + 1)
                t.matmul(p.ps[:, 2, :], p.ones[0:HEADS, :], b["rsel"][:, :], start=True, stop=True
                         ).then_inc(bc.sem, 1)
                pe.wait_ge(si.sem, i * 2 + si.base + 2)
                for s in range(TT):
                    bank, c = blocks[s]
                    ins = t.matmul(p.ps[:, bank, c:c + width(s)], b["kT"][:, s * P:(s + 1) * P],
                                   b["qT"][:, s * P:], start=True, stop=True, skip_group_check=True)
                ins.then_inc(sc.sem, 1)
                lin(i, 3)
                pe.wait_ge(taken.sem, i * 3 + o0 + 3)
                for j in range(TT):
                    ins = t.transpose(p.ps[:, 3, j * P:(j + 1) * P], b["vT"][:, j * P:(j + 1) * P], p.ident[:, :])
                ins.then_inc(vt.sem, 1)
                pe.wait_ge(vs.sem, i + vs.base + 1)
                pe.wait_ge(sw.sem, i + sw.base + 1)
                for j in range(TT):
                    for s in range(j + 1):
                        ins = t.matmul(p.ps[:, 2 + j // 2, (j % 2) * 130:(j % 2) * 130 + 130],
                                       W[:, s, j * P:(j + 1) * P], b["vs"][:, s, :], start=s == 0, stop=s == j)
                ins.then_inc(nu.sem, 1)
            turn(pe, NH + hn.base + 1)

        @block.scalar
        def _(act):
            a = nc.scalar
            if half == 0:
                act.sem_inc(sg.sem, 1)
            with act.Fori(0, NH) as i:
                for j in range(4):
                    p.split_hi(act, i * 4 + u0 + j + 1, (u0 + j + 1) % RAW, i + (u0 + j + 1) // RAW + 1)
                    if j == 0:
                        act.wait_ge(yy.sem, i + yy.base + 1)
                        a.activation(p.yh[:, i, :], b["yf"][:, :], ACT.Copy).then_inc(yh.sem, 1)
                    if j < 2:
                        act.wait_ge(cv.sem, i * 2 + cv.base + j + 1)
                        a.activation(b["kT" if j == 0 else "qT"][:, :], b["tmp"][:, 1, :], ACT.Silu
                                     ).then_inc(si.sem, 1)
                for s in range(TT):
                    act.wait_ge(ag.sem, i * 4 + ag.base + s + 1)
                    a.activation(W[:, s, s * P:], W[:, s, s * P:], ACT.Exp).then_inc(ex.sem, 1)
                act.wait_ge(used.sem, i * 4 + u0 + 4)
                a.activation(b["os"][:, :], p.ps[:, 1, :], ACT.Sigmoid).then_inc(sg.sem, 1)
                act.wait_ge(nu.sem, i + nu.base + 1)
                for j in range(TT):
                    ins = a.activation(b["sqj"][:, :], p.ps[:, 2 + j // 2, (j % 2) * 130:(j % 2) * 130 + P],
                                       ACT.Square, accum_out=b["small"][:, 0, j:j + 1])
                    ins.then_inc(sq.sem, 1)
                    act.wait_ge(sq.sem, i * 4 + sq.base + j + 1)
                act.wait_ge(ms.sem, i + ms.base + 1)
                a.activation(b["small"][:, 3, :], b["small"][:, 3, :], ACT.Sqrt).then_inc(ro.sem, 1)
            act.wait_ge(yy.sem, NH + yy.base + 1)
            a.activation(p.yh[:, 0, :], b["yf"][:, :], ACT.Copy).then_inc(yh.sem, 1)

        @block.vector
        def _(dve):
            v = nc.vector
            link = Chain(dve, p.sig("dve_chain"))
            sm = b["small"]
            dve.sem_inc(hn.sem, 1)

            def lo(i, j):
                p.split_lo(dve, i * 4 + u0 + j + 1, (u0 + j + 1) % RAW)

            def conv(i, j):
                dve.wait_ge(used.sem, i * 4 + u0 + j + 1)
                v.tensor_copy(b["qk"][:, j, CONV - 1:], p.ps[:, j % 2, :]).then_inc(taken.sem, 1)
                dve.wait_ge(taken.sem, i * 3 + o0 + j + 1)
                if j:
                    dve.wait_ge(si.sem, i * 2 + si.base + j)
                tile = i + (HEADS if j == 0 else 0) + half * NH
                conv_steps(nc, link, b["qk"][:, j, :], (b["tmp"][:, 0, :], b["tmp"][:, 1, :]),
                           [p.par[:, bass.ds(tile * CONV + COLS["od_conv_w"] + k, 1)] for k in range(CONV)],
                           p.par[:, bass.ds(tile + COLS["od_conv_b"], 1)]).then_inc(cv.sem, 1)

            with dve.Fori(0, NH) as i:
                link.enter(i, 2 * 3 + 13)
                h = i + half * NH
                lo(i, 0)
                gate(dve, i, h - 1).then_inc(yy.sem, 1)
                conv(i, 0)
                lo(i, 1)
                link(split(dve, i, i))
                conv(i, 1)
                lo(i, 2)
                dve.wait_ge(used.sem, i * 4 + u0 + 3)
                v.tensor_copy(b["vT"][:, :], p.ps[:, 0, :]).then_inc(taken.sem, 1)
                v.tensor_scalar(b["rsel"][:, :], b["negG"][:, :], p.ident[0:HEADS, bass.ds(h, 1)], None,
                                ALU.mult).then_inc(se.sem, 1)
                lo(i, 3)
                dve.wait_ge(bc.sem, i + bc.base + 1)
                for s in range(TT):
                    v.tensor_scalar(W[:, s, s * P:], p.ps[:, 2, s * P:], b["cols"][:, 0, s, bass.ds(h, 1)], 0.0,
                                    ALU.add, ALU.min).then_inc(ag.sem, 1)
                dve.wait_ge(sc.sem, i + sc.base + 1)
                for s in range(TT):
                    dve.wait_ge(ex.sem, i * 4 + ex.base + s + 1)
                    bank, c = blocks[s]
                    ins = v.scalar_tensor_tensor(out=W[:, s, s * P:], in0=p.ps[:, bank, c:c + width(s)],
                                                 scalar=SC, in1=W[:, s, s * P:], op0=ALU.mult, op1=ALU.mult)
                    link(ins)
                for s in range(TT):
                    ins = v.tensor_tensor(W[:, s, s * P:(s + 1) * P], W[:, s, s * P:(s + 1) * P],
                                          p.incl[:, 0:P], ALU.mult)
                ins.then_inc(sw.sem, 1)
                dve.wait_ge(vt.sem, i + vt.base + 1)
                v.tensor_copy(b["vs"][:, :, 0:P], p.ps[:, 3, :].rearrange("p (j e) -> p j e", j=TT)
                              ).then_inc(vs.sem, 1)
                dve.wait_ge(sq.sem, i * 4 + sq.base + 4)
                den = p.ps[:, 2:4, 0:260].rearrange("p b (j e) -> p b j e", e=130)[:, :, :, P]
                s4 = [sm[:, k, :] for k in range(5)]
                link(v.tensor_copy(s4[1].rearrange("p (b j) -> p b j", b=2), den))
                link(v.scalar_tensor_tensor(out=s4[2], in0=s4[1], scalar=-1.0, in1=s4[1], op0=ALU.mult,
                                            op1=ALU.max))
                link(v.tensor_tensor(s4[2], s4[2], b["cols"][:, 1, :, bass.ds(h, 1)].rearrange("p j o -> p (j o)"),
                                     ALU.max))
                link(v.reciprocal(s4[1], s4[2]))
                link(v.scalar_tensor_tensor(out=s4[2], in0=s4[0], scalar=1.0 / P, in1=s4[1], op0=ALU.mult,
                                            op1=ALU.mult))
                link(v.tensor_tensor(s4[2], s4[2], s4[1], ALU.mult))
                v.tensor_scalar(s4[3], s4[2], EPS, None, ALU.add).then_inc(ms.sem, 1)
                dve.wait_ge(ro.sem, i + ro.base + 1)
                link(v.reciprocal(s4[4], s4[3]))
                link(v.tensor_tensor(s4[4], s4[4], s4[1], ALU.mult))
                num = p.ps[:, 2:4, 0:260].rearrange("p b (j e) -> p b j e", e=130)[:, :, :, 0:P]
                v.tensor_tensor(b["hn"][:, :, :].rearrange("p (b j) e -> p b j e", b=2), num,
                                s4[4].rearrange("p (b j) -> p b j", b=2).unsqueeze(3).to_broadcast([P, 2, 2, P]),
                                ALU.mult).then_inc(hn.sem, 1)
                link.leave(NH)
            gate(dve, NH, half * NH + NH - 1).then_inc(yy.sem, 1)
            link(split(dve, NH, 0))
            link.done()
    for s, n in ((cv, 2), (si, 2), (se, 1), (bc, 1), (sc, 1), (ag, 4), (ex, 4), (sw, 1), (vt, 1),
                 (vs, 1), (nu, 1), (sg, 1), (sq, 4), (ms, 1), (ro, 1)):
        s.base += n * NH
    for s in (yy, yh, hn, tu):
        s.base += NH + 1
    p.unit += 4 * NH
    p.out += 3 * NH


def store(p, src):
    nc = p.nc
    done = p.sig("stored")
    with nc.Block() as block:
        @block.sync
        def _(sp):
            sp.dma_start(p.dram["out"], src[:, :, :]).then_inc(done.sem, 16)
            sp.wait_ge(done.sem, done.at(16))
    done.base += 16


def add_to(p):
    return lambda i, ps: p.nc.vector.tensor_tensor(p.x[:, i, :], ps, p.x[:, i, :], ALU.add)


def firsts(src, n=RAW):
    return [src[j, :, :] for j in range(n)]


def ffn_firsts(d, layer):
    w, u = d[f"wq{layer}"], d[f"u{layer}"]
    return [w[0, :, :], u[0, :, :], w[1, :, :], u[1, :, :]]


def ffn(p, layer, nxt):
    d = p.dram
    wq, us, vs, gate, pw_ = (d[f"{n}{layer}"] for n in ("wq", "u", "v", "gate", "plew"))
    norm(p, p.x, f"norm_ffn{layer}", out=(p.hh, p.hl))
    with ExitStack() as outer:
        b = {"sel": p.sb("selected", [P, 3, T + TG], ctx=outer)}
        rows = Rows(p, d["acts"], p.sb("gelu", [P, 2, T], ctx=outer))
        with ExitStack() as ctx:
            b["side_index"] = p.sb("key_index", [P, TT, 2, P], ctx=ctx)
            b["top"] = p.sb("top_sums", [P, TT, P], ctx=ctx)
            b["pos"] = p.sb("top_pos", [P, TT, P], U32, ctx=ctx)
            n1 = 2 * PEER_HEADS + 4
            peer_topk(p, b, rows, wq, us, d[f"sub{layer}"], firsts(us[n1:]))
            peer_decode(p, b, rows, us, n1, firsts(us[n1 + 12:]))
        peer_gates(p, b, rows, us, n1 + 12, d["gates"], firsts(vs))
    peer_values(p, d["acts"], d["gates"], vs, [pw_[0, :, :], pw_[1, :, :], gate[0, :, :], gate[1, :, :]])
    norm(p, p.x, f"norm_ple{layer}", out=(p.hh, p.hl))
    with ExitStack() as ctx:
        pw = p.sb("embedded", [P, DK, T], ctx=ctx)
        sg = p.sb("ple_gate", [P, DK, T], ctx=ctx)
        ple_embed(p, pw, pw_, d["emb"][layer], [gate[2, :, :], gate[3, :, :]])
        linear(p, [(gate, DK, 1, [(p.hh, p.hl)],
                    lambda i, ps: p.nc.vector.tensor_copy(sg[:, i, :], ps))], nxt)
        ple_add(p, sg, pw)


def trunk(nc, dram):
    with ExitStack() as ctx:
        p = Program(nc, ctx, dram)
        start(p, firsts(dram["ev_in"]))
        norm(p, p.x, "norm_mix0", out=(p.hh, p.hl))
        with ExitStack() as c:
            b = {"z": p.sb("z", [P, DK, T], ctx=c), "xbc": p.sb("xbc", [P, XBC, CONV - 1 + T], ctx=c),
                 "q": p.sb("q", [P, 8, T], ctx=c)}
            with ExitStack() as c2:
                b["dtraw"] = p.sb("dt_raw", [HEADS, T], ctx=c2)
                with ExitStack() as c3:
                    b["kd"] = p.sb("k_twice", [P, 2, 640], ctx=c3)
                    b["vt"] = p.sb("v_rows", [P, 640], ctx=c3)
                    even_in(p, b, firsts(dram["ev_out"]))
                    even_attention(p, b)
                b["dt"] = p.sb("dt", [HEADS, T], ctx=c2)
                b["adt"] = p.sb("a_dt", [HEADS, T], ctx=c2)
                even_conv(p, b)
                even_ssd(p, b)
            norm(p, b["z"], "out_norm", out=(p.hh, p.hl))
        linear(p, [(dram["ev_out"], 16, 2, [(p.hh, p.hl), (p.yh, p.yl)], add_to(p))], ffn_firsts(dram, 0))
        ffn(p, 0, firsts(dram["od_in"]))
        norm(p, p.x, "norm_mix1", out=(p.hh, p.hl))
        with ExitStack() as c:
            b = {"negG": p.sb("neg_g", [HEADS, T], ctx=c), "cols": p.sb("gate_cols", [P, 2, TT, HEADS], ctx=c),
                 "hn": p.sb("head_out", [P, TT, P], ctx=c), "os": p.sb("o_sigmoid", [P, T], ctx=c),
                 "qk": p.sb("qk_rows", [P, 2, CONV - 1 + T], ctx=c), "vs": p.sb("v_turned_od", [P, TT, 130], ctx=c)}
            odd_gates(p, b, firsts(dram["od_in"], 5)[1:])
            for n, shape in (("w", [P, TT, T]), ("kT", [P, T]), ("qT", [P, T]), ("vT", [P, T]),
                             ("tmp", [P, 2, T]), ("yf", [P, T]), ("rsel", [HEADS, T]), ("sqj", [P, P]),
                             ("small", [P, 5, TT])):
                b[n] = p.sb(f"od_{n}", shape, ctx=c)
            y = [(p.yh, p.yl)]
            w = dram["od_in"]
            odd_heads(p, b, 0, w[1:33], firsts(dram["od_out"]))
            linear(p, [(dram["od_out"], 8, 1, y, add_to(p))], firsts(w[33:65]))
            odd_heads(p, b, 1, w[33:65], firsts(dram["od_out"][8:16]))
            linear(p, [(dram["od_out"][8:16], 8, 1, y, add_to(p))], ffn_firsts(dram, 1))
        ffn(p, 1, firsts(dram["ev_in"], 1))
        norm(p, p.x, "norm_final", dst=p.x)
        store(p, p.x)


def _units(w, tiles=DK):
    K, N = w.shape
    return np.ascontiguousarray(w.reshape(K // (tiles * P), tiles, P, N // P, P).transpose(3, 0, 2, 1, 4)
                                ).reshape(-1, P, tiles * P)


def _cols(v):
    return v.reshape(-1, P).T


def _rows16(v):
    out = np.zeros((P, 1), v.dtype)
    out[:HEADS, 0] = v
    return out


def _lay_out(i):
    w = i["ev_w_in"][0]
    at = np.cumsum([0, INNER, XBC * P, HEADS, 1024, P, P])
    z, xbc, dt, q, k, v = (w[:, a:c] for a, c in zip(at[:-1], at[1:]))
    dt = np.pad(dt, ((0, 0), (0, P - HEADS)))
    kk = [k[:, :64], k[:, :64], k[:, 64:], k[:, 64:]]
    m = {"ev_in": _units(np.concatenate([z, xbc, q, *kk, v, dt], 1)), "ev_out": _units(i["ev_w_out"][0])}
    w = i["od_w_in"][0]
    I = HEADS * P
    q, k, v, o = (w[:, a * I:(a + 1) * I].reshape(D, HEADS, P) for a in range(4))
    g = np.zeros((D, P), w.dtype)
    g[:, 0:HEADS] = w[:, 4 * I:4 * I + HEADS]
    g[:, 32:32 + HEADS] = w[:, 4 * I + HEADS:]
    m["od_in"] = _units(np.concatenate([g, np.stack([k, q, v, o], 2).reshape(D, 4 * I)], 1))
    w = i["od_w_out"][0]
    m["od_out"] = np.concatenate([_units(np.roll(x.reshape(8, P, D), 1, 0).reshape(1024, D))
                                  for x in (w[:1024], w[1024:])], 0)
    for n in range(2):
        m[f"wq{n}"] = _units(i["pk_w_q"][n].reshape(D, -1))
        s = np.stack([i["pk_sub_k1"][n], i["pk_sub_k2"][n]], 1)
        m[f"sub{n}"] = s.reshape(16, KEYS, P).transpose(2, 0, 1)
        m[f"u{n}"] = _units(i["pk_u"][n].T)
        m[f"v{n}"] = i["pk_v"][n].reshape(NBLOCK, BLOCK, KEYS, DK, P).transpose(0, 3, 2, 1, 4).reshape(-1, P, UNIT)
        m[f"gate{n}"] = _units(i["ple_gate"][n])
        m[f"plew{n}"] = i["ple_w"][n].reshape(2, P, 2, 4, P).transpose(2, 1, 3, 0, 4).reshape(2, P, UNIT)
        m[f"emb{n}"] = i["p"][n, 0].T.reshape(2, P, T).transpose(1, 0, 2)
    m["x"] = i["x"][0].T.reshape(DK, P, T).transpose(1, 0, 2)
    taps = lambda w: w.reshape(CONV, -1, P).transpose(2, 1, 0).reshape(P, -1)
    m["par"] = np.concatenate(
        [_cols(i[n][l]) for n in ("norm_mix", "norm_ffn", "norm_ple") for l in range(2)]
        + [_cols(i["norm_final"]), _cols(i["ev_out_norm"][0]), _cols(np.repeat(i["ev_d_skip"][0], 64)),
           taps(i["ev_conv_w"][0]), _cols(i["ev_conv_b"][0]), 
           np.repeat(i["ev_sinks"].reshape(2, 4, 2).transpose(0, 2, 1).reshape(1, -1), P, 0),
           taps(i["od_conv_w"][0]), _cols(i["od_conv_b"][0]), _cols(i["od_head_norm"][0]),
           _rows16(i["ev_dt_bias"][0]), _rows16(i["ev_a_log"][0]), _rows16(i["od_i_bias"][0]),
           _rows16(i["od_f_bias"][0])], 1)
    return {k: np.ascontiguousarray(a) for k, a in m.items()}


def build(nc, shapes):
    dram = {n: nc.dram_tensor(f"in_{n}", s, F32, kind="ExternalInput").ap() for n, s in shapes.items()}
    dram["emb"] = [dram["emb0"], dram["emb1"]]
    dram["out"] = nc.dram_tensor("out_0", [P, DK, T], F32, kind="ExternalOutput").ap()
    dram["gates"] = nc.dram_tensor("gates", [NTG + 2, P, KEYS * TG], F32, kind="Internal").ap()
    dram["acts"] = nc.dram_tensor("acts", [KEYS, P, T], F32, kind="Internal").ap()
    trunk(nc, dram)


def kernel(**inputs):
    import concourse.bacc as bacc
    from concourse.bass_utils import run_bass_kernel_spmd

    arrays = _lay_out({k: np.asarray(v) for k, v in inputs.items()})
    nc = bacc.Bacc("TRN2", target_bir_lowering=False, num_devices=1)
    build(nc, {n: list(a.shape) for n, a in arrays.items()})
    r = run_bass_kernel_spmd(nc, [{f"in_{n}": a for n, a in arrays.items()}], core_ids=[0])
    return r.results[0]["out_0"].transpose(2, 1, 0).reshape(1, T, D)
```

```python
from contextlib import ExitStack

import concourse.bass as bass
import numpy as np
from concourse import mybir

F32 = mybir.dt.float32
F32R = mybir.dt.float32r
U32 = mybir.dt.uint32
ALU = mybir.AluOpType
ACT = mybir.ActivationFunctionType
AX_X = mybir.AxisListType.X

P = 128
T = 512
TT = T // P
D = 1024
DK = D // P
UNIT = DK * P
EPS = 1e-6
RAW = 4
SPL = 2
INNER = 1024
XBC = 12
CONV = 4
HEADS = 16
SEL = 16
PEER_HEADS = 8
KEYS = 128
BLOCK = 8
NBLOCK = KEYS // BLOCK
TG = 32
NTG = T // TG
NEG = -1e30

COLS = {}
_at = 0
for _name, _n in (("norm_mix0", 8), ("norm_mix1", 8), ("norm_ffn0", 8), ("norm_ffn1", 8),
                  ("norm_ple0", 8), ("norm_ple1", 8), ("norm_final", 8), ("out_norm", 8),
                  ("d_skip", 8), ("conv_w", 4 * XBC), ("conv_b", XBC), ("sinks", HEADS),
                  ("od_conv_w", 4 * 32), ("od_conv_b", 32), ("head_norm", HEADS),
                  ("dt_bias", 1), ("a_log", 1), ("i_bias", 1), ("f_bias", 1)):
    COLS[_name] = _at
    _at += _n
NPAR = _at


class Signal:

    def __init__(self, nc, ctx, name):
        self.sem = ctx.enter_context(nc.semaphore(name))
        self.base = 0

    def at(self, k):
        return self.base + k


class Chain:

    def __init__(self, eng, signal):
        self.eng, self.counter, self.n, self.off = eng, signal, 0, 0

    def __call__(self, ins):
        self.n += 1
        ins.then_inc(self.counter.sem, 1)
        self.eng.wait_ge(self.counter.sem, self.off + self.counter.base + self.n)

    def enter(self, i, per):
        self.off, self.start, self.per = i * per, self.n, per

    def leave(self, count):
        assert self.n - self.start == self.per, (self.n - self.start, self.per)
        self.n += self.per * (count - 1)
        self.off = 0

    def done(self):
        self.counter.base += self.n


class Program:
    def __init__(self, nc, ctx, dram):
        self.nc, self.ctx, self.dram = nc, ctx, dram
        self.unit = RAW
        self.out = 2
        self.sems = {}
        self.names = {}
        sb = self.sb
        self.x = sb("residual", [P, DK, T])
        self.hh = sb("h_hi", [P, DK, T], F32R)
        self.hl = sb("h_lo", [P, DK, T], F32R)
        self.yh = sb("y_hi", [P, DK, T], F32R)
        self.yl = sb("y_lo", [P, DK, T], F32R)
        self.raw = sb("w_raw", [P, RAW, UNIT])
        self.wh = sb("w_hi", [P, SPL, UNIT], F32R)
        self.wl = sb("w_lo", [P, SPL, UNIT], F32R)
        self.par = sb("params", [P, NPAR])
        self.ones = sb("ones", [P, P])
        self.ident = sb("ident", [P, P])
        self.incl = sb("incl", [P, T])
        self.after = sb("after", [P, P])
        self.iota = sb("iota", [P, P])
        self.ps = ctx.enter_context(nc.psum_tensor("ps", [P, 8, 512], F32))

    def sb(self, name, shape, dt=F32, ctx=None):
        n = self.names[name] = self.names.get(name, 0) + 1
        name = name if n == 1 else f"{name}_{n}"
        return (ctx or self.ctx).enter_context(self.nc.sbuf_tensor(name, shape, dt))

    def sig(self, name):
        if name not in self.sems:
            self.sems[name] = Signal(self.nc, self.ctx, name)
        return self.sems[name]

    def col(self, name, k=0, rows=P):
        c = COLS[name] + k
        return self.par[0:rows, c:c + 1]

    def load(self, sp, u, slot, src):
        hi, lo, loaded = self.sig("w_hi_ready"), self.sig("w_lo_ready"), self.sig(f"w_loaded{slot}")
        sp.wait_ge(hi.sem, u - RAW + 1)
        sp.wait_ge(lo.sem, u - RAW + 1)
        sp.dma_start(self.raw[:, slot, :], src).then_inc(loaded.sem, 16)

    def split_hi(self, act, u, slot, loads):
        act.wait_ge(self.sig(f"w_loaded{slot}").sem, 16 * loads)
        act.wait_ge(self.sig("w_used").sem, u - SPL + 1)
        self.nc.scalar.activation(self.wh[:, slot % SPL, :], self.raw[:, slot, :],
                                  ACT.Copy).then_inc(self.sig("w_hi_ready").sem, 1)

    def split_lo(self, dve, u, slot):
        dve.wait_ge(self.sig("w_hi_ready").sem, u + 1)
        self.nc.vector.tensor_tensor(self.wl[:, slot % SPL, :], self.raw[:, slot, :],
                                     self.wh[:, slot % SPL, :].bitcast(F32),
                                     ALU.subtract).then_inc(self.sig("w_lo_ready").sem, 1)

    def product(self, pe, u, slot, out, rh, rl, first=True, last=True, tiles=range(DK), wait_tile=None):
        pe.wait_ge(self.sig("w_lo_ready").sem, u + 1)
        s = slot % SPL
        n = len(tiles)
        for j, k in enumerate(tiles):
            if wait_tile is not None:
                wait_tile(k)
            w = slice(j * P, (j + 1) * P)
            for m, (a, b) in enumerate(((self.wh, rh), (self.wh, rl), (self.wl, rh))):
                ins = self.nc.tensor.matmul(out, a[:, s, w], b[:, k, :], start=first and j == 0 and m == 0,
                                            stop=last and j == n - 1 and m == 2)
        return ins


def prefetch(p, sp, srcs):
    for j, s in enumerate(srcs):
        u = p.unit + j
        p.load(sp, u, u % RAW, s)


def start(p, nxt):
    nc = p.nc
    ld, const = p.sig("inputs_loaded"), p.sig("const_ready")
    with nc.Block() as block:
        @block.sync
        def _(sp):
            for j in range(RAW):
                sp.sem_inc(p.sig(f"w_loaded{j}").sem, 16)
            sp.dma_start(p.x[:, :, :], p.dram["x"]).then_inc(ld.sem, 16)
            sp.dma_start(p.par[:, :], p.dram["par"]).then_inc(ld.sem, 16)
            prefetch(p, sp, nxt)
            sp.wait_ge(ld.sem, 32)

        @block.scalar
        def _(act):
            act.sem_inc(p.sig("w_hi_ready").sem, RAW)
            p.split_hi(act, RAW, 0, 2)

        @block.tensor
        def _(pe):
            pe.sem_inc(p.sig("w_used").sem, RAW)

        @block.vector
        def _(dve):
            dve.sem_inc(p.sig("w_lo_ready").sem, RAW)
            dve.sem_inc(p.sig("out_taken").sem, 2)
            p.split_lo(dve, RAW, 0)

        @block.gpsimd
        def _(pool):
            nc.gpsimd.memset(p.ones[:, :], 1.0)
            nc.gpsimd.memset(p.incl[:, :], 1.0)
            nc.gpsimd.memset(p.after[:, :], 1.0)
            nc.gpsimd.iota(p.iota[:, :], pattern=[[1, P]], base=0, channel_multiplier=0,
                           allow_small_or_imprecise_dtypes=True)
            nc.gpsimd.memset(p.ident[:, :], 0.0).then_inc(const.sem, 1)
            pool.wait_ge(const.sem, 1)
            nc.gpsimd.affine_select(out=p.ident[:, :], in_=p.ident[:, :], compare_op=ALU.not_equal,
                                    fill=1.0, base=0, pattern=[[-1, P]], channel_multiplier=1)
            nc.gpsimd.affine_select(out=p.incl[:, :], in_=p.incl[:, :], compare_op=ALU.is_ge,
                                    fill=0.0, base=0, pattern=[[1, T]], channel_multiplier=-1)
            nc.gpsimd.affine_select(out=p.after[:, :], in_=p.after[:, :], compare_op=ALU.is_ge,
                                    fill=0.0, base=-1, pattern=[[-1, P]], channel_multiplier=1)
    const.base += 1
    ld.base += 32


def norm(p, src, gain, out=None, dst=None, nxt=(), beside=None):
    nc = p.nc
    sq, ssum, root, scaled, hi_done = (p.sig(n) for n in ("squared", "sumsq", "root", "scaled", "norm_hi"))
    chain = p.sig("dve_chain")
    with ExitStack() as ctx:
        s2 = p.sb("squares", [P, 2, T], ctx=ctx)
        rstd = p.sb("rstd", [P, T], ctx=ctx)
        hf = p.sb("normed", [P, 2, T], ctx=ctx)
        block = ctx.enter_context(nc.Block())

        @block.sync
        def _(sp):
            if beside:
                beside.sync(sp)
            prefetch(p, sp, nxt)

        @block.scalar
        def _(act):
            for k in range(DK):
                if k >= 2:
                    act.wait_ge(ssum.sem, ssum.at(k - 1))
                nc.scalar.activation(s2[:, k % 2, :], src[:, k, :], ACT.Square).then_inc(sq.sem, 1)
            if beside:
                beside.act_first(act)
            act.wait_ge(ssum.sem, ssum.at(DK))
            nc.scalar.activation(rstd[:, :], p.ps[:, 7, :], ACT.Copy, scale=1.0 / (DK * P),
                                 bias=EPS).then_inc(root.sem, 1)
            act.wait_ge(root.sem, root.at(1))
            nc.scalar.activation(rstd[:, :], rstd[:, :], ACT.Sqrt).then_inc(root.sem, 1)
            if beside:
                beside.act_second(act)
            if out is not None:
                for k in range(DK):
                    act.wait_ge(scaled.sem, scaled.at(k + 1))
                    nc.scalar.activation(out[0][:, k, :], hf[:, k % 2, :], ACT.Copy).then_inc(hi_done.sem, 1)
                    if beside:
                        beside.act_tile(act, k)

        @block.tensor
        def _(pe):
            for k in range(DK):
                pe.wait_ge(sq.sem, sq.at(k + 1))
                nc.tensor.matmul(p.ps[:, 7, :], p.ones[:, :], s2[:, k % 2, :], start=(k == 0),
                                 stop=(k == DK - 1)).then_inc(ssum.sem, 1)
            if beside:
                beside.tensor(pe, root)

        @block.vector
        def _(dve):
            link = Chain(dve, chain)
            if beside:
                beside.vector_first(dve)
            dve.wait_ge(root.sem, root.at(2))
            link(nc.vector.reciprocal(rstd[:, :], rstd[:, :]))
            for k in range(DK + 1):
                if k < DK:
                    o = hf[:, k % 2, :] if out is not None else dst[:, k, :]
                    if out is not None and k >= 2:
                        dve.wait_ge(hi_done.sem, hi_done.at(k - 1))
                    nc.vector.scalar_tensor_tensor(out=o, in0=src[:, k, :], scalar=p.col(gain, k),
                                                   in1=rstd[:, :], op0=ALU.mult,
                                                   op1=ALU.mult).then_inc(scaled.sem, 1)
                if k and out is not None:
                    dve.wait_ge(hi_done.sem, hi_done.at(k))
                    link(nc.vector.tensor_tensor(out[1][:, k - 1, :], hf[:, (k - 1) % 2, :],
                                                 out[0][:, k - 1, :].bitcast(F32), ALU.subtract))
            link.done()
            if beside:
                beside.vector_last(dve)
    sq.base += DK
    ssum.base += DK
    root.base += 2
    scaled.base += DK
    if out is not None:
        hi_done.base += DK


def steps_of(p, jobs):
    u, o = p.unit, p.out
    for job in jobs:
        n, per = job[1], job[2]
        each = min(n, RAW)
        assert n % each == 0 and each % per == 0 and (each // per) % 2 == 0 and o % 2 == 0
        yield u, o, n // each, each, job
        u += n
        o += n // per


def looped(eng, p, jobs, body, skip=0):
    for u, o, count, each, job in steps_of(p, jobs):
        lo, skip = skip, 0
        if count - lo <= 0:
            continue
        if count - lo == 1:
            body(u + each * lo, o + each // job[2] * lo, lo, each, job, u)
        else:
            with eng.Fori(lo, count) as i:
                body(i * each + u, i * (each // job[2]) + o, i, each, job, u)


def linear(p, jobs, nxt):
    nc = p.nc
    used, taken, seen = p.sig("w_used"), p.sig("out_taken"), p.sig("out_seen")
    total = sum(j[1] for j in jobs)
    with nc.Block() as block:
        @block.sync
        def _(sp):
            def body(u, o, i, each, job, at):
                for j in range(each):
                    p.load(sp, u + j, (at + j) % RAW, job[0][i * each + j, :, :])
            assert min(jobs[0][1], RAW) == RAW
            looped(sp, p, jobs, body, skip=1)
            p.unit += total
            prefetch(p, sp, nxt)
            p.unit -= total

        @block.scalar
        def _(act):
            def body(u, o, i, each, job, at):
                for j in range(1, each + 1):
                    loads = (at + j) // RAW + 1
                    if each == RAW:
                        loads = i + loads
                    p.split_hi(act, u + j, (at + j) % RAW, loads)
                    if job[5:]:
                        act.wait_ge(used.sem, u + j)
                        job[5](i * each + j - 1, p.ps[:, (j - 1) % 2, :]).then_inc(seen.sem, 1)
            looped(act, p, jobs, body)

        @block.vector
        def _(dve):
            def body(u, o, i, each, job, at):
                per = job[2]
                for j in range(each):
                    p.split_lo(dve, u + j + 1, (at + j + 1) % RAW)
                    if j % per == per - 1:
                        q = j // per
                        if job[5:]:
                            dve.wait_ge(seen.sem, i * each + seen.base + j + 1)
                        else:
                            dve.wait_ge(used.sem, u + j + 1)
                        job[4](i * (each // per) + q, p.ps[:, q % 2, :]).then_inc(taken.sem, 1)
            looped(dve, p, jobs, body)

        @block.tensor
        def _(pe):
            def body(u, o, i, each, job, at):
                per = job[2]
                for j in range(each):
                    q = j // per
                    if j % per == 0:
                        pe.wait_ge(taken.sem, o + q - 1)
                    rh, rl = job[3][j % per]
                    p.product(pe, u + j, (at + j) % RAW, p.ps[:, q % 2, :], rh, rl,
                              first=j % per == 0, last=j % per == per - 1).then_inc(used.sem, 1)
            looped(pe, p, jobs, body)
    seen.base += sum(j[1] for j in jobs if j[5:])
    p.unit += total
    p.out += sum(j[1] // j[2] for j in jobs)


def even_in(p, b, nxt):
    nc = p.nc
    with nc.Block() as block:
        @block.gpsimd
        def _(pool):
            nc.gpsimd.memset(b["xbc"][:, :, 0:CONV - 1], 0.0)
            nc.gpsimd.memset(b["kd"][:, :, :], 0.0)
            nc.gpsimd.memset(b["vt"][:, :], 0.0)
    h = [(p.hh, p.hl)]
    w = p.dram["ev_in"]
    v = nc.vector

    def tail(i, psum):
        if i < 2:
            return v.tensor_copy(b["kd"][:, i, 64:64 + T], psum)
        if i == 2:
            return v.tensor_copy(b["vt"][:, 64:64 + T], psum)
        return v.tensor_copy(b["dtraw"][:, :], psum[0:HEADS, :])

    linear(p, [(w, 8, 1, h, lambda i, ps: v.tensor_copy(b["z"][:, i, :], ps)),
               (w[8:20], XBC, 1, h, lambda i, ps: v.tensor_copy(b["xbc"][:, i, CONV - 1:], ps)),
               (w[20:28], 8, 1, h, lambda i, ps: v.tensor_copy(b["q"][:, i, :], ps)),
               (w[28:32], 4, 1, h, tail)], nxt)


def conv_steps(nc, link, src, dst, taps, bias):
    v = nc.vector
    link(v.tensor_scalar(dst[0], src[:, 0:T], taps[0], bias, ALU.mult, ALU.add))
    for k in range(1, CONV):
        ins = v.scalar_tensor_tensor(out=dst[k], in0=src[:, k:k + T], scalar=taps[k], in1=dst[k - 1],
                                     op0=ALU.mult, op1=ALU.add)
        if k < CONV - 1:
            link(ins)
    return ins


def log1p_rows(v, link, rows, small, src, bias, xb, ab, e1, ln, rc):
    dve = link.eng
    link(v.tensor_scalar(xb[:, :], src, bias, None, ALU.add))
    v.scalar_tensor_tensor(out=ab[:, :], in0=xb[:, :], scalar=-1.0, in1=xb[:, :], op0=ALU.mult,
                           op1=ALU.max).then_inc(rows.sem, 1)
    dve.wait_ge(small.sem, small.at(1))
    v.tensor_scalar(ab[:, :], e1[:, :], 1.0, None, ALU.add).then_inc(rows.sem, 1)
    dve.wait_ge(rows.sem, rows.at(2))
    link(v.reciprocal(rc[:, :], ab[:, :]))
    dve.wait_ge(small.sem, small.at(2))
    link(v.tensor_scalar(ab[:, :], ab[:, :], -1.0, None, ALU.add))
    link(v.tensor_tensor(ab[:, :], e1[:, :], ab[:, :], ALU.subtract))
    link(v.tensor_tensor(ab[:, :], ab[:, :], rc[:, :], ALU.mult))
    link(v.tensor_tensor(ln[:, :], ln[:, :], ab[:, :], ALU.add))


def log1p_act(act, nc, rows, small, e1, ab, ln):
    act.wait_ge(rows.sem, rows.at(1))
    nc.scalar.activation(e1[:, :], ab[:, :], ACT.Exp, scale=-1.0).then_inc(small.sem, 1)
    act.wait_ge(rows.sem, rows.at(2))
    nc.scalar.activation(ln[:, :], ab[:, :], ACT.Ln).then_inc(small.sem, 1)


def even_attention(p, b):
    nc = p.nc
    names = ("att_scores", "att_shifted", "att_exp", "att_probs", "att_turned", "att_copied", "att_out",
             "att_hi", "att_lo", "att_v", "att_masks", "att_v_taken")
    sc, sh, se, pr, st, sy, so, shi, slo, sv, sma, svt = (p.sig(n) for n in names)
    SC = 64 ** -0.5
    H = 4
    E = TT * HEADS // H
    with ExitStack() as ctx:
        vp = b["vt"][:, :].rearrange("p (m t) -> p m t", t=P)
        mask = p.sb("att_mask", [P, 2, 192], ctx=ctx)
        S = p.sb("scores", [P, 2, H, 192], ctx=ctx)
        mx = p.sb("att_max", [P, 2, H], ctx=ctx)
        nm = p.sb("att_max_negated", [P, 2, H], ctx=ctx)
        es = p.sb("att_sink_exp", [P, 2, H], ctx=ctx)
        sm = p.sb("att_sum", [P, 2, H], ctx=ctx)
        pt = p.sb("probs_turned", [P, 2, 2, H * P], ctx=ctx)
        tmp = p.sb("conv_sums", [P, 2, T], ctx=ctx)
        block = ctx.enter_context(nc.Block())

        def unit(e):
            return e // 4, e % 4 // 2, e % 4 * H, e % 2

        @block.gpsimd
        def _(pool):
            g = nc.gpsimd
            g.memset(mask[:, :, :], 0.0).then_inc(sma.sem, 1)
            pool.wait_ge(sma.sem, sma.at(1))
            g.memset(mask[64:P, :, 0:64], NEG)
            g.memset(mask[0:64, :, 128:192], NEG).then_inc(sma.sem, 1)
            pool.wait_ge(sma.sem, sma.at(2))
            g.memset(mask[:, 0, 0:64], NEG).then_inc(sma.sem, 1)

        @block.tensor
        def _(pe):
            t = nc.tensor
            for m in range(5):
                ins = t.transpose(p.ps[:, m // 4, (m % 4) * P:(m % 4 + 1) * P],
                                  b["vt"][:, m * P:(m + 1) * P], p.ident[:, :])
            ins.then_inc(sv.sem, 1)
            pe.wait_ge(svt.sem, svt.at(2))
            for e in range(-2, E + 1):
                if e + 2 < E:
                    j, g, first, s = unit(e + 2)
                    if e >= 0:
                        pe.wait_ge(sh.sem, sh.at(e + 1))
                    for h in range(H):
                        hd = first + 2 * (h % 2) + h // 2
                        rows = slice(64 * (hd % 2), 64 * (hd % 2) + 64)
                        ins = t.matmul(p.ps[:, 2 * s + h // 2, (h % 2) * 256:(h % 2) * 256 + 192],
                                       b["q"][rows, hd // 2, j * P:(j + 1) * P],
                                       b["kd"][rows, g, j * P:j * P + 192], start=True, stop=True)
                    ins.then_inc(sc.sem, 1)
                if 0 <= e < E:
                    j, g, first, s = unit(e)
                    if e >= 2:
                        pe.wait_ge(slo.sem, slo.at(e - 1))
                    pe.wait_ge(pr.sem, pr.at(e + 1))
                    for h in range(H):
                        t.transpose(p.ps[:, 4 + 2 * s, h * P:(h + 1) * P], S[:, s, h, 0:P], p.ident[:, :])
                        ins = t.transpose(p.ps[0:64, 5 + 2 * s, h * P:(h + 1) * P], S[:, s, h, P:192],
                                          p.ident[:, :])
                    ins.then_inc(st.sem, 1)
                if e >= 1:
                    j, g, first, s = unit(e - 1)
                    pe.wait_ge(sy.sem, sy.at(e))
                    c = slice(64 * g, 64 * g + 64)
                    for h in range(H):
                        o = p.ps[64 * (h // 2):64 * (h // 2) + 64, 4 + 2 * s, (h % 2) * P:(h % 2 + 1) * P]
                        t.matmul(o, vp[:, j, c], pt[:, s, 0, h * P:(h + 1) * P], start=True, stop=False)
                        ins = t.matmul(o, vp[0:64, j + 1, c], pt[0:64, s, 1, h * P:(h + 1) * P],
                                       start=False, stop=True)
                    ins.then_inc(so.sem, 1)

        @block.scalar
        def _(act):
            a = nc.scalar
            for e in range(-1, E + 1):
                if e + 1 < E:
                    s = unit(e + 1)[3]
                    act.wait_ge(sh.sem, sh.at(e + 2))
                    a.activation(es[:, s, :], es[:, s, :], ACT.Exp)
                    for h in range(H):
                        ins = a.activation(S[:, s, h, :], S[:, s, h, :], ACT.Exp, bias=nm[:, s, h:h + 1],
                                           accum_out=sm[:, s, h:h + 1])
                    ins.then_inc(se.sem, 1)
                if 0 <= e < E:
                    s = unit(e)[3]
                    act.wait_ge(st.sem, st.at(e + 1))
                    if e >= 2:
                        act.wait_ge(so.sem, so.at(e - 1))
                    a.activation(pt[:, s, 0, :], p.ps[:, 4 + 2 * s, :], ACT.Copy)
                    a.activation(pt[0:64, s, 1, :], p.ps[0:64, 5 + 2 * s, :], ACT.Copy).then_inc(sy.sem, 1)
                if e >= 1:
                    j, g, first, s = unit(e - 1)
                    act.wait_ge(so.sem, so.at(e))
                    a.activation(p.yh[:, first // 2:first // 2 + 2, j * P:(j + 1) * P],
                                 p.ps[:, 4 + 2 * s, 0:2 * P].rearrange("p (h t) -> p h t", h=2),
                                 ACT.Copy).then_inc(shi.sem, 1)

        @block.vector
        def _(dve):
            v = nc.vector
            link = Chain(dve, p.sig("dve_chain"))
            dve.wait_ge(sma.sem, sma.at(3))
            dve.wait_ge(sv.sem, sv.at(1))
            v.tensor_copy(vp[:, 0:4, :], p.ps[:, 0, :].rearrange("p (m t) -> p m t", m=4)).then_inc(svt.sem, 1)
            v.tensor_copy(vp[:, 4, :], p.ps[:, 1, 0:P]).then_inc(svt.sem, 1)
            dve.wait_ge(svt.sem, svt.at(2))
            for e in range(-1, E + 1):
                if e + 1 < E:
                    j, g, first, s = unit(e + 1)
                    sink = p.par[:, COLS["sinks"] + first:COLS["sinks"] + first + H]
                    dve.wait_ge(sc.sem, sc.at(e + 2))
                    if e + 1 >= 2:
                        dve.wait_ge(st.sem, st.at(e))
                    raw = p.ps[:, 2 * s:2 * s + 2, :].rearrange("p b (h m) -> p (b h) m", h=2)[:, :, 0:192]
                    m = mask[:, min(j, 1), :].unsqueeze(1).to_broadcast([P, H, 192])
                    link(v.scalar_tensor_tensor(out=S[:, s, :, :], in0=raw, scalar=SC, in1=m, op0=ALU.mult,
                                                op1=ALU.add))
                    link(v.tensor_reduce(mx[:, s, :], S[:, s, :, :], AX_X, ALU.max))
                    link(v.tensor_tensor(mx[:, s, :], mx[:, s, :], sink, ALU.max))
                    v.tensor_scalar(nm[:, s, :], mx[:, s, :], -1.0, None, ALU.mult)
                    v.tensor_tensor(es[:, s, :], sink, mx[:, s, :], ALU.subtract).then_inc(sh.sem, 1)
                if 0 <= e < E:
                    s = unit(e)[3]
                    dve.wait_ge(se.sem, se.at(e + 1))
                    link(v.tensor_tensor(sm[:, s, :], sm[:, s, :], es[:, s, :], ALU.add))
                    link(v.reciprocal(sm[:, s, :], sm[:, s, :]))
                    v.tensor_tensor(S[:, s, :, :], S[:, s, :, :],
                                    sm[:, s, :].unsqueeze(2).to_broadcast([P, H, 192]),
                                    ALU.mult).then_inc(pr.sem, 1)
                if 0 <= e < XBC:
                    link(conv_steps(nc, link, b["xbc"][:, e, :],
                                    (tmp[:, 0, :], tmp[:, 1, :], tmp[:, 0, :], b["xbc"][:, e, CONV - 1:]),
                                    [p.col("conv_w", e * CONV + k) for k in range(CONV)], p.col("conv_b", e)))
                if e >= 1:
                    j, g, first, s = unit(e - 1)
                    dve.wait_ge(shi.sem, shi.at(e))
                    y = slice(first // 2, first // 2 + 2)
                    v.tensor_tensor(p.yl[:, y, j * P:(j + 1) * P],
                                    p.ps[:, 4 + 2 * s, 0:2 * P].rearrange("p (h t) -> p h t", h=2),
                                    p.yh[:, y, j * P:(j + 1) * P].bitcast(F32), ALU.subtract
                                    ).then_inc(slo.sem, 1)
            link.done()
    for s in (sc, sh, se, pr, st, sy, so, shi, slo):
        s.base += E
    sv.base += 1
    svt.base += 2
    sma.base += 3


def even_dt(p, b):
    nc = p.nc
    small, rows = (p.sig(n) for n in ("act_small", "rows_ready"))
    H = HEADS
    with ExitStack() as ctx:
        xb = p.sb("dt_biased", [H, T], ctx=ctx)
        ab = p.sb("dt_abs", [H, T], ctx=ctx)
        e1 = p.sb("dt_exp", [H, T], ctx=ctx)
        ln = p.sb("dt_log", [H, T], ctx=ctx)
        rc = p.sb("dt_recip", [H, T], ctx=ctx)
        na = p.sb("a_neg", [H, 1], ctx=ctx)
        block = ctx.enter_context(nc.Block())

        @block.vector
        def _(dve):
            v = nc.vector
            link = Chain(dve, p.sig("dve_chain"))
            log1p_rows(v, link, rows, small, b["dtraw"][:, :], p.col("dt_bias", 0, H), xb, ab, e1, ln, rc)
            link(v.tensor_scalar(xb[:, :], xb[:, :], 0.0, None, ALU.max))
            link(v.tensor_tensor(b["dt"][:, :], xb[:, :], ln[:, :], ALU.add))
            dve.wait_ge(small.sem, small.at(3))
            link(v.tensor_scalar(na[:, :], na[:, :], -1.0, None, ALU.mult))
            link(v.tensor_scalar(b["adt"][:, :], b["dt"][:, :], na[:, 0:1], None, ALU.mult))
            link.done()

        @block.scalar
        def _(act):
            log1p_act(act, nc, rows, small, e1, ab, ln)
            nc.scalar.activation(na[:, :], p.col("a_log", 0, H), ACT.Exp).then_inc(small.sem, 1)
            for c in range(0, XBC, 4):
                x = b["xbc"][:, c:c + 4, CONV - 1:]
                nc.scalar.activation(x, x, ACT.Silu)
            nc.scalar.activation(b["z"][:, :, :], b["z"][:, :, :], ACT.Silu)
    small.base += 3
    rows.base += 2


def even_ssd(p, b):
    nc = p.nc
    names = ("ssd_turned", "ssd_cols", "ssd_cb", "ssd_cb_done", "ssd_x", "ssd_xt", "ssd_xdt", "ssd_factors",
             "ssd_arg", "ssd_exp", "ssd_m", "ssd_m_used", "ssd_decays")
    (tn, co, cb, cbd, sx, sxt, sxd, fa, ar, ex, sm, mf, dc) = (p.sig(n) for n in names)
    dchain = p.sig("dve_chain")
    H = HEADS
    R = 4
    with ExitStack() as ctx:
        cbm = b["q"]
        cols = p.sb("dt_cols", [P, 2, TT, H + 2], ctx=ctx)
        ac = p.sb("decay_cols", [P, TT, 2], ctx=ctx)
        xs = p.sb("x_pair", [P, T], ctx=ctx)
        xd = p.sb("x_dt", [P, TT, P], ctx=ctx)
        fa1 = p.sb("decays_after", [P, 2, TT, P], ctx=ctx)
        fb1 = p.sb("decays_all", [P, 2, TT, P], ctx=ctx)
        E = p.sb("decay_exp", [P, R, T], ctx=ctx)
        M = p.sb("ssd_weights", [P, R, T], ctx=ctx)
        yt = xs
        block = ctx.enter_context(nc.Block())

        def width(i):
            return T - i * P

        @block.tensor
        def _(pe):
            t = nc.tensor
            for k in range(2):
                for j in range(TT):
                    ins = t.transpose(p.ps[:, 6, (k * TT + j) * H:(k * TT + j + 1) * H],
                                      b[("adt", "dt")[k]][:, j * P:(j + 1) * P], p.ident[0:H, 0:H])
            ins.then_inc(tn.sem, 1)
            for g in range(2):
                if g:
                    pe.wait_ge(cbd.sem, cbd.at(4))
                for i in range(TT):
                    ins = t.matmul(p.ps[:, i, 0:width(i)], b["xbc"][:, 8 + g, 3 + i * P:3 + (i + 1) * P],
                                   b["xbc"][:, 10 + g, 3 + i * P:], start=True, stop=True)
                ins.then_inc(cb.sem, 1)
            pe.wait_ge(cbd.sem, cbd.at(8))
            pe.sem_inc(mf.sem, R)
            pe.sem_inc(ar.sem, 8)
            for g in range(2):
                with pe.Fori(0, 4) as cc:
                    c = cc + 4 * g
                    def weigh(n):
                        h, i = divmod(n, TT)
                        pe.wait_ge(sm.sem, c * 8 + sm.base + R + n + 1)
                        if n == 0:
                            pe.wait_ge(sxd.sem, c + sxd.base + 1)
                        o = p.ps[64 * h:64 * h + 64, 5, i * P:T]
                        return t.matmul(o, xd[:, i, 64 * h:64 * h + 64], M[:, n % R, 0:width(i)],
                                        start=i == 0, stop=i == TT - 1, skip_group_check=True)

                    for n in range(8):
                        h, i = divmod(n, TT)
                        if i == 0:
                            pe.wait_ge(fa.sem, c * 2 + fa.base + h + 1)
                        pe.wait_ge(ex.sem, c * 8 + ex.base + n + 1)
                        bank = p.ps[:, n % R, :]
                        for j in range(i, TT):
                            f = fa1 if j == i else fb1
                            ins = t.matmul(bank[:, (j - i) * P:width(i)], f[:, h, j, :], p.incl[:, 0:width(j)],
                                           start=j == i, stop=j == TT - 1, skip_group_check=True)
                        ins.then_inc(ar.sem, 1)
                        if n == R - 2:
                            pe.wait_ge(sx.sem, c + sx.base + 1)
                            for j in range(TT):
                                ins = t.transpose(p.ps[:, 4, j * P:(j + 1) * P], xs[:, j * P:(j + 1) * P],
                                                  p.ident[:, :])
                            ins.then_inc(sxt.sem, 1)
                        if n >= R - 1:
                            weigh(n - R + 1).then_inc(mf.sem, 1)
                    for n in range(9 - R, 8):
                        weigh(n).then_inc(mf.sem, 1)

        @block.scalar
        def _(act):
            a = nc.scalar
            act.sem_inc(ex.sem, R)
            with act.Fori(0, 8) as c:
                for n in range(8):
                    i = n % TT
                    act.wait_ge(ar.sem, c * 8 + ar.base + 8 + n + 1)
                    act.wait_ge(sm.sem, c * 8 + sm.base + n + 1)
                    a.activation(E[:, n % R, 0:width(i)], p.ps[:, n % R, 0:width(i)], ACT.Exp).then_inc(ex.sem, 1)

        @block.gpsimd
        def _(pool):
            g_ = nc.gpsimd
            with pool.Fori(0, 8) as c:
                pool.wait_ge(dc.sem, c + dc.base + 1)
                for h in range(2):
                    pool.wait_ge(ar.sem, c * 8 + ar.base + 4 * h + 4)
                    s = ac[:, :, h:h + 1].to_broadcast([P, TT, P])
                    g_.tensor_tensor(fa1[:, h, :, :], p.after[:, :].unsqueeze(1).to_broadcast([P, TT, P]),
                                     s, ALU.mult)
                    g_.tensor_copy(fb1[:, h, :, :], s).then_inc(fa.sem, 1)

        @block.vector
        def _(dve):
            v = nc.vector
            link = Chain(dve, dchain)
            dve.wait_ge(tn.sem, tn.at(1))
            v.memset(cols[:, :, :, H:], 0.0)
            v.tensor_copy(cols[:, :, :, 0:H],
                          p.ps[:, 6, 0:2 * TT * H].rearrange("p (k j h) -> p k j h", k=2, j=TT)
                          ).then_inc(co.sem, 1)
            for g in range(2):
                dve.wait_ge(cb.sem, cb.at(g + 1))
                for i in range(TT):
                    v.tensor_tensor(cbm[:, g * TT + i, 0:width(i)], p.ps[:, i, 0:width(i)],
                                    p.incl[:, 0:width(i)], ALU.mult).then_inc(cbd.sem, 1)
            dve.wait_ge(cbd.sem, cbd.at(8))
            dve.wait_ge(co.sem, co.at(1))
            v.tensor_copy(ac[:, :, :], cols[:, 0, :, 0:2]).then_inc(dc.sem, 1)
            dve.sem_inc(sm.sem, R)
            for g in range(2):
                with dve.Fori(0, 4) as cc:
                    c = cc + 4 * g
                    link.enter(cc, 2)
                    v.tensor_copy(xs[:, :], b["xbc"][:, c, 3:]).then_inc(sx.sem, 1)
                    dve.wait_ge(sxt.sem, c + sxt.base + 1)
                    for h in range(2):
                        ins = v.tensor_tensor(
                            xd[:, :, 64 * h:64 * h + 64],
                            p.ps[:, 4, :].rearrange("p (j q) -> p j q", j=TT)[:, :, 64 * h:64 * h + 64],
                            cols[:, 1, :, bass.ds(c * 2 + h, 1)].to_broadcast([P, TT, 64]), ALU.mult)
                    ins.then_inc(sxd.sem, 1)
                    for n in range(8):
                        i = n % TT
                        dve.wait_ge(ex.sem, c * 8 + ex.base + R + n + 1)
                        dve.wait_ge(mf.sem, c * 8 + mf.base + n + 1)
                        v.tensor_tensor(M[:, n % R, 0:width(i)], E[:, n % R, 0:width(i)],
                                        cbm[:, g * TT + i, 0:width(i)], ALU.mult).then_inc(sm.sem, 1)
                        if n == 4:
                            v.tensor_copy(ac[:, :, :], cols[:, 0, :, bass.ds(c * 2 + 2, 2)]).then_inc(dc.sem, 1)
                    dve.wait_ge(mf.sem, c * 8 + mf.base + 8 + R)
                    link(v.scalar_tensor_tensor(out=yt[:, :], in0=xs[:, :],
                                                scalar=p.par[:, bass.ds(c + COLS["d_skip"], 1)],
                                                in1=p.ps[:, 5, :], op0=ALU.mult, op1=ALU.add))
                    link(v.tensor_tensor(b["z"][:, c, :], yt[:, :], b["z"][:, c, :], ALU.mult))
                    link.leave(4)
            link.done()
    for s, n in ((tn, 1), (co, 1), (cb, 2), (cbd, 8), (sx, 8), (sxt, 8), (sxd, 8), (fa, 16), (ar, 72),
                 (ex, 64 + R), (sm, 64 + R), (mf, 64 + R), (dc, 9)):
        s.base += n


class Rows:

    def __init__(self, p, acts, ga):
        self.p, self.acts, self.ga = p, acts, ga
        self.ge = p.sig("gelu_ready")
        self.stored = (p.sig("gelu_stored0"), p.sig("gelu_stored1"))

    def open(self, act):
        act.sem_inc(self.ge.sem, 2)
        for s in range(2):
            act.sem_inc(self.stored[s].sem, 16)

    def multiply(self, pe, n, s, u, slot):
        p = self.p
        pe.wait_ge(self.ge.sem, n + self.ge.base + 1)
        p.product(pe, u, slot, p.ps[:, s, :], p.hh, p.hl).then_inc(p.sig("w_used").sem, 1)

    def gelu(self, act, n, m, s, u):
        p = self.p
        act.wait_ge(p.sig("w_used").sem, u + 1)
        act.wait_ge(self.stored[s].sem, m * 16 + self.stored[s].base + 16)
        p.nc.scalar.activation(self.ga[:, s, :], p.ps[:, s, :], ACT.Gelu).then_inc(self.ge.sem, 1)
        act.wait_ge(self.ge.sem, n + self.ge.base + 3)
        act.dma_start(self.row(n), self.ga[:, s, :]).then_inc(self.stored[s].sem, 16)

    def row(self, n):
        return self.acts[n, :, :]

    def close(self, act):
        for s in range(2):
            act.wait_ge(self.stored[s].sem, self.stored[s].at(16 + 16 * KEYS // 2))

    def done(self):
        self.ge.base += KEYS + 2
        for s in range(2):
            self.stored[s].base += 16 + 16 * KEYS // 2


def peer_topk(p, b, rows, wq, us, sub, nxt):
    nc = p.nc
    names = ("q_taken", "scores_ready", "scores_taken", "topk_free")
    qt, sr, stk, tf = (p.sig(n) for n in names)
    used, dchain = p.sig("w_used"), p.sig("dve_chain")
    H = PEER_HEADS
    with ExitStack() as ctx:
        subk = p.sb("sub_keys", [P, 2 * H, KEYS], ctx=ctx)
        qf = p.sb("peer_q", [P, 2, T], ctx=ctx)
        s1 = p.sb("peer_scores", [P, 2, TT * KEYS], ctx=ctx)
        s2 = p.sb("peer_scores_left", [P, TT * KEYS], ctx=ctx)
        V = p.sb("side_top", [P, TT, 2, SEL], ctx=ctx)
        I = p.sb("side_index", [P, TT, 2, SEL], U32, ctx=ctx)
        cs = p.sb("pair_sums", [P, TT, SEL * SEL], ctx=ctx)
        held = p.sb("wait_holder", [P, 8], ctx=ctx)
        tv = p.sb("pair_top", [P, TT, SEL], ctx=ctx)
        ti = p.sb("pair_pos", [P, TT, SEL], U32, ctx=ctx)
        cl = p.sb("pair_sums_left", [P, TT, SEL * SEL], ctx=ctx)
        u0 = p.unit
        N = 4 * H + 4
        block = ctx.enter_context(nc.Block())
        sl = p.sig("sub_loaded")

        @block.sync
        def _(sp):
            sp.dma_start(subk[:, :, :], sub).then_inc(sl.sem, 16)
            with sp.Fori(1, H) as h:
                for j in range(4):
                    p.load(sp, h * 4 + u0 + j, (u0 + j) % RAW, (wq, us)[j % 2][h * 2 + j // 2, :, :])
            for j in range(4):
                p.load(sp, u0 + 4 * H + j, (u0 + j) % RAW, us[2 * H + j, :, :])
            p.unit += N
            prefetch(p, sp, nxt)
            p.unit -= N
            sp.wait_ge(sl.sem, sl.at(16))

        @block.tensor
        def _(pe):
            pe.sem_inc(sr.sem, 2)
            with pe.Fori(0, H) as h:
                for s in range(2):
                    u = h * 4 + u0 + 2 * s
                    pe.wait_ge(qt.sem, h * 2 + qt.base + s + 1)
                    p.product(pe, u, (u0 + 2 * s) % RAW, p.ps[:, 4 + s, :], p.hh, p.hl).then_inc(used.sem, 1)
                    rows.multiply(pe, h * 2 + s, s, u + 1, (u0 + 2 * s + 1) % RAW)
                    pe.wait_ge(qt.sem, h * 2 + qt.base + s + 3)
                    pe.wait_ge(stk.sem, h * 2 + stk.base + s + 1)
                    pe.wait_ge(sl.sem, sl.at(16))
                    for t in range(TT):
                        ins = nc.tensor.matmul(p.ps[:, 2 + s, t * KEYS:(t + 1) * KEYS],
                                               qf[:, s, t * P:(t + 1) * P],
                                               subk[:, bass.ds(h * 2 + s, 1), :].rearrange("p o k -> p (o k)"),
                                               start=True, stop=True)
                    ins.then_inc(sr.sem, 1)
            for j in range(4):
                rows.multiply(pe, 2 * H + j, j % 2, u0 + 4 * H + j, (u0 + j) % RAW)

        @block.scalar
        def _(act):
            rows.open(act)
            act.sem_inc(qt.sem, 2)
            act.sem_inc(stk.sem, 2)
            with act.Fori(0, H) as h:
                for s in range(2):
                    u, at = h * 4 + u0 + 2 * s, u0 + 2 * s
                    p.split_hi(act, u + 1, (at + 1) % RAW, h + (at + 1) // RAW + 1)
                    act.wait_ge(used.sem, u + 1)
                    act.wait_ge(sr.sem, h * 2 + sr.base + s + 1)
                    nc.scalar.activation(qf[:, s, :], p.ps[:, 4 + s, :], ACT.Copy).then_inc(qt.sem, 1)
                    p.split_hi(act, u + 2, (at + 2) % RAW, h + (at + 2) // RAW + 1)
                    rows.gelu(act, h * 2 + s, h, s, u + 1)
                    act.wait_ge(sr.sem, h * 2 + sr.base + s + 3)
                    act.wait_ge(tf.sem, h * 2 + tf.base + s + 1)
                    nc.scalar.activation(s1[:, s, :], p.ps[:, 2 + s, :], ACT.Copy).then_inc(stk.sem, 1)
            for j in range(4):
                u = u0 + 4 * H + j
                p.split_hi(act, u + 1, (u + 1) % RAW, (u + 1) // RAW + 1)
                rows.gelu(act, 2 * H + j, H + j // 2, j % 2, u)

        @block.vector
        def _(dve):
            v = nc.vector
            link = Chain(dve, dchain)
            dve.sem_inc(tf.sem, 2)

            def best8(values, vals, hold):
                v.memset(held[:, hold:hold + 1], 0.0)
                for t in range(TT):
                    ins = v.max(out=vals[t], in_=values[t])
                return ins

            def where8(values, vals, index, hold, left=None):
                v.memset(held[:, hold:hold + 1], 0.0)
                for t in range(TT):
                    ins = v.max_index(out=index[t], in_max=vals[t], in_values=values[t])
                    if left:
                        ins = v.match_replace(out=left[t], in_to_replace=vals[t], in_values=values[t],
                                              imm_value=-3.0e38)
                return ins

            def top_side(s):
                sv = [s1[:, s, t * KEYS:(t + 1) * KEYS] for t in range(TT)]
                lv = [s2[:, t * KEYS:(t + 1) * KEYS] for t in range(TT)]
                vv = [[V[:, t, s, 8 * k:8 * k + 8] for t in range(TT)] for k in range(2)]
                iv = [[I[:, t, s, 8 * k:8 * k + 8] for t in range(TT)] for k in range(2)]
                link(best8(sv, vv[0], 0))
                link(where8(sv, vv[0], iv[0], 1, lv))
                link(best8(lv, vv[1], 2))
                where8(lv, vv[1], iv[1], 3).then_inc(tf.sem, 1)

            def step(h, first=False, last=False):
                csv, clv = [cs[:, t, :] for t in range(TT)], [cl[:, t, :] for t in range(TT)]
                tvv = [[tv[:, t, 8 * k:8 * k + 8] for t in range(TT)] for k in range(2)]
                tiv = [[ti[:, t, 8 * k:8 * k + 8] for t in range(TT)] for k in range(2)]

                def lo(j):
                    p.split_lo(dve, h * 4 + u0 + j + 1, (u0 + j + 1) % RAW)
                lo(0)
                if not first:
                    dve.wait_ge(stk.sem, h * 2 + stk.base + 2)
                    top_side(1)
                lo(1)
                if not first:
                    dve.wait_ge(tf.sem, h * 2 + tf.base + 2)
                    v.tensor_copy(b["side_index"][:, :, :, bass.ds((h - 1) * SEL, SEL)], I[:, :, :, :])
                    for t in range(TT):
                        ins = v.tensor_tensor(cs[:, t, :].rearrange("p (a c) -> p a c", a=SEL),
                                              V[:, t, 0, :].unsqueeze(2).to_broadcast([P, SEL, SEL]),
                                              V[:, t, 1, :].unsqueeze(1).to_broadcast([P, SEL, SEL]), ALU.add)
                    link(ins)
                    link(best8(csv, tvv[0], 4))
                lo(2)
                if not first:
                    link(where8(csv, tvv[0], tiv[0], 5, clv))
                    link(best8(clv, tvv[1], 6))
                    link(where8(clv, tvv[1], tiv[1], 7))
                    v.tensor_copy(b["top"][:, :, bass.ds((h - 1) * SEL, SEL)], tv[:, :, :])
                    link(v.tensor_copy(b["pos"][:, :, bass.ds((h - 1) * SEL, SEL)], ti[:, :, :]))
                lo(3)
                if not last:
                    dve.wait_ge(stk.sem, h * 2 + stk.base + 3)
                    top_side(0)

            step(0, first=True)
            with dve.Fori(1, H) as h:
                link.enter(h - 1, 12)
                step(h)
                link.leave(H - 1)
            step(H, last=True)
            link.done()
    qt.base += 2 * H + 2
    sr.base += 2 * H + 2
    stk.base += 2 * H + 2
    tf.base += 2 * H + 2
    sl.base += 16
    p.unit += N


def peer_decode(p, b, rows, us, n0, nxt):
    nc = p.nc
    names = ("gate_shifted", "gate_exp", "dec_ready", "dec_turned")
    gs, ge, dr, dt = (p.sig(n) for n in names)
    S = PEER_HEADS * SEL
    NS = TT * S
    N, u0 = 12, p.unit
    with ExitStack() as ctx:
        pi = p.sb("pos_half", [P, 2, NS], U32, ctx=ctx)
        pf = p.sb("pos_float", [P, 2, NS], ctx=ctx)
        eq = p.sb("pos_equal", [P, S * SEL], ctx=ctx)
        key = p.sb("keys_found", [P, 3, NS], ctx=ctx)
        gsum = p.sb("gate_sum", [P, TT * PEER_HEADS], ctx=ctx)
        gx = p.sb("gate_terms", [P, NS], ctx=ctx)
        block = ctx.enter_context(nc.Block())

        @block.sync
        def _(sp):
            with sp.Fori(1, N // 4) as i:
                for j in range(4):
                    p.load(sp, i * 4 + u0 + j, (u0 + j) % RAW, us[i * 4 + n0 + j, :, :])
            p.unit += N
            prefetch(p, sp, nxt)
            p.unit -= N

        @block.scalar
        def _(act):
            act.wait_ge(gs.sem, gs.at(1))
            nc.scalar.activation(gx[:, :], gx[:, :], ACT.Exp).then_inc(ge.sem, 1)
            with act.Fori(0, N // 4) as i:
                for j in range(4):
                    u = u0 + j + 1
                    p.split_hi(act, i * 4 + u, u % RAW, i + u // RAW + 1)
                    rows.gelu(act, i * 4 + n0 + j, i * 2 + (n0 + j) // 2, (n0 + j) % 2, i * 4 + u0 + j)

        @block.tensor
        def _(pe):
            with pe.Fori(0, N // 4) as i:
                for j in range(4):
                    rows.multiply(pe, i * 4 + n0 + j, (n0 + j) % 2, i * 4 + u0 + j, (u0 + j) % RAW)
            pe.wait_ge(dr.sem, dr.at(1))
            for k in range(3):
                for t in range(TT):
                    ins = nc.tensor.transpose(p.ps[:, 2 + k, t * P:(t + 1) * P],
                                              key[:, k, t * P:(t + 1) * P], p.ident[:, :])
            ins.then_inc(dt.sem, 1)

        @block.vector
        def _(dve):
            v = nc.vector
            link = Chain(dve, p.sig("dve_chain"))
            los = iter(range(u0 + 1, u0 + N + 1))

            def lo():
                u = next(los, None)
                if u is not None:
                    p.split_lo(dve, u, u % RAW)

            top = b["top"][:, :, :].rearrange("p t (h s) -> p (t h) s", s=SEL)
            g3 = gx[:, :].rearrange("p (g s) -> p g s", s=SEL)
            v.tensor_tensor(g3, top, top[:, :, 0:1].to_broadcast([P, TT * PEER_HEADS, SEL]),
                            ALU.subtract).then_inc(gs.sem, 1)
            lo()
            pos = b["pos"][:, :, :].rearrange("p t s -> p (t s)")
            v.tensor_scalar(pi[:, 0, :], pos, 4, None, ALU.logical_shift_right)
            link(v.tensor_scalar(pi[:, 1, :], pos, 15, None, ALU.bitwise_and))
            link(v.tensor_copy(pf[:, :, :], pi[:, :, :]))
            dve.wait_ge(ge.sem, ge.at(1))
            link(v.tensor_reduce(gsum[:, :], g3, AX_X, ALU.add))
            link(v.reciprocal(gsum[:, :], gsum[:, :]))
            link(v.tensor_tensor(key[:, 2, :].rearrange("p (g s) -> p g s", s=SEL), g3,
                                 gsum[:, :].unsqueeze(2).to_broadcast([P, TT * PEER_HEADS, SEL]), ALU.mult))
            for t in range(TT):
                for k in range(2):
                    e3 = eq[:, :].rearrange("p (s n) -> p s n", n=SEL)
                    want = pf[:, k, t * S:(t + 1) * S].unsqueeze(2).to_broadcast([P, S, SEL])
                    have = p.iota[:, 0:SEL].unsqueeze(1).to_broadcast([P, S, SEL])
                    link(v.tensor_tensor(e3, want, have, ALU.is_equal))
                    lo()
                    e4 = eq[:, :].rearrange("p (h s n) -> p h s n", h=PEER_HEADS, n=SEL)
                    tab = b["side_index"][:, t, k, :].rearrange("p (h n) -> p h n", n=SEL)
                    link(v.tensor_tensor(e4, e4, tab.unsqueeze(2).to_broadcast([P, PEER_HEADS, SEL, SEL]),
                                         ALU.mult))
                    if k:
                        lo()
                    link(v.tensor_reduce(key[:, k, t * S:(t + 1) * S], e3, AX_X, ALU.add))
            dve.sem_inc(dr.sem, 1)
            dve.wait_ge(dt.sem, dt.at(1))
            v.memset(b["sel"][:, :, T:], 0.0)
            link(v.tensor_copy(b["sel"][:, :, 0:T], p.ps[:, 2:5, :]))
            link.done()
            assert next(los, None) is None
    for s in (gs, ge, dr, dt):
        s.base += 1
    p.unit += N


def peer_gates(p, b, rows, us, n0, gates, nxt):
    nc = p.nc
    names = ("hot_first", "hot_second", "gate_summed", "gate_copied", "gate_stored0", "gate_stored1",
             "gate_keys", "gate_zeroed")
    h1, h2, gm, gc, gd0, gd1, gk, gz = (p.sig(n) for n in names)
    gd = (gd0, gd1)
    R = 16
    H0 = 1
    TS = 2 * TG
    Q = TS // 4
    UN = 12
    NS = T // TS
    u0 = p.unit
    assert NS * UN == KEYS - n0

    def fours(k):
        return range(Q * k // (UN - 2), Q * (k + 1) // (UN - 2)) if k < UN - 2 else ()

    with ExitStack() as ctx:
        o1 = p.sb("first_hot", [P, R, KEYS], ctx=ctx)
        o2 = p.sb("second_hot", [P, R, KEYS], ctx=ctx)
        held = p.sb("wait_holder", [P, Q], ctx=ctx)
        kb = p.sb("token_keys", [P, 2, 3, TG], ctx=ctx)
        gb = p.sb("gate_group", [P, 2, KEYS, TG], ctx=ctx)
        sel = b["sel"]
        block = ctx.enter_context(nc.Block())

        @block.vector
        def _(dve):
            v = nc.vector
            v.tensor_copy(kb[:, 0, :, :], sel[:, :, 0:TG]).then_inc(gk.sem, 1)
            with dve.Fori(0, NS) as g:
                for k in range(UN):
                    p.split_lo(dve, g * UN + u0 + k + 1, (u0 + k + 1) % RAW)
                    for q in fours(k):
                        if q == 4:
                            dve.wait_ge(h2.sem, g * TS + h2.base + H0)
                            v.tensor_copy(kb[:, 1, :, :], sel[:, :, bass.ds(g * TS + TG, TG)]
                                          ).then_inc(gk.sem, 1)
                        if q == 12:
                            dve.wait_ge(h2.sem, g * TS + h2.base + TG + H0)
                            v.tensor_copy(kb[:, 0, :, :], sel[:, :, bass.ds(g * TS + TS, TG)]
                                          ).then_inc(gk.sem, 1)
                        if q % 8 == 0:
                            dve.wait_ge(gk.sem, g * 2 + gk.base + q // 8 + 1)
                        dve.wait_ge(gm.sem, g * TS + gm.base + 4 * q + 4)
                        for t in range(4 * q, 4 * q + 4):
                            c = kb[:, t // TG, :, t % TG:t % TG + 1]
                            ins = v.tensor_scalar(o1[:, t % R, :], p.iota[:, :], c[:, 0, :], c[:, 2, :],
                                                  ALU.is_equal, ALU.mult)
                        ins.then_inc(h1.sem, 4)

        @block.gpsimd
        def _(pool):
            pool.sem_inc(h2.sem, H0)
            nc.gpsimd.memset(gb[:, :, :, :], 0.0).then_inc(gz.sem, 1)

            def store(half, place):
                pool.dma_start(gates[place, :, :], gb[:, half, :, :].rearrange("p a t -> p (a t)")
                               ).then_inc(gd[half].sem, 16)

            pool.wait_ge(gz.sem, gz.at(1))
            store(0, NTG + 1)
            with pool.Fori(0, NS) as g:
                for q in range(Q):
                    if q == 5:
                        pool.wait_ge(gc.sem, g * Q + gc.base + 2)
                        store(1, g * 2)
                    if q == 13:
                        pool.wait_ge(gc.sem, g * Q + gc.base + 2 + Q // 2)
                        store(0, g * 2 + 1)
                    if q % 8 == 0:
                        pool.wait_ge(gk.sem, g * 2 + gk.base + q // 8 + 1)
                    pool.wait_ge(gm.sem, g * TS + gm.base + 4 * q + 4)
                    nc.gpsimd.tensor_tensor(held[:, q:q + 1], p.ones[:, 0:1], p.ones[:, 0:1], ALU.mult)
                    for t in range(4 * q, 4 * q + 4):
                        ins = nc.gpsimd.tensor_scalar(o2[:, t % R, :], p.iota[:, :],
                                                      kb[:, t // TG, 1, t % TG:t % TG + 1], None,
                                                      ALU.is_equal)
                    ins.then_inc(h2.sem, 4)
            pool.wait_ge(gc.sem, gc.at(2 + Q * NS))
            store(1, NTG)
            for s in range(2):
                pool.wait_ge(gd[s].sem, gd[s].at(16 * (NS + 1)))

        @block.tensor
        def _(pe):
            pe.sem_inc(gm.sem, R)
            with pe.Fori(0, NS) as g:
                for k in range(UN):
                    rows.multiply(pe, g * UN + n0 + k, (n0 + k) % 2, g * UN + u0 + k, (u0 + k) % RAW)
                    for q in fours(k):
                        pe.wait_ge(h1.sem, g * TS + h1.base + 4 * q + 4)
                        pe.wait_ge(h2.sem, g * TS + h2.base + H0 + 4 * q + 4)
                        pe.wait_ge(gc.sem, g * Q + gc.base + q + 1)
                        for r in range(4):
                            ins = nc.tensor.matmul(p.ps[:, 2 + q % 2, r * KEYS:(r + 1) * KEYS],
                                                   o2[:, (4 * q + r) % R, :], o1[:, (4 * q + r) % R, :],
                                                   start=True, stop=True)
                        ins.then_inc(gm.sem, 4)

        @block.scalar
        def _(act):
            act.wait_ge(gz.sem, gz.at(1))
            act.sem_inc(gc.sem, 2)
            with act.Fori(0, NS) as g:
                for k in range(UN):
                    u = u0 + k + 1
                    p.split_hi(act, g * UN + u, u % RAW, g * (UN // RAW) + u // RAW + 1)
                    rows.gelu(act, g * UN + n0 + k, g * (UN // 2) + (n0 + k) // 2, (n0 + k) % 2, g * UN + u0 + k)
                    for q in fours(k):
                        half, at = divmod(4 * q, TG)
                        act.wait_ge(gm.sem, g * TS + gm.base + R + 4 * q + 4)
                        if at == 0:
                            act.wait_ge(gd[half].sem, g * 16 + gd[half].base + 16)
                        nc.scalar.activation(gb[:, half, :, at:at + 4].rearrange("p a t -> p t a"),
                                             p.ps[:, 2 + q % 2, :].rearrange("p (t a) -> p t a", t=4),
                                             ACT.Copy).then_inc(gc.sem, 1)
            rows.close(act)

        @block.sync
        def _(sp):
            for j in range(RAW, UN):
                p.load(sp, u0 + j, (u0 + j) % RAW, us[n0 + j, :, :])
            with sp.Fori(1, NS) as g:
                for k in range(UN):
                    p.load(sp, g * UN + u0 + k, (u0 + k) % RAW, us[g * UN + n0 + k, :, :])
            p.unit += NS * UN
            prefetch(p, sp, nxt)
            p.unit -= NS * UN
    h1.base += T
    h2.base += T + H0
    gm.base += T + R
    gc.base += T // 4 + 2
    gk.base += 2 * NS + 1
    gz.base += 1
    for s in gd:
        s.base += 16 * (NS + 1)
    rows.done()
    p.unit += NS * UN


def peer_values(p, acts, gates, vs, nxt):
    nc = p.nc
    names = ("gated", "act_hi", "act_lo", "block_loaded0", "block_loaded1",
             "first_gates", "first_rows", "first_rest")
    gt_, ah, al, bl0, bl1, fg, fr, fs = (p.sig(n) for n in names)
    bl = (bl0, bl1)
    used = p.sig("w_used")
    u0 = p.unit
    B = BLOCK
    halves = ((p.yh, p.yl), (p.hh, p.hl))
    with ExitStack() as ctx:
        at = p.sb("gelu_block", [P, 2, B, T], ctx=ctx)
        gt = p.sb("gate_block", [P, 2, NTG, B * TG], ctx=ctx)
        block = ctx.enter_context(nc.Block())

        def blocks(eng, body):
            body(0, 0, 0, 0)
            with eng.Fori(0, NBLOCK // 2 - 1) as ii:
                for k in range(2):
                    body(ii * 2 + 1 + k, (1 + k) % 2, None, ii + 1)
            body(NBLOCK - 1, 1, NBLOCK - 1, None)

        @block.sync
        def _(sp):
            for j in range(RAW, B):
                p.load(sp, u0 + j, (u0 + j) % RAW, vs[j, :, :])
            with sp.Fori(1, NBLOCK) as i:
                for j in range(B):
                    p.load(sp, i * B + u0 + j, (u0 + j) % RAW, vs[i * B + j, :, :])
            p.unit += B * NBLOCK
            prefetch(p, sp, nxt)
            p.unit -= B * NBLOCK

        @block.gpsimd
        def _(pool):
            rows = acts.rearrange("n p t -> p n t")
            some = gates[1:NTG + 1, :, :].rearrange("g p m -> p g m")
            pool.dma_start(gt[:, 0, :, :], some[:, :, 0:B * TG]).then_inc(fg.sem, 16)
            pool.dma_start(at[:, 0, 0:2, :], rows[:, 0:2, :]).then_inc(fr.sem, 16)
            pool.dma_start(at[:, 0, 2:B, :], rows[:, 2:B, :]).then_inc(fs.sem, 16)

            def body(i, s, fixed, half):
                if fixed != NBLOCK - 1:
                    pool.wait_ge(al.sem, i * B + al.base + 2 * B)
                    pool.dma_start(at[:, 1 - s, :, :], rows[:, bass.ds(i * B + B, B), :]
                                   ).then_inc(bl[1 - s].sem, 16)
                    pool.dma_start(gt[:, 1 - s, :, :], some[:, :, bass.ds(i * (B * TG) + B * TG, B * TG)]
                                   ).then_inc(bl[1 - s].sem, 16)
            blocks(pool, body)

        def hi(act, i, s, j):
            act.wait_ge(gt_.sem, i * B + gt_.base + j + 1)
            nc.scalar.activation(halves[s][0][:, j, :], at[:, s, j, :], ACT.Copy).then_inc(ah.sem, 1)

        def mult(dve, i, s, j, ii):
            if ii is None:
                for sig, row in ((fg, 0), (fr, 0), (fs, 2)):
                    if j == row:
                        dve.wait_ge(sig.sem, sig.at(16))
            elif j == 0:
                dve.wait_ge(bl[s].sem, ii * 32 + bl[s].base + 32 * s)
            a3 = at[:, s, j, :].rearrange("p (g t) -> p g t", g=NTG)
            nc.vector.tensor_tensor(a3, a3, gt[:, s, :, j * TG:(j + 1) * TG], ALU.mult).then_inc(gt_.sem, 1)

        def lo(dve, i, s, j):
            dve.wait_ge(ah.sem, i * B + ah.base + j + 1)
            nc.vector.tensor_tensor(halves[s][1][:, j, :], at[:, s, j, :],
                                    halves[s][0][:, j, :].bitcast(F32), ALU.subtract).then_inc(al.sem, 1)

        @block.tensor
        def _(pe):
            def body(i, s, fixed, half):
                for j in range(B):
                    def tile(k):
                        if j == 0:
                            pe.wait_ge(al.sem, i * B + al.base + 2 * B + k + 1)
                    p.product(pe, i * B + u0 + j, (u0 + j) % RAW, p.ps[:, j, :], *halves[s],
                              first=fixed == 0, last=fixed == NBLOCK - 1, wait_tile=tile
                              ).then_inc(used.sem, 1)
            blocks(pe, body)

        @block.scalar
        def _(act):
            for j in range(B):
                hi(act, 0, 0, j)

            def body(i, s, fixed, half):
                for j in range(B):
                    u = u0 + j + 1
                    p.split_hi(act, i * B + u, u % RAW, i * (B // RAW) + u // RAW + 1)
                    if fixed != NBLOCK - 1:
                        hi(act, i + 1, 1 - s, j)
            blocks(act, body)

        @block.vector
        def _(dve):
            dve.sem_inc(al.sem, 2 * B)
            for j in range(B):
                mult(dve, 0, 0, j, None)
                if j:
                    lo(dve, 0, 0, j - 1)

            def body(i, s, fixed, half):
                for j in range(B):
                    p.split_lo(dve, i * B + u0 + j + 1, (u0 + j + 1) % RAW)
                    if j == 0:
                        lo(dve, i, s, B - 1)
                    if fixed != NBLOCK - 1:
                        mult(dve, i + 1, 1 - s, j, half)
                        if j:
                            lo(dve, i + 1, 1 - s, j - 1)
                    else:
                        dve.wait_ge(used.sem, u0 + i * B + j + 1)
                        nc.vector.tensor_tensor(p.x[:, j, :], p.ps[:, j, :], p.x[:, j, :], ALU.add)
            blocks(dve, body)
    for s in (gt_, ah):
        s.base += KEYS
    al.base += KEYS + 2 * B
    bl0.base += 32 * (NBLOCK // 2 - 1)
    bl1.base += 32 * NBLOCK // 2
    for s in (fg, fr, fs):
        s.base += 16
    p.unit += B * NBLOCK


class Embedding:

    def __init__(self, p, pw, e, emb):
        self.p, self.pw, self.e, self.emb, self.u0 = p, pw, e, emb, p.unit
        self.ld, self.hi, self.lo = p.sig("emb_loaded"), p.sig("emb_hi"), p.sig("emb_lo")
        self.used = p.sig("w_used")

    def sync(self, sp):
        sp.dma_start(self.e[:, :, :], self.emb).then_inc(self.ld.sem, 16)

    def act_first(self, act):
        p, u = self.p, self.u0 + 1
        act.wait_ge(self.ld.sem, self.ld.at(16))
        p.nc.scalar.activation(p.yh[:, 0:2, :], self.e[:, :, :], ACT.Copy).then_inc(self.hi.sem, 1)
        p.split_hi(act, u, u % RAW, u // RAW + 1)

    def act_second(self, act):
        u = self.u0 + 2
        self.p.split_hi(act, u, u % RAW, u // RAW + 1)

    def act_tile(self, act, k):
        act.wait_ge(self.used.sem, self.u0 + 1 + k // 4)
        self.p.nc.scalar.activation(self.pw[:, k, :], self.p.ps[:, k, :], ACT.Copy)

    def vector_first(self, dve):
        p, u = self.p, self.u0 + 1
        dve.wait_ge(self.hi.sem, self.hi.at(1))
        p.nc.vector.tensor_tensor(p.yl[:, 0:2, :], self.e[:, :, :], p.yh[:, 0:2, :].bitcast(F32),
                                  ALU.subtract).then_inc(self.lo.sem, 1)
        p.split_lo(dve, u, u % RAW)

    def vector_last(self, dve):
        u = self.u0 + 2
        self.p.split_lo(dve, u, u % RAW)

    def tensor(self, pe, root):
        p = self.p
        pe.wait_ge(self.lo.sem, self.lo.at(1))
        for j in range(2):
            u = self.u0 + j
            if j:
                pe.wait_ge(root.sem, root.at(1))
            pe.wait_ge(p.sig("w_lo_ready").sem, u + 1)
            for q in range(4):
                for k in range(2):
                    w_ = slice((q * 2 + k) * P, (q * 2 + k + 1) * P)
                    for m, (a, y) in enumerate(((p.wh, p.yh), (p.wh, p.yl), (p.wl, p.yh))):
                        ins = p.nc.tensor.matmul(p.ps[:, 4 * j + q, :], a[:, u % SPL, w_], y[:, k, :],
                                                 start=k == 0 and m == 0, stop=k == 1 and m == 2)
            ins.then_inc(self.used.sem, 1)

    def done(self):
        self.ld.base += 16
        self.hi.base += 1
        self.lo.base += 1
        self.p.unit += 2


def ple_gate(p, gate, pw, sg, nxt):
    v, md = p.nc.vector, p.sig("ple_mul")

    def add(i, ps):
        v.tensor_tensor(sg[:, i, :], sg[:, i, :], pw[:, i, :], ALU.mult).then_inc(md.sem, 1)
        v.wait_ge(md.sem, i + md.base + 1)
        return v.tensor_tensor(p.x[:, i, :], p.x[:, i, :], sg[:, i, :], ALU.add)

    linear(p, [(gate, DK, 1, [(p.hh, p.hl)], add,
                lambda i, ps: p.nc.scalar.activation(sg[:, i, :], ps, ACT.Sigmoid))], nxt)
    md.base += DK


def odd_gates(p, b, nxt):
    nc = p.nc
    small, rows, used = p.sig("act_small"), p.sig("rows_ready"), p.sig("w_used")
    tn = p.sig("gates_turned")
    H = HEADS
    u = p.unit
    with ExitStack() as ctx:
        names = ("xb", "ab", "e1", "ln", "rc", "F", "ig", "G", "one", "em")
        r = {n: p.sb(f"gate_{n}", [H, T], ctx=ctx) for n in names}
        block = ctx.enter_context(nc.Block())

        @block.sync
        def _(sp):
            p.unit += 4
            prefetch(p, sp, nxt[3:4])
            p.unit -= 4

        @block.scalar
        def _(act):
            p.split_hi(act, u + 1, (u + 1) % RAW, (u + 1) // RAW + 1)
            log1p_act(act, nc, rows, small, r["e1"], r["ab"], r["ln"])
            act.wait_ge(rows.sem, rows.at(3))
            nc.scalar.activation(r["em"][:, :], r["em"][:, :], ACT.Exp, scale=-1.0).then_inc(small.sem, 1)

        @block.tensor
        def _(pe):
            p.product(pe, u, u % RAW, p.ps[:, 7, :], p.hh, p.hl).then_inc(used.sem, 1)
            pe.wait_ge(small.sem, small.at(3))
            for k, n in enumerate(("ig", "em")):
                for j in range(TT):
                    ins = nc.tensor.transpose(p.ps[:, 6, (k * TT + j) * H:(k * TT + j + 1) * H],
                                              r[n][:, j * P:(j + 1) * P], p.ident[0:H, 0:H])
            ins.then_inc(tn.sem, 1)

        @block.vector
        def _(dve):
            v = nc.vector
            link = Chain(dve, p.sig("dve_chain"))
            v.memset(r["one"][:, :], 1.0)
            p.split_lo(dve, u + 1, (u + 1) % RAW)
            dve.wait_ge(used.sem, u + 1)
            link(v.tensor_copy(r["G"][:, :], p.ps[32:32 + H, 7, :]))
            log1p_rows(v, link, rows, small, r["G"][:, :], p.col("f_bias", 0, H), r["xb"], r["ab"],
                       r["e1"], r["ln"], r["rc"])
            link(v.tensor_scalar(r["xb"][:, :], r["xb"][:, :], 0.0, None, ALU.min))
            link(v.tensor_tensor(r["xb"][:, :], r["xb"][:, :], r["ln"][:, :], ALU.subtract))
            link(v.tensor_tensor_scan(r["F"][:, :], r["one"][:, :], r["xb"][:, :], 0.0, ALU.mult, ALU.add))
            link(v.tensor_scalar(r["ig"][:, :], p.ps[0:H, 7, :], p.col("i_bias", 0, H), None, ALU.add))
            link(v.tensor_tensor(r["ig"][:, :], r["ig"][:, :], r["F"][:, :], ALU.subtract))
            link(v.tensor_tensor_scan(r["G"][:, :], r["one"][:, :], r["ig"][:, :], 0.0, ALU.mult, ALU.max))
            link(v.tensor_scalar(b["negG"][:, :], r["G"][:, :], -1.0, None, ALU.mult))
            v.tensor_tensor(r["em"][:, :], r["F"][:, :], r["G"][:, :], ALU.add).then_inc(rows.sem, 1)
            dve.wait_ge(tn.sem, tn.at(1))
            link(v.tensor_copy(b["cols"][:, :, :, :].rearrange("p k j h -> p (k j h)"),
                               p.ps[:, 6, 0:2 * TT * H]))
            link(v.memset(b["hn"][:, :, :], 0.0))
            link(v.memset(b["os"][:, :], 0.0))
            link(v.memset(b["qk"][:, :, 0:CONV - 1], 0.0))
            link(v.memset(b["vs"][:, :, :], 1.0))
            link.done()
    small.base += 3
    rows.base += 3
    tn.base += 1
    p.unit += 1


def odd_heads(p, b, half, w, nxt):
    nc = p.nc
    names = ("od_conv", "od_silu", "od_y", "od_yhi", "od_sel", "od_bc", "od_s", "od_arg", "od_exp", "od_sw",
             "od_vt", "od_vs", "od_num", "od_sig", "od_ssq", "od_ms", "od_root", "od_hn", "od_turn")
    (cv, si, yy, yh, se, bc, sc, ag, ex, sw, vt, vs, nu, sg, sq, ms, ro, hn, tu) = (p.sig(n) for n in names)
    used, taken = p.sig("w_used"), p.sig("out_taken")
    u0, o0 = p.unit, p.out
    NH = HEADS // 2
    SC = P ** -0.5
    W = b["w"]
    blocks = [(4, 0), (5, 0), (6, 0), (6, 256)]

    def width(i):
        return T - i * P

    def turn(pe, n):
        pe.wait_ge(hn.sem, n)
        for j in range(TT):
            ins = nc.tensor.transpose(p.ps[:, 7, j * P:(j + 1) * P], b["hn"][:, j, :], p.ident[:, :])
        ins.then_inc(tu.sem, 1)

    def gate(dve, n, h):
        dve.wait_ge(tu.sem, n + tu.base + 1)
        dve.wait_ge(sg.sem, n + sg.base + 1)
        return nc.vector.scalar_tensor_tensor(out=b["yf"][:, :], in0=p.ps[:, 7, :],
                                              scalar=p.par[:, bass.ds(h + COLS["head_norm"], 1)],
                                              in1=b["os"][:, :], op0=ALU.mult, op1=ALU.mult)

    def split(dve, n, slot):
        dve.wait_ge(yh.sem, n + yh.base + 1)
        return nc.vector.tensor_tensor(p.yl[:, slot, :], b["yf"][:, :], p.yh[:, slot, :].bitcast(F32),
                                       ALU.subtract)

    with nc.Block() as block:
        @block.sync
        def _(sp):
            with sp.Fori(1, NH) as i:
                for j in range(4):
                    p.load(sp, i * 4 + u0 + j, (u0 + j) % RAW, w[i * 4 + j, :, :])
            p.unit += 4 * NH
            prefetch(p, sp, nxt)
            p.unit -= 4 * NH

        @block.tensor
        def _(pe):
            t = nc.tensor

            def lin(i, j):
                if j == 1:
                    pe.wait_ge(sg.sem, i + sg.base + 1)
                else:
                    pe.wait_ge(taken.sem, i * 3 + o0 + (0, None, 1, 2)[j])
                p.product(pe, i * 4 + u0 + j, (u0 + j) % RAW, p.ps[:, j % 2, :], p.hh, p.hl
                          ).then_inc(used.sem, 1)

            def output(i):
                pe.wait_ge(vs.sem, i + vs.base + 1)
                pe.wait_ge(sw.sem, i + sw.base + 1)
                for j in range(TT):
                    for s in range(j + 1):
                        ins = t.matmul(p.ps[:, 2 + j // 2, (j % 2) * 130:(j % 2) * 130 + 130],
                                       W[:, s, j * P:(j + 1) * P], b["vs"][:, s, :], start=s == 0, stop=s == j)
                ins.then_inc(nu.sem, 1)

            with pe.Fori(0, NH) as i:
                lin(i, 0)
                output(i)
                lin(i, 1)
                lin(i, 2)
                turn(pe, i + hn.base + 1)
                pe.wait_ge(se.sem, i + se.base + 1)
                t.matmul(p.ps[:, 2, :], p.ones[0:HEADS, :], b["rsel"][:, :], start=True, stop=True
                         ).then_inc(bc.sem, 1)
                pe.wait_ge(si.sem, i * 2 + si.base + 2)
                for s in range(TT):
                    bank, c = blocks[s]
                    ins = t.matmul(p.ps[:, bank, c:c + width(s)], b["kT"][:, s * P:(s + 1) * P],
                                   b["qT"][:, s * P:], start=True, stop=True, skip_group_check=True)
                ins.then_inc(sc.sem, 1)
                lin(i, 3)
                pe.wait_ge(taken.sem, i * 3 + o0 + 3)
                for j in range(TT):
                    ins = t.transpose(p.ps[:, 3, j * P:(j + 1) * P], b["vT"][:, j * P:(j + 1) * P], p.ident[:, :])
                ins.then_inc(vt.sem, 1)
            output(NH)
            turn(pe, NH + hn.base + 1)

        @block.scalar
        def _(act):
            a = nc.scalar
            if half == 0:
                act.sem_inc(sg.sem, 1)

            def squares(i):
                act.wait_ge(nu.sem, i + nu.base + 1)
                for j in range(TT):
                    ins = a.activation(b["sqj"][:, :], p.ps[:, 2 + j // 2, (j % 2) * 130:(j % 2) * 130 + P],
                                       ACT.Square, accum_out=b["small"][:, 0, j:j + 1])
                    ins.then_inc(sq.sem, 1)
                    act.wait_ge(sq.sem, i * 4 + sq.base + j + 1)
                act.wait_ge(ms.sem, i + ms.base + 1)
                a.activation(b["small"][:, 3, :], b["small"][:, 3, :], ACT.Sqrt).then_inc(ro.sem, 1)

            def hi(i, slot):
                act.wait_ge(yy.sem, i + yy.base + 1)
                a.activation(p.yh[:, slot, :], b["yf"][:, :], ACT.Copy).then_inc(yh.sem, 1)

            def split(i, j):
                p.split_hi(act, i * 4 + u0 + j + 1, (u0 + j + 1) % RAW, i + (u0 + j + 1) // RAW + 1)

            def silu(i, j):
                act.wait_ge(cv.sem, i * 2 + cv.base + j + 1)
                a.activation(b["kT" if j == 0 else "qT"][:, :], b["tmp"][:, 1, :], ACT.Silu
                             ).then_inc(si.sem, 1)

            with act.Fori(0, NH) as i:
                split(i, 0)
                silu(i, 0)
                split(i, 1)
                squares(i)
                split(i, 2)
                silu(i, 1)
                split(i, 3)
                hi(i, i)
                for s in range(TT):
                    act.wait_ge(ag.sem, i * 4 + ag.base + s + 1)
                    a.activation(W[:, s, s * P:], W[:, s, s * P:], ACT.Exp).then_inc(ex.sem, 1)
                act.wait_ge(used.sem, i * 4 + u0 + 4)
                a.activation(b["os"][:, :], p.ps[:, 1, :], ACT.Sigmoid).then_inc(sg.sem, 1)
            squares(NH)
            hi(NH, 0)

        @block.vector
        def _(dve):
            v = nc.vector
            link = Chain(dve, p.sig("dve_chain"))
            sm = b["small"]
            if half == 0:
                v.memset(W[:, :, :], 0.0)
                v.memset(b["emc"][:, :], 1.0).then_inc(sw.sem, 1)
            else:
                dve.sem_inc(sw.sem, 1)
            dve.sem_inc(vs.sem, 1)

            def lo(i, j):
                p.split_lo(dve, i * 4 + u0 + j + 1, (u0 + j + 1) % RAW)

            def conv(i, j):
                dve.wait_ge(used.sem, i * 4 + u0 + j + 1)
                v.tensor_copy(b["qk"][:, j, CONV - 1:], p.ps[:, j % 2, :]).then_inc(taken.sem, 1)
                dve.wait_ge(taken.sem, i * 3 + o0 + j + 1)
                if j:
                    dve.wait_ge(si.sem, i * 2 + si.base + j)
                tile = i + (HEADS if j == 0 else 0) + half * NH
                conv_steps(nc, link, b["qk"][:, j, :], [b["tmp"][:, k % 2, :] for k in range(CONV)],
                           [p.par[:, bass.ds(tile * CONV + COLS["od_conv_w"] + k, 1)] for k in range(CONV)],
                           p.par[:, bass.ds(tile + COLS["od_conv_b"], 1)]).then_inc(cv.sem, 1)


            def normed(i):
                dve.wait_ge(nu.sem, i + nu.base + 1)
                dve.wait_ge(sq.sem, i * 4 + sq.base + 4)
                den = p.ps[:, 2:4, 0:260].rearrange("p b (j e) -> p b j e", e=130)[:, :, :, P]
                s4 = [sm[:, k, :] for k in range(5)]
                link(v.tensor_copy(s4[1].rearrange("p (b j) -> p b j", b=2), den))
                link(v.scalar_tensor_tensor(out=s4[2], in0=s4[1], scalar=-1.0, in1=s4[1], op0=ALU.mult,
                                            op1=ALU.max))
                link(v.tensor_tensor(s4[2], s4[2], b["emc"][:, :], ALU.max))
                link(v.reciprocal(s4[1], s4[2]))
                link(v.scalar_tensor_tensor(out=s4[2], in0=s4[0], scalar=1.0 / P, in1=s4[1], op0=ALU.mult,
                                            op1=ALU.mult))
                link(v.tensor_tensor(s4[2], s4[2], s4[1], ALU.mult))
                v.tensor_scalar(s4[3], s4[2], EPS, None, ALU.add).then_inc(ms.sem, 1)
                dve.wait_ge(ro.sem, i + ro.base + 1)
                link(v.reciprocal(s4[4], s4[3]))
                link(v.tensor_tensor(s4[4], s4[4], s4[1], ALU.mult))
                num = p.ps[:, 2:4, 0:260].rearrange("p b (j e) -> p b j e", e=130)[:, :, :, 0:P]
                v.tensor_tensor(b["hn"][:, :, :].rearrange("p (b j) e -> p b j e", b=2), num,
                                s4[4].rearrange("p (b j) -> p b j", b=2).unsqueeze(3).to_broadcast([P, 2, 2, P]),
                                ALU.mult).then_inc(hn.sem, 1)

            with dve.Fori(0, NH) as i:
                link.enter(i, 2 * 3 + 13)
                h = i + half * NH
                lo(i, 0)
                conv(i, 0)
                lo(i, 1)
                normed(i)
                v.tensor_scalar(b["rsel"][:, :], b["negG"][:, :], p.ident[0:HEADS, bass.ds(h, 1)], None,
                                ALU.mult).then_inc(se.sem, 1)
                conv(i, 1)
                lo(i, 2)
                dve.wait_ge(used.sem, i * 4 + u0 + 3)
                v.tensor_copy(b["vT"][:, :], p.ps[:, 0, :]).then_inc(taken.sem, 1)
                gate(dve, i, h - 1).then_inc(yy.sem, 1)
                lo(i, 3)
                dve.wait_ge(bc.sem, i + bc.base + 1)
                for s in range(TT):
                    v.tensor_scalar(W[:, s, s * P:], p.ps[:, 2, s * P:], b["cols"][:, 0, s, bass.ds(h, 1)], 0.0,
                                    ALU.add, ALU.min).then_inc(ag.sem, 1)
                v.tensor_copy(b["emc"][:, :], b["cols"][:, 1, :, bass.ds(h, 1)].rearrange("p j o -> p (j o)"))
                link(split(dve, i, i))
                dve.wait_ge(sc.sem, i + sc.base + 1)
                for s in range(TT):
                    dve.wait_ge(ex.sem, i * 4 + ex.base + s + 1)
                    bank, c = blocks[s]
                    ins = v.scalar_tensor_tensor(out=W[:, s, s * P:], in0=p.ps[:, bank, c:c + width(s)],
                                                 scalar=SC, in1=W[:, s, s * P:], op0=ALU.mult, op1=ALU.mult)
                    link(ins)
                for s in range(TT):
                    ins = v.tensor_tensor(W[:, s, s * P:(s + 1) * P], W[:, s, s * P:(s + 1) * P],
                                          p.incl[:, 0:P], ALU.mult)
                ins.then_inc(sw.sem, 1)
                dve.wait_ge(vt.sem, i + vt.base + 1)
                v.tensor_copy(b["vs"][:, :, 0:P], p.ps[:, 3, :].rearrange("p (j e) -> p j e", j=TT)
                              ).then_inc(vs.sem, 1)
                link.leave(NH)
            normed(NH)
            gate(dve, NH, half * NH + NH - 1).then_inc(yy.sem, 1)
            link(split(dve, NH, 0))
            link.done()
    for s, n in ((cv, 2), (si, 2), (se, 1), (bc, 1), (sc, 1), (ag, 4), (ex, 4), (vt, 1), (sg, 1)):
        s.base += n * NH
    for s, n in ((yy, 1), (yh, 1), (hn, 1), (tu, 1), (sw, 1), (vs, 1), (nu, 1), (sq, 4), (ms, 1), (ro, 1)):
        s.base += n * (NH + 1)
    p.unit += 4 * NH
    p.out += 3 * NH


def store(p, src):
    nc = p.nc
    done = p.sig("stored")
    with nc.Block() as block:
        @block.sync
        def _(sp):
            sp.dma_start(p.dram["out"], src[:, :, :]).then_inc(done.sem, 16)
            sp.wait_ge(done.sem, done.at(16))
    done.base += 16


def add_to(p):
    return lambda i, ps: p.nc.vector.tensor_tensor(p.x[:, i, :], ps, p.x[:, i, :], ALU.add)


def firsts(src, n=RAW):
    return [src[j, :, :] for j in range(n)]


def ffn_firsts(d, layer):
    w, u = d[f"wq{layer}"], d[f"u{layer}"]
    return [w[0, :, :], u[0, :, :], w[1, :, :], u[1, :, :]]


def ffn(p, layer, nxt):
    d = p.dram
    wq, us, vs, gate, pw_ = (d[f"{n}{layer}"] for n in ("wq", "u", "v", "gate", "plew"))
    norm(p, p.x, f"norm_ffn{layer}", out=(p.hh, p.hl))
    with ExitStack() as outer:
        b = {"sel": p.sb("selected", [P, 3, T + TG], ctx=outer)}
        rows = Rows(p, d["acts"], p.sb("gelu", [P, 2, T], ctx=outer))
        with ExitStack() as ctx:
            b["side_index"] = p.sb("key_index", [P, TT, 2, P], ctx=ctx)
            b["top"] = p.sb("top_sums", [P, TT, P], ctx=ctx)
            b["pos"] = p.sb("top_pos", [P, TT, P], U32, ctx=ctx)
            n1 = 2 * PEER_HEADS + 4
            peer_topk(p, b, rows, wq, us, d[f"sub{layer}"], firsts(us[n1:]))
            peer_decode(p, b, rows, us, n1, firsts(us[n1 + 12:]))
        peer_gates(p, b, rows, us, n1 + 12, d["gates"], firsts(vs))
    peer_values(p, d["acts"], d["gates"], vs, [pw_[0, :, :], pw_[1, :, :], gate[0, :, :], gate[1, :, :]])
    with ExitStack() as ctx:
        pw = p.sb("embedded", [P, DK, T], ctx=ctx)
        sg = p.sb("ple_gate", [P, DK, T], ctx=ctx)
        embedding = Embedding(p, pw, p.sb("embedding", [P, 2, T], ctx=ctx), d["emb"][layer])
        p.unit += RAW
        norm(p, p.x, f"norm_ple{layer}", out=(p.hh, p.hl), nxt=[gate[2, :, :], gate[3, :, :]], beside=embedding)
        p.unit -= RAW
        embedding.done()
        ple_gate(p, gate, pw, sg, nxt)


def trunk(nc, dram):
    with ExitStack() as ctx:
        p = Program(nc, ctx, dram)
        start(p, firsts(dram["ev_in"]))
        norm(p, p.x, "norm_mix0", out=(p.hh, p.hl))
        with ExitStack() as c:
            b = {"z": p.sb("z", [P, DK, T], ctx=c), "xbc": p.sb("xbc", [P, XBC, CONV - 1 + T], ctx=c),
                 "q": p.sb("q", [P, 8, T], ctx=c)}
            with ExitStack() as c2:
                b["dtraw"] = p.sb("dt_raw", [HEADS, T], ctx=c2)
                with ExitStack() as c3:
                    b["kd"] = p.sb("k_twice", [P, 2, 640], ctx=c3)
                    b["vt"] = p.sb("v_rows", [P, 640], ctx=c3)
                    even_in(p, b, firsts(dram["ev_out"]))
                    even_attention(p, b)
                b["dt"] = b["dtraw"]
                b["adt"] = p.sb("a_dt", [HEADS, T], ctx=c2)
                even_dt(p, b)
                even_ssd(p, b)
            norm(p, b["z"], "out_norm", out=(p.hh, p.hl))
        linear(p, [(dram["ev_out"], 16, 2, [(p.hh, p.hl), (p.yh, p.yl)], add_to(p))], ffn_firsts(dram, 0))
        ffn(p, 0, firsts(dram["od_in"]))
        norm(p, p.x, "norm_mix1", out=(p.hh, p.hl))
        with ExitStack() as c:
            b = {"negG": p.sb("neg_g", [HEADS, T], ctx=c), "cols": p.sb("gate_cols", [P, 2, TT, HEADS], ctx=c),
                 "hn": p.sb("head_out", [P, TT, P], ctx=c), "os": p.sb("o_sigmoid", [P, T], ctx=c),
                 "qk": p.sb("qk_rows", [P, 2, CONV - 1 + T], ctx=c), "vs": p.sb("v_turned_od", [P, TT, 130], ctx=c)}
            odd_gates(p, b, firsts(dram["od_in"], 5)[1:])
            for n, shape in (("w", [P, TT, T]), ("kT", [P, T]), ("qT", [P, T]), ("vT", [P, T]),
                             ("tmp", [P, 2, T]), ("yf", [P, T]), ("rsel", [HEADS, T]), ("sqj", [P, P]),
                             ("small", [P, 5, TT]), ("emc", [P, TT])):
                b[n] = p.sb(f"od_{n}", shape, ctx=c)
            y = [(p.yh, p.yl)]
            w = dram["od_in"]
            odd_heads(p, b, 0, w[1:33], firsts(dram["od_out"]))
            linear(p, [(dram["od_out"], 8, 1, y, add_to(p))], firsts(w[33:65]))
            odd_heads(p, b, 1, w[33:65], firsts(dram["od_out"][8:16]))
            linear(p, [(dram["od_out"][8:16], 8, 1, y, add_to(p))], ffn_firsts(dram, 1))
        ffn(p, 1, firsts(dram["ev_in"], 1))
        norm(p, p.x, "norm_final", dst=p.x)
        store(p, p.x)


def _units(w, tiles=DK):
    K, N = w.shape
    return np.ascontiguousarray(w.reshape(K // (tiles * P), tiles, P, N // P, P).transpose(3, 0, 2, 1, 4)
                                ).reshape(-1, P, tiles * P)


def _cols(v):
    return v.reshape(-1, P).T


def _rows16(v):
    out = np.zeros((P, 1), v.dtype)
    out[:HEADS, 0] = v
    return out


def _lay_out(i):
    w = i["ev_w_in"][0]
    at = np.cumsum([0, INNER, XBC * P, HEADS, 1024, P, P])
    z, xbc, dt, q, k, v = (w[:, a:c] for a, c in zip(at[:-1], at[1:]))
    dt = np.pad(dt, ((0, 0), (0, P - HEADS)))
    kk = [k[:, :64], k[:, :64], k[:, 64:], k[:, 64:]]
    m = {"ev_in": _units(np.concatenate([z, xbc, q, *kk, v, dt], 1)), "ev_out": _units(i["ev_w_out"][0])}
    w = i["od_w_in"][0]
    I = HEADS * P
    q, k, v, o = (w[:, a * I:(a + 1) * I].reshape(D, HEADS, P) for a in range(4))
    g = np.zeros((D, P), w.dtype)
    g[:, 0:HEADS] = w[:, 4 * I:4 * I + HEADS]
    g[:, 32:32 + HEADS] = w[:, 4 * I + HEADS:]
    m["od_in"] = _units(np.concatenate([g, np.stack([k, q, v, o], 2).reshape(D, 4 * I)], 1))
    w = i["od_w_out"][0]
    m["od_out"] = np.concatenate([_units(np.roll(x.reshape(8, P, D), 1, 0).reshape(1024, D))
                                  for x in (w[:1024], w[1024:])], 0)
    for n in range(2):
        m[f"wq{n}"] = _units(i["pk_w_q"][n].reshape(D, -1))
        s = np.stack([i["pk_sub_k1"][n], i["pk_sub_k2"][n]], 1)
        m[f"sub{n}"] = s.reshape(16, KEYS, P).transpose(2, 0, 1)
        m[f"u{n}"] = _units(i["pk_u"][n].T)
        m[f"v{n}"] = i["pk_v"][n].reshape(NBLOCK, BLOCK, KEYS, DK, P).transpose(0, 3, 2, 1, 4).reshape(-1, P, UNIT)
        m[f"gate{n}"] = _units(i["ple_gate"][n])
        m[f"plew{n}"] = i["ple_w"][n].reshape(2, P, 2, 4, P).transpose(2, 1, 3, 0, 4).reshape(2, P, UNIT)
        m[f"emb{n}"] = i["p"][n, 0].T.reshape(2, P, T).transpose(1, 0, 2)
    m["x"] = i["x"][0].T.reshape(DK, P, T).transpose(1, 0, 2)
    taps = lambda w: w.reshape(CONV, -1, P).transpose(2, 1, 0).reshape(P, -1)
    m["par"] = np.concatenate(
        [_cols(i[n][l]) for n in ("norm_mix", "norm_ffn", "norm_ple") for l in range(2)]
        + [_cols(i["norm_final"]), _cols(i["ev_out_norm"][0]), _cols(np.repeat(i["ev_d_skip"][0], 64)),
           taps(i["ev_conv_w"][0]), _cols(i["ev_conv_b"][0]), 
           np.repeat(i["ev_sinks"].reshape(4, 2, 2).transpose(0, 2, 1).reshape(1, -1), P, 0),
           taps(i["od_conv_w"][0]), _cols(i["od_conv_b"][0]), _cols(i["od_head_norm"][0]),
           _rows16(i["ev_dt_bias"][0]), _rows16(i["ev_a_log"][0]), _rows16(i["od_i_bias"][0]),
           _rows16(i["od_f_bias"][0])], 1)
    return {k: np.ascontiguousarray(a) for k, a in m.items()}


def build(nc, shapes):
    dram = {n: nc.dram_tensor(f"in_{n}", s, F32, kind="ExternalInput").ap() for n, s in shapes.items()}
    dram["emb"] = [dram["emb0"], dram["emb1"]]
    dram["out"] = nc.dram_tensor("out_0", [P, DK, T], F32, kind="ExternalOutput").ap()
    dram["gates"] = nc.dram_tensor("gates", [NTG + 2, P, KEYS * TG], F32, kind="Internal").ap()
    dram["acts"] = nc.dram_tensor("acts", [KEYS, P, T], F32, kind="Internal").ap()
    trunk(nc, dram)


def kernel(**inputs):
    import concourse.bacc as bacc
    from concourse.bass_utils import run_bass_kernel_spmd

    arrays = _lay_out({k: np.asarray(v) for k, v in inputs.items()})
    nc = bacc.Bacc("TRN2", target_bir_lowering=False, num_devices=1)
    build(nc, {n: list(a.shape) for n, a in arrays.items()})
    r = run_bass_kernel_spmd(nc, [{f"in_{n}": a for n, a in arrays.items()}], core_ids=[0])
    return r.results[0]["out_0"].transpose(2, 1, 0).reshape(1, T, D)
```
